# Optimizing a Trainium2 kernel written in Bass

```python
import math
import jax
import jax.numpy as jnp
from jax import lax
import numpy as np

D_MODEL = 1024
BATCH = 1
SEQ = 256
DEPTH = 2

HEAD_DIM = 64
MIX_WIDTH = D_MODEL
A_HEADS = 4
DIFF_QK_DIM = HEAD_DIM // 2
DIFF_V_DIM = HEAD_DIM
B_HEADS = 6
C_HEADS = 6
DILATED_PATTERNS = ((128, 1), (512, 4), (2048, 16))
Q_BLOCK = 128
ROPE_THETA = 10000.0
D_FF = 2816
CONV_WIDTH = 3
NORM_EPS = 1e-6
SUBLN_EPS = 1e-5
FORGET_BIAS_INIT = 4.0

A_Q = A_HEADS * 2 * DIFF_QK_DIM
A_K = A_HEADS * 2 * DIFF_QK_DIM
A_V = A_HEADS * DIFF_V_DIM
B_W = B_HEADS * HEAD_DIM
C_W = C_HEADS * HEAD_DIM
IN_COLS = A_Q + A_K + A_V + 3 * B_W + 3 * C_W + C_HEADS


def rmsnorm(x, g, eps=NORM_EPS):
    xf = x.astype(jnp.float32)
    y = xf * lax.rsqrt(jnp.mean(xf * xf, axis=-1, keepdims=True) + eps)
    return (y * g.astype(jnp.float32)).astype(x.dtype)

def rope_tables(seq, dim):
    inv = 1.0 / (ROPE_THETA ** (jnp.arange(0, dim, 2, dtype=jnp.float32) / dim))
    ang = jnp.arange(seq, dtype=jnp.float32)[:, None] * inv[None, :]
    return jnp.cos(ang), jnp.sin(ang)

def apply_rope(x, cos, sin):
    half = x.shape[-1] // 2
    xf = x.astype(jnp.float32)
    x1, x2 = xf[..., :half], xf[..., half:]
    out = jnp.concatenate([x1 * cos - x2 * sin, x2 * cos + x1 * sin], axis=-1)
    return out.astype(x.dtype)

def diff_attention(q, k, v, lam):
    bn, h, _, t, dk = q.shape
    nb = t // Q_BLOCK
    qb = q.reshape(bn, h, 2, nb, Q_BLOCK, dk).transpose(3, 0, 1, 2, 4, 5)
    kpos = jnp.arange(t)
    scale = dk ** -0.5
    vf = v.astype(jnp.float32)

    def block(args):
        qblk, bi = args
        s = jnp.einsum('bhmqd,bhmkd->bhmqk', qblk, k).astype(jnp.float32) * scale
        qpos = bi * Q_BLOCK + jnp.arange(Q_BLOCK)
        s = jnp.where(kpos[None, :] <= qpos[:, None], s, -jnp.inf)
        p = jax.nn.softmax(s, axis=-1)
        a = p[:, :, 0] - lam * p[:, :, 1]
        return jnp.einsum('bhqk,bhkd->bhqd', a, vf)

    o = lax.map(block, (qb, jnp.arange(nb)))
    return o.transpose(1, 2, 0, 3, 4).reshape(bn, h, t, -1)

def forgetting_attention(q, k, v, cum_logf):
    bn, h, t, hd = q.shape
    nb = t // Q_BLOCK
    qb = q.reshape(bn, h, nb, Q_BLOCK, hd).transpose(2, 0, 1, 3, 4)
    fb = cum_logf.reshape(bn, h, nb, Q_BLOCK).transpose(2, 0, 1, 3)
    kpos = jnp.arange(t)
    scale = hd ** -0.5
    vf = v.astype(jnp.float32)

    def block(args):
        qblk, fq, bi = args
        s = jnp.einsum('bhqd,bhkd->bhqk', qblk, k).astype(jnp.float32) * scale
        s = s + fq[..., :, None] - cum_logf[..., None, :]
        qpos = bi * Q_BLOCK + jnp.arange(Q_BLOCK)
        s = jnp.where(kpos[None, :] <= qpos[:, None], s, -jnp.inf)
        p = jax.nn.softmax(s, axis=-1)
        return jnp.einsum('bhqk,bhkd->bhqd', p, vf)

    o = lax.map(block, (qb, fb, jnp.arange(nb)))
    return o.transpose(1, 2, 0, 3, 4).reshape(bn, h, t, hd)

def banded_window_attention(q, k, v, w):
    bn, g, l, hd = q.shape
    nb = l // w
    qb = q.reshape(bn, g, nb, w, hd)

    def with_prev(a):
        a = a.reshape(bn, g, nb, w, hd)
        prev = jnp.pad(a, ((0, 0), (0, 0), (1, 0), (0, 0), (0, 0)))[:, :, :-1]
        return jnp.concatenate([prev, a], axis=3)

    kk, vv = with_prev(k), with_prev(v)
    s = jnp.einsum('bgnqd,bgnkd->bgnqk', qb, kk).astype(jnp.float32) * (hd ** -0.5)
    dist = jnp.arange(w)[:, None] + w - jnp.arange(2 * w)[None, :]
    kidx = jnp.arange(nb)[:, None] * w + jnp.arange(2 * w)[None, :] - w
    mask = ((dist >= 0) & (dist <= w))[None, :, :] & (kidx >= 0)[:, None, :]
    s = jnp.where(mask, s, -jnp.inf)
    m = jnp.max(s, axis=-1, keepdims=True)
    p = jnp.exp(s - m)
    den = jnp.sum(p, axis=-1, keepdims=True)
    o = jnp.einsum('bgnqk,bgnkd->bgnqd', p, vv.astype(jnp.float32)) / den
    lse = (m + jnp.log(den))[..., 0]
    return o.reshape(bn, g, l, hd), lse.reshape(bn, g, l)

def dilated_mixture_attention(q, k, v):
    bn, h, t, hd = q.shape
    outs, lses = [], []
    for window, d in DILATED_PATTERNS:
        l = t // d
        w = window // d
        lp = -(-l // w) * w

        def fold(a):
            a = a.reshape(bn, h, l, d, hd).transpose(0, 1, 3, 2, 4).reshape(bn, h * d, l, hd)
            return jnp.pad(a, ((0, 0), (0, 0), (0, lp - l), (0, 0)))

        o, lse = banded_window_attention(fold(q), fold(k), fold(v), w)
        o = o[:, :, :l].reshape(bn, h, d, l, hd).transpose(0, 1, 3, 2, 4).reshape(bn, h, t, hd)
        lse = lse[:, :, :l].reshape(bn, h, d, l).transpose(0, 1, 3, 2).reshape(bn, h, t)
        outs.append(o)
        lses.append(lse)
    wts = jax.nn.softmax(jnp.stack(lses, axis=0), axis=0)
    return jnp.sum(wts[..., None] * jnp.stack(outs, axis=0), axis=0)

def causal_depthwise_conv(g, w, b):
    t = g.shape[1]
    gp = jnp.pad(g, ((0, 0), (CONV_WIDTH - 1, 0), (0, 0)))
    y = b
    for i in range(CONV_WIDTH):
        y = y + gp[:, i:i + t] * w[i]
    return y

def mixer_layer(h, w_in, w_out, lam_params, subln_g, forget_bias, lam_init, cos_a, sin_a, cos_b, sin_b):
    bn, t, _ = h.shape
    proj = h @ w_in
    cuts = np.cumsum([A_Q, A_K, A_V, B_W, B_W, B_W, C_W, C_W, C_W])
    qa, ka, va, qb, kb, vb, qc, kc, vc, fz = jnp.split(proj, cuts, axis=-1)

    qa = apply_rope(qa.reshape(bn, t, A_HEADS, 2, DIFF_QK_DIM).transpose(0, 2, 3, 1, 4), cos_a, sin_a)
    ka = apply_rope(ka.reshape(bn, t, A_HEADS, 2, DIFF_QK_DIM).transpose(0, 2, 3, 1, 4), cos_a, sin_a)
    va = va.reshape(bn, t, A_HEADS, DIFF_V_DIM).transpose(0, 2, 1, 3)
    lp = lam_params.astype(jnp.float32)
    lam = jnp.exp(jnp.sum(lp[0] * lp[1])) - jnp.exp(jnp.sum(lp[2] * lp[3])) + lam_init
    oa = diff_attention(qa, ka, va, lam)
    oa = oa * lax.rsqrt(jnp.mean(oa * oa, axis=-1, keepdims=True) + SUBLN_EPS)
    oa = oa * subln_g.astype(jnp.float32) * (1.0 - lam_init)

    def heads(a, n):
        return a.reshape(bn, t, n, HEAD_DIM).transpose(0, 2, 1, 3)
    qb = apply_rope(heads(qb, B_HEADS), cos_b, sin_b)
    kb = apply_rope(heads(kb, B_HEADS), cos_b, sin_b)
    ob = dilated_mixture_attention(qb, kb, heads(vb, B_HEADS))

    logf = jax.nn.log_sigmoid((fz + forget_bias).astype(jnp.float32))
    cum_logf = lax.cumsum(logf, axis=1).transpose(0, 2, 1)
    oc = forgetting_attention(heads(qc, C_HEADS), heads(kc, C_HEADS), heads(vc, C_HEADS), cum_logf)

    def merge(o):
        return o.transpose(0, 2, 1, 3).reshape(bn, t, -1)
    o = jnp.concatenate([merge(oa), merge(ob), merge(oc)], axis=-1).astype(h.dtype)
    return o @ w_out

def first_inputs(seed: int = 0) -> dict:
    key = jax.random.key(seed)
    ks = jax.random.split(key, 18)
    f32 = jnp.float32
    n = jax.random.normal
    return {
        'x': n(ks[0], (BATCH, SEQ, D_MODEL), f32),
        'c': n(ks[1], (BATCH, D_MODEL), f32),
        'w_mod': n(ks[2], (DEPTH, D_MODEL, 6 * D_MODEL), f32) * (0.5 * D_MODEL ** -0.5),
        'b_mod': n(ks[3], (DEPTH, 6 * D_MODEL), f32) * 0.02,
        'g_attn': 1.0 + 0.02 * n(ks[4], (DEPTH, D_MODEL), f32),
        'w_in': n(ks[5], (DEPTH, D_MODEL, IN_COLS), f32) * D_MODEL ** -0.5,
        'diff_lambda': n(ks[6], (DEPTH, 4, DIFF_QK_DIM), f32) * 0.1,
        'subln_g': 1.0 + 0.02 * n(ks[7], (DEPTH, DIFF_V_DIM), f32),
        'forget_bias': FORGET_BIAS_INIT + 0.5 * n(ks[8], (DEPTH, C_HEADS), f32),
        'w_out': n(ks[9], (DEPTH, MIX_WIDTH, D_MODEL), f32) * MIX_WIDTH ** -0.5,
        'g_mlp': 1.0 + 0.02 * n(ks[10], (DEPTH, D_MODEL), f32),
        'w_up': n(ks[11], (DEPTH, D_MODEL, 2 * D_FF), f32) * D_MODEL ** -0.5,
        'conv_w': n(ks[12], (DEPTH, CONV_WIDTH, D_FF), f32) * CONV_WIDTH ** -0.5,
        'conv_b': n(ks[13], (DEPTH, D_FF), f32) * 0.02,
        'w_down': n(ks[14], (DEPTH, D_FF, D_MODEL), f32) * D_FF ** -0.5,
        'g_final': 1.0 + 0.02 * n(ks[15], (D_MODEL,), f32),
    }

def first_block(x, c, w_mod, b_mod, g_attn, w_in, diff_lambda, subln_g, forget_bias, w_out,
              g_mlp, w_up, conv_w, conv_b, w_down, g_final):
    t = x.shape[1]
    cos_a, sin_a = rope_tables(t, DIFF_QK_DIM)
    cos_b, sin_b = rope_tables(t, HEAD_DIM)
    sc = jax.nn.silu(c)
    for layer in range(DEPTH):
        lam_init = 0.8 - 0.6 * math.exp(-0.3 * layer)
        mod = sc @ w_mod[layer] + b_mod[layer]
        shift1, scale1, gate1, shift2, scale2, gate2 = [m[:, None, :] for m in jnp.split(mod, 6, axis=-1)]

        h = rmsnorm(x, g_attn[layer]) * (1.0 + scale1) + shift1
        o = mixer_layer(h, w_in[layer], w_out[layer], diff_lambda[layer], subln_g[layer],
                        forget_bias[layer], lam_init, cos_a, sin_a, cos_b, sin_b)
        x = x + gate1 * o

        h = rmsnorm(x, g_mlp[layer]) * (1.0 + scale2) + shift2
        up = h @ w_up[layer]
        u, g = up[..., :D_FF], up[..., D_FF:]
        g = causal_depthwise_conv(g, conv_w[layer], conv_b[layer])
        x = x + gate2 * ((jax.nn.silu(g) * u) @ w_down[layer])
    return rmsnorm(x, g_final)


GRID_W = 64
EPS = 1e-6

NA_HEADS = 6
NA_WIN_H = 8
NA_WIN_W = 16
A_WIDTH = NA_HEADS * HEAD_DIM

MLA_HEADS = 6
MLA_Q_RANK = 256
MLA_KV_RANK = 128
MLA_NOPE = 64
MLA_ROPE = 32
MLA_QK = MLA_NOPE + MLA_ROPE
MLA_V = 64
B_WIDTH = MLA_HEADS * MLA_V

CONV_GROUPS = 4
CONV_CH = CONV_GROUPS * HEAD_DIM
CONV_W = 3
C_WIDTH = CONV_CH

D_MIX = A_WIDTH + B_WIDTH + C_WIDTH
IN_SIZES = (A_WIDTH, A_WIDTH, A_WIDTH, MLA_Q_RANK, MLA_KV_RANK, MLA_ROPE, C_WIDTH, C_WIDTH, C_WIDTH)
IN_COLS_2 = sum(IN_SIZES)

N_EXPERTS = 16
EXPERT_FF = 1024
CAPACITY_FACTOR = 2


def rms_norm(x, g):
    xf = x.astype(jnp.float32)
    y = xf * lax.rsqrt(jnp.mean(xf * xf, axis=-1, keepdims=True) + EPS)
    return (y * g.astype(jnp.float32)).astype(x.dtype)

def rope(x, pos):
    half = x.shape[-1] // 2
    inv = ROPE_THETA ** (-jnp.arange(half, dtype=jnp.float32) / half)
    ang = pos.astype(jnp.float32)[:, None] * inv[None, :]
    cos = jnp.cos(ang)[None, :, None, :]
    sin = jnp.sin(ang)[None, :, None, :]
    xf = x.astype(jnp.float32)
    x1, x2 = xf[..., :half], xf[..., half:]
    return jnp.concatenate([x1 * cos - x2 * sin, x2 * cos + x1 * sin], axis=-1).astype(x.dtype)

def neighbourhood_attention(q, k, v, rpb):
    b, s, h, dh = q.shape
    rows = s // GRID_W
    wh = min(NA_WIN_H, rows)
    ww = NA_WIN_W
    cols = np.arange(GRID_W)
    col_idx = np.clip(cols - ww // 2, 0, GRID_W - ww)[:, None] + np.arange(ww)[None, :]
    col_off = col_idx - cols[:, None] + (NA_WIN_W - 1)
    qg = q.reshape(b, rows, GRID_W, h, dh).transpose(1, 0, 2, 3, 4)
    kg = k.reshape(b, rows, GRID_W, h, dh)
    vg = v.reshape(b, rows, GRID_W, h, dh)
    scale = dh ** -0.5

    def one_row(args):
        r, q_row = args
        r0 = jnp.clip(r - wh // 2, 0, rows - wh)
        k_win = lax.dynamic_slice_in_dim(kg, r0, wh, axis=1)[:, :, col_idx]
        v_win = lax.dynamic_slice_in_dim(vg, r0, wh, axis=1)[:, :, col_idx]
        row_off = r0 + jnp.arange(wh) - r + (NA_WIN_H - 1)
        bias = rpb[:, row_off[:, None, None], col_off[None, :, :]].transpose(0, 2, 1, 3)
        sc = jnp.einsum('bqhd,biqjhd->bhqij', q_row, k_win).astype(jnp.float32) * scale
        sc = sc + bias.astype(jnp.float32)[None]
        p = jax.nn.softmax(sc.reshape(b, h, GRID_W, wh * ww), axis=-1).reshape(sc.shape).astype(v.dtype)
        return jnp.einsum('bhqij,biqjhd->bqhd', p, v_win)

    o = lax.map(one_row, (jnp.arange(rows), qg))
    return o.transpose(1, 0, 2, 3, 4).reshape(b, s, h * dh)

def mla_attention(q, k, v):
    b, s, h, dq = q.shape
    dv = v.shape[-1]
    nblk = s // Q_BLOCK
    scale = dq ** -0.5
    qb = q.reshape(b, nblk, Q_BLOCK, h, dq).transpose(1, 0, 2, 3, 4)

    def one_block(q_blk):
        sc = jnp.einsum('bqhd,bkhd->bhqk', q_blk, k).astype(jnp.float32) * scale
        p = jax.nn.softmax(sc, axis=-1).astype(v.dtype)
        return jnp.einsum('bhqk,bkhd->bqhd', p, v)

    o = lax.map(one_block, qb)
    return o.transpose(1, 0, 2, 3, 4).reshape(b, s, h * dv)

def short_conv_mixer(hc, bc, cc, conv_w):
    u = cc * hc
    y = lax.conv_general_dilated(
        u, conv_w[:, None, :].astype(u.dtype), window_strides=(1,),
        padding=((CONV_W // 2, CONV_W // 2),), dimension_numbers=('NWC', 'WIO', 'NWC'),
        feature_group_count=u.shape[-1])
    return bc * y

def expert_choice_moe(x, w_router, b_router, w_gate, w_up, w_down):
    b, s, d = x.shape
    cap = CAPACITY_FACTOR * s // N_EXPERTS
    logits = jnp.einsum('bsd,de->bse', x, w_router).astype(jnp.float32) + b_router.astype(jnp.float32)
    aff = jax.nn.softmax(logits, axis=-1)
    gate, idx = lax.top_k(aff.transpose(0, 2, 1), cap)
    bidx = jnp.arange(b)[:, None, None]
    xs = x[bidx, idx]
    hid = jax.nn.silu(jnp.einsum('becd,edf->becf', xs, w_gate)) * jnp.einsum('becd,edf->becf', xs, w_up)
    ys = jnp.einsum('becf,efd->becd', hid, w_down) * gate[..., None].astype(x.dtype)
    return jnp.zeros_like(x).at[bidx, idx].add(ys)

def hybrid_layer(x, pos, norm_mix, w_in, q_norm_a, k_norm_a, rpb, cq_norm, w_uq, ckv_norm, w_ukv,
                 q_norm_b, k_norm_b, conv_w, out_norm, w_out, norm_ffn, w_router, b_router,
                 w_gate, w_up, w_down):
    b, s, _ = x.shape
    hn = rms_norm(x, norm_mix)
    proj = jnp.einsum('bsd,dc->bsc', hn, w_in)
    splits = np.cumsum(IN_SIZES)[:-1].tolist()
    qa, ka, va, cq, ckv, kr, hc, bc, cc = jnp.split(proj, splits, axis=-1)

    qa = rms_norm(qa.reshape(b, s, NA_HEADS, HEAD_DIM), q_norm_a)
    ka = rms_norm(ka.reshape(b, s, NA_HEADS, HEAD_DIM), k_norm_a)
    va = va.reshape(b, s, NA_HEADS, HEAD_DIM)
    out_a = neighbourhood_attention(qa, ka, va, rpb)

    qb = jnp.einsum('bsr,rc->bsc', rms_norm(cq, cq_norm), w_uq).reshape(b, s, MLA_HEADS, MLA_QK)
    kv = jnp.einsum('bsr,rc->bsc', rms_norm(ckv, ckv_norm), w_ukv).reshape(b, s, MLA_HEADS, MLA_NOPE + MLA_V)
    kb = jnp.concatenate(
        [kv[..., :MLA_NOPE], jnp.broadcast_to(kr[:, :, None, :], (b, s, MLA_HEADS, MLA_ROPE))], axis=-1)
    vb = kv[..., MLA_NOPE:]
    qb = rms_norm(qb, q_norm_b)
    kb = rms_norm(kb, k_norm_b)
    qb = jnp.concatenate([qb[..., :MLA_NOPE], rope(qb[..., MLA_NOPE:], pos)], axis=-1)
    kb = jnp.concatenate([kb[..., :MLA_NOPE], rope(kb[..., MLA_NOPE:], pos)], axis=-1)
    out_b = mla_attention(qb, kb, vb)

    out_c = short_conv_mixer(hc, bc, cc, conv_w)

    mixed = jnp.concatenate([
        rms_norm(out_a, out_norm[:A_WIDTH]),
        rms_norm(out_b, out_norm[A_WIDTH:A_WIDTH + B_WIDTH]),
        rms_norm(out_c, out_norm[A_WIDTH + B_WIDTH:]),
    ], axis=-1)
    x = x + jnp.einsum('bsc,cd->bsd', mixed, w_out)
    x = x + expert_choice_moe(rms_norm(x, norm_ffn), w_router, b_router, w_gate, w_up, w_down)
    return x

def second_inputs(seed: int = 0) -> dict:
    key = jax.random.key(seed)
    ks = jax.random.split(key, 22)
    f32 = jnp.float32

    def nrm(k, shape, scale):
        return jax.random.normal(k, shape, f32) * scale

    def gain(k, shape):
        return 1.0 + 0.05 * jax.random.normal(k, shape, f32)

    res_scale = (2 * DEPTH) ** -0.5
    return {
        'x': nrm(ks[0], (BATCH, SEQ, D_MODEL), 1.0),
        'norm_mix': gain(ks[1], (DEPTH, D_MODEL)),
        'w_in': nrm(ks[2], (DEPTH, D_MODEL, IN_COLS_2), D_MODEL ** -0.5),
        'q_norm_a': gain(ks[3], (DEPTH, HEAD_DIM)),
        'k_norm_a': gain(ks[4], (DEPTH, HEAD_DIM)),
        'rpb': nrm(ks[5], (DEPTH, NA_HEADS, 2 * NA_WIN_H - 1, 2 * NA_WIN_W - 1), 0.1),
        'cq_norm': gain(ks[6], (DEPTH, MLA_Q_RANK)),
        'w_uq': nrm(ks[7], (DEPTH, MLA_Q_RANK, MLA_HEADS * MLA_QK), MLA_Q_RANK ** -0.5),
        'ckv_norm': gain(ks[8], (DEPTH, MLA_KV_RANK)),
        'w_ukv': nrm(ks[9], (DEPTH, MLA_KV_RANK, MLA_HEADS * (MLA_NOPE + MLA_V)), MLA_KV_RANK ** -0.5),
        'q_norm_b': gain(ks[10], (DEPTH, MLA_QK)),
        'k_norm_b': gain(ks[11], (DEPTH, MLA_QK)),
        'conv_w': nrm(ks[12], (DEPTH, CONV_W, CONV_CH), CONV_W ** -0.5),
        'out_norm': gain(ks[13], (DEPTH, D_MIX)),
        'w_out': nrm(ks[14], (DEPTH, D_MIX, D_MODEL), D_MIX ** -0.5 * res_scale),
        'norm_ffn': gain(ks[15], (DEPTH, D_MODEL)),
        'w_router': nrm(ks[16], (DEPTH, D_MODEL, N_EXPERTS), D_MODEL ** -0.5),
        'b_router': nrm(ks[17], (DEPTH, N_EXPERTS), 0.01),
        'w_gate': nrm(ks[18], (DEPTH, N_EXPERTS, D_MODEL, EXPERT_FF), D_MODEL ** -0.5),
        'w_up': nrm(ks[19], (DEPTH, N_EXPERTS, D_MODEL, EXPERT_FF), D_MODEL ** -0.5),
        'w_down': nrm(ks[20], (DEPTH, N_EXPERTS, EXPERT_FF, D_MODEL), EXPERT_FF ** -0.5),
    }

def second_block(x, norm_mix, w_in, q_norm_a, k_norm_a, rpb, cq_norm, w_uq, ckv_norm, w_ukv,
              q_norm_b, k_norm_b, conv_w, out_norm, w_out, norm_ffn, w_router, b_router,
              w_gate, w_up, w_down):
    pos = jnp.arange(x.shape[1], dtype=jnp.int32)
    for l in range(DEPTH):
        x = hybrid_layer(x, pos, norm_mix[l], w_in[l], q_norm_a[l], k_norm_a[l], rpb[l], cq_norm[l],
                         w_uq[l], ckv_norm[l], w_ukv[l], q_norm_b[l], k_norm_b[l], conv_w[l],
                         out_norm[l], w_out[l], norm_ffn[l], w_router[l], b_router[l],
                         w_gate[l], w_up[l], w_down[l])
    return x


def setup_inputs(seed=0):
    out = dict(first_inputs(seed))
    for name, value in second_inputs(seed + 1).items():
        if name != "x":
            out[name + "_2"] = value
    return out


def reference(
    x, c, w_mod, b_mod, g_attn, w_in, diff_lambda, subln_g, forget_bias, w_out, g_mlp, w_up,
    conv_w, conv_b, w_down, g_final, norm_mix_2, w_in_2, q_norm_a_2, k_norm_a_2, rpb_2,
    cq_norm_2, w_uq_2, ckv_norm_2, w_ukv_2, q_norm_b_2, k_norm_b_2, conv_w_2, out_norm_2,
    w_out_2, norm_ffn_2, w_router_2, b_router_2, w_gate_2, w_up_2, w_down_2,
):
    x = first_block(
        x, c, w_mod, b_mod, g_attn, w_in, diff_lambda, subln_g, forget_bias, w_out, g_mlp, w_up,
        conv_w, conv_b, w_down, g_final,
    )
    return second_block(
        x, norm_mix_2, w_in_2, q_norm_a_2, k_norm_a_2, rpb_2, cq_norm_2, w_uq_2, ckv_norm_2,
        w_ukv_2, q_norm_b_2, k_norm_b_2, conv_w_2, out_norm_2, w_out_2, norm_ffn_2, w_router_2,
        b_router_2, w_gate_2, w_up_2, w_down_2,
    )


_drawn_inputs = setup_inputs


def setup_inputs(seed=0):
    import zlib

    import numpy as np

    out = dict(_drawn_inputs(seed))
    spreads = {}
    factors = {'g_attn': 3.952,
     'diff_lambda': 3.565,
     'subln_g': 5.825,
     'g_mlp': 3.276,
     'conv_b': 4.23,
     'q_norm_a_2': 3.117,
     'k_norm_a_2': 3.32,
     'cq_norm_2': 3.652,
     'q_norm_b_2': 3.806,
     'k_norm_b_2': 3.653,
     'b_router_2': 8.0}
    for name, (base, spread) in spreads.items():
        noise = np.random.default_rng([zlib.crc32(name.encode()), seed]).standard_normal(out[name].shape)
        drawn = base * np.exp(spread * noise) if base else spread * noise
        out[name] = jnp.asarray(drawn.astype(out[name].dtype))
    for name, factor in factors.items():
        out[name] = (out[name] * factor).astype(out[name].dtype)
    return out
```

```python
import math
import numpy as np
import concourse.bass as bass
from concourse import mybir
from contextlib import ExitStack

F32 = mybir.dt.float32
ALU = mybir.AluOpType
ACT = mybir.ActivationFunctionType
AX = mybir.AxisListType

P = 128
T = 256
NC_ = T // P
D = 1024
KD = D // P
DEPTH = 2
N = 512
HD = 64
AH, BH, CH = 4, 6, 6
IN1 = 3078
DFF = 2816
FCH = DFF // P
UPT = FCH // 2
IN2 = 2336
NAH = 6
MLH, MQK = 6, 96
EXP, CAP, EFF = 16, 32, 1024
EG = 4
GRID = 64
NEG = -1.0e30

B1_Q = {"A": 0, "B": 768, "C": 1920}
B1_K = {"A": 256, "B": 1152, "C": 2304}
B1_V = {"A": 512, "B": 1536, "C": 2688}
B1_F = 3072
QA2, KA2, VA2, CQ2, CKV2, KR2, HC2, BC2, CC2 = 0, 384, 768, 1152, 1408, 1536, 1568, 1824, 2080

SLOTS = 6
TILE = 4096
MOD0, MODT = 0, 12
B1_TILES = (
    [("mod", i) for i in range(4)]
    + [t for j in range(6) for t in (("in", j), ("mod", 4 + j))]
    + [("in", 6), ("mod", 10), ("mod", 11)]
    + [("out", i) for i in range(2)]
    + [("up", i) for i in range(UPT)]
    + [("down", i) for i in range((FCH + 3) // 4)]
)
B1_AT = {t: i for i, t in enumerate(B1_TILES)}
B1_N = -(-len(B1_TILES) // SLOTS) * SLOTS
B2_TILES = [("in", i) for i in range(5)] + [("out", 0), ("out", 1), ("small", 0)]
B2_AT = {t: i for i, t in enumerate(B2_TILES)}
B2_HEAD = -(-len(B2_TILES) // SLOTS) * SLOTS
G_TILES = 3 * KD
GROUPS = EXP // EG
B2_N = B2_HEAD + GROUPS * G_TILES
assert G_TILES % SLOTS == 0

TAB = {}


def _tab():
    at = 0
    for name, n in (("E", 384), ("ones", P), ("causal", 512), ("mult", 512), ("tri", T), ("colmask", GRID),
                    ("cosA", 64), ("sinA", 64), ("cosB", 128), ("sinB", 128), ("cosM", 64), ("sinM", 64),
                    ("iota", CAP), ("inv14", 28), ("inv3", 6), ("inv64", 8), ("inv96", 24), ("invD", 2), ("eps5", 8), ("eps6", 28),
                    ("half", 28), ("lam", 4)):
        TAB[name] = (at, n)
        at += n
    return at


NTAB = _tab()

C1 = {"g_attn": (0, 8), "g_mlp": (8, 8), "b_mod": (16, 48), "conv_w": (64, 66), "conv_b": (130, 22)}
NC1 = 152
C2 = {"norm_mix": (0, 8), "norm_ffn": (8, 8), "out_norm": (16, 8), "cq": (24, 2), "ckv": (26, 1), "qn": (27, 1),
      "kn": (28, 1)}
NC2 = 29
NCOLS = 2 * NC1 + 8 + 2 * NC2
R1 = {"subln": (0, 64), "fb": (64, 6), "lam": (70, 128)}
NR1 = 198
R2 = {"qnb": (0, 96), "knb": (96, 96), "router": (192, 16)}
NR2 = 208
NROWS = 2 * NR1 + 2 * NR2

MAPS1 = 2 * AH + BH + CH
MAPS2 = NAH + MLH
B1_COUNT = {
    "b1_gate_bias": 16, "b1_dve_step": 0, "b1_act_step": 0, "b1_pool_step": 0,
    "b1_sumsq": 4, "b1_rstd": 2, "b1_normed": 2, "b1_stream_flipped": 8, "b1_stream_by_dve": 8, "b1_stream_by_act": 8,
    "b1_mod_summed": 12, "b1_mod_ready": 12, "b1_gain_ready": 2,
    "b1_proj_by_act": 7, "b1_proj_by_dve": 7, "b1_rotated": 2, "b1_qk_flipped": 8, "b1_qk_ready": 8,
    "b1_forget_abs": 1, "b1_forget_log": 1, "b1_forget_ready": 1, "b1_cumsum_done": 4, "b1_cumsum_read": 4, "b1_lambda_dots": 1, "b1_lambda_exps": 1,
    "b1_scores_done": MAPS1, "b1_scores_read": MAPS1, "b1_max_ready": MAPS1, "b1_probs_ready": MAPS1, "b1_probs_flipped": MAPS1, "b1_probsT_ready": MAPS1,
    "b1_out_done": MAPS1, "b1_out_read": MAPS1, "b1_diff_sumsq": 1, "b1_diff_rstd": 1, "b1_diff_ready": 1,
    "b1_heads_flipped": 4, "b1_heads_by_dve": 2, "b1_heads_by_act": 2, "b1_mixer_added": 1, "b1_layer_added": 1,
    "b1_conv_done": UPT, "b1_silu_done": UPT, "b1_product_ready": UPT,
}
B2_COUNT = {
    "b2_bias_loaded": 16 * 4 * NAH, "b2_dve_step": 0, "b2_act_step": 0, "b2_pool_step": 0,
    "b2_sumsq": 4, "b2_rstd": 2, "b2_normed": 2, "b2_stream_flipped": 8, "b2_stream_by_dve": 8, "b2_stream_by_act": 8,
    "b2_proj_by_act": 5, "b2_proj_by_dve": 5, "b2_head_sumsq": 1, "b2_compressed_sumsq": 1, "b2_head_rstd": 1, "b2_heads_normed": 2, "b2_qk_flipped": 5, "b2_qk_ready": 5,
    "b2_uq_done": 4, "b2_uq_by_act": 2, "b2_uq_by_dve": 2, "b2_kv_done": 4, "b2_kv_by_act": 2, "b2_kv_by_dve": 2,
    "b2_taps_ready": 1, "b2_shifts_done": 1, "b2_shifts_read": 1, "b2_conv_ready": 1, "b2_latent_sumsq": 1, "b2_latent_rstd": 1, "b2_latent_ready": 1,
    "b2_head_flipped": MLH, "b2_head_ready": MLH,
    "b2_scores_done": MAPS2, "b2_scores_read": MAPS2, "b2_max_ready": MAPS2, "b2_probs_ready": MAPS2, "b2_probs_flipped": MAPS2, "b2_probsT_ready": MAPS2,
    "b2_out_done": MAPS2, "b2_out_read": MAPS2, "b2_mixed_sumsq": 1, "b2_mixed_rstd": 1, "b2_mixed_ready": 1,
    "b2_heads_flipped": 4, "b2_heads_by_dve": 2, "b2_heads_by_act": 2, "b2_mixer_added": 1, "b2_layer_added": 1,
    "b2_logits_ready": 1, "b2_affinity_exps": 1, "b2_affinity_ready": 1, "b2_affinity_flipped": 1, "b2_slots_ready": 1, "b2_slots_flipped": 1, "b2_bias_ready": 1,
}
G_COUNT = {
    "g_dve_step": 5, "g_act_step": 3,
    "g_chosen": 1, "g_weighted": 1, "g_rows_done": 2, "g_rows_by_dve": 1, "g_rows_by_act": 1, "g_weights_flipped": 1, "g_weights_ready": 1,
    "g_gate_silu": 2, "g_hidden_ready": 2, "g_hidden_flipped": 2, "g_hidden_by_dve": 1, "g_hidden_by_act": 1, "g_result_by_act": 1, "g_result_by_dve": 1, "g_scatter_done": 4, "g_scatter_added": 4,
}
B1_COUNT.update({"b1_dve_step": 218, "b1_act_step": 21, "b1_pool_step": 6})
B2_COUNT.update({"b2_dve_step": 94, "b2_act_step": 29, "b2_pool_step": 13})
COUNTS = {**B1_COUNT, **B2_COUNT, **G_COUNT}
ONCE = ("const_loaded", "tab_ready", "csil", "rpb_pad", "rpb_clear", "rpb_stored", "ring_seed",
        "fin_sumsq", "fin_rstd", "fin_g", "x_final", "out_stored", "once_dve", "once_act", "once_pool")
MISCOUNT = []


class Count:

    def __init__(self, sems, turn, counts, step):
        self.sems, self.turn, self.counts, self.step = sems, turn, counts, step
        self.sent, self.last = {}, None

    def at(self, name, k):
        return self.sems[name], k if self.turn is None else self.turn * self.counts[name] + k

    def up(self, name=None):
        name = name or self.step
        self.sent[name] = self.sent.get(name, 0) + 1
        self.last = (name, self.sent[name])
        return self.sems[name]

    def own(self):
        return self.at(*self.last)

    def end(self):
        for name, n in self.sent.items():
            if n != self.counts[name]:
                MISCOUNT.append((name, n, self.counts[name]))


def two_blocks(nc, a, out):
    ctx = ExitStack()
    with ctx:
        def sb(name, shape):
            return ctx.enter_context(nc.sbuf_tensor(name, shape, F32))

        ring = sb("ring", [P, SLOTS, TILE])
        x = sb("x", [P, NC_, D])
        hT = sb("hT", [P, 2048])
        tab = sb("tab", [P, NTAB])
        cols = sb("cols", [P, NCOLS])
        rows = sb("rows", [P, NROWS])
        ccol = sb("ccol", [P, NC1])
        crow = sb("crow", [P, NR2])
        wide = sb("wide", [P, 6160])
        qk = sb("qk", [P, 4096])
        sm = sb("sm", [P, 3, N])
        pT = sb("pT", [P, 2, N])
        gbuf = sb("gbuf", [P, 3072])
        sc = sb("sc", [P, 768])
        ps = [ctx.enter_context(nc.psum_tensor(f"ps{i}", [P, N], F32)) for i in range(8)]

        small = {}
        at = [0]

        def sm_(name, n):
            small[name] = sc[:, at[0]:at[0] + n]
            at[0] += n
            return small[name]

        csil = sm_("csil", 8)
        ss = sm_("ss", 28)
        rs = sm_("rs", 28)
        tmp28 = sm_("tmp28", 28)
        modc = sm_("modc", 48)
        acol = sm_("acol", 16)
        lamv = sm_("lamv", 4)
        lamt = sm_("lamt", 64)
        fz = sm_("fz", 12)
        fa = sm_("fa", 12)
        fe = sm_("fe", 12)
        nlf = sm_("nlf", 12)
        nfq = sm_("nfq", 12)
        den = sm_("den", 40)
        rden = sm_("rden", 40)
        nmx = sm_("nmx", 40)
        lcur = sm_("lcur", 2)
        aff = sm_("aff", 32)
        affe = sm_("affe", 32)
        slot = sm_("slot", 32)
        mx2 = sm_("mx2", 2)
        dn2 = sm_("dn2", 2)
        rd2 = sm_("rd2", 2)
        m8 = sm_("m8", 8)
        pad = sm_("pad", 1)
        assert at[0] <= 768

        def tb(name):
            o, n = TAB[name]
            return tab[:, o:o + n]

        E = tb("E")
        ident = E[:, P:2 * P]
        ones = tb("ones")
        tri = tb("tri")
        causal = tb("causal").rearrange("p (c k) -> p c k", c=2)
        mult = tb("mult").rearrange("p (c k) -> p c k", c=2)
        h8 = hT[:, :].rearrange("p (k t) -> p k t", k=KD)
        xn = wide[:, 0:2048].rearrange("p (c d) -> p c d", c=2)
        proj1 = wide[:, 0:2 * IN1].rearrange("p (c n) -> p c n", c=2)
        proj2 = wide[:, 0:2 * IN2].rearrange("p (c n) -> p c n", c=2)
        prod = wide[:, 0:FCH * T].rearrange("p (f t) -> p f t", f=FCH)
        qkT = qk[:, :].rearrange("p (b t) -> p b t", b=16)
        gates = gbuf[:, 0:2048].rearrange("p (i n) -> p i n", i=4)
        acc = gbuf[:, 2048:3072].rearrange("p (i n) -> p i n", i=2)
        oA = gbuf[:, 2048:3072].rearrange("p (h m c d) -> p h m c d", h=AH, m=2, c=2)
        nbias = gbuf[:, :].rearrange("p (h c k) -> p h c k", h=NAH, c=2)
        nfrow = hT[:, 0:1536].rearrange("p (h k) -> p h k", h=CH)
        cT = qk[:, 1536:2304].rearrange("p (b t) -> p b t", b=3)
        qb = qk[:, 2304:3456].rearrange("p (c n) -> p c n", c=2)
        kb = hT[:, 0:1152].rearrange("p (c n) -> p c n", c=2)
        xqk = [qk[:, 3456:3968], hT[:, 1152:1664]]
        vb = wide[:, 4672:5440].rearrange("p (c h d) -> p c h d", c=2, h=MLH)
        cv2 = wide[:, 5440:5952].rearrange("p (c n) -> p c n", c=2)
        xsT = wide[:, 2048:3072].rearrange("p (k s) -> p k s", k=KD)
        hid = wide[:, 3072:4096]
        hidT = wide[:, 4096:5120].rearrange("p (k s) -> p k s", k=KD)
        ysb = wide[:, 5120:6144]
        selP = sm[:, 0, 0:256].rearrange("p (c e s) -> p c e s", c=2, e=EG)
        selG = sm[:, 0, 256:512].rearrange("p (c e s) -> p c e s", c=2, e=EG)
        pgT = sm[:, 1, 0:256].rearrange("p (c t) -> p c t", c=2)
        rscratch = sm[:, 2, 0:256]
        rsel = pT[:, 0, 0:256]
        rcum = pT[:, 0, 256:512]
        rpad = hT[:, 0:128]

        copies = nc.dram_tensor("bias_copies", [DEPTH, NAH * 7, GRID, P], F32, kind="Internal").ap()

        sems = {}
        for name in (*COUNTS, *ONCE, "tile_done"):
            sems[name] = ctx.enter_context(nc.semaphore(name))
        tile_done = sems.pop("tile_done")
        arrived = [ctx.enter_context(nc.semaphore(f"slot_loaded{i}")) for i in range(SLOTS)]

        def arrivals(tiles):
            seen, at_ = [0] * SLOTS, []
            for t, kind in enumerate(tiles):
                n = 32 if kind[0] == "up" else 48 + 16 if kind[0] == "small" else 16
                seen[t % SLOTS] += n
                at_.append(seen[t % SLOTS])
            return at_, seen

        B1_ARR, B1_SEEN = arrivals(B1_TILES)
        B2_ARR, B2_HSEEN = arrivals(B2_TILES)
        B2_SEEN = [h + 16 * GROUPS * G_TILES // SLOTS for h in B2_HSEEN]

        def b1_loaded(L, t):
            i = t % SLOTS
            return arrived[i], L * B1_SEEN[i] + B1_ARR[t]

        def b2_loaded(L, t):
            i = t % SLOTS
            return arrived[i], L * B2_SEEN[i] + (DEPTH * B1_SEEN[i] + B2_ARR[t])

        def g_loaded(L, g, j):
            i = j % SLOTS
            first = DEPTH * B1_SEEN[i] + B2_HSEEN[i] + 16 * (j // SLOTS + 1)
            return arrived[i], L * B2_SEEN[i] + g * (16 * G_TILES // SLOTS) + first

        def b1_used(L, t):
            return L * B1_N + (SLOTS + t + 1)

        def b2_used(L, t):
            return L * B2_N + (DEPTH * B1_N + SLOTS + t + 1)

        def g_used(L, g, j):
            return L * B2_N + g * G_TILES + (DEPTH * B1_N + B2_HEAD + SLOTS + j + 1)

        def slot_at(t):
            return ring[:, t % SLOTS, :]

        def cc1(name, i=0, n=1):
            o, _ = C1[name]
            return ccol[:, o + i:o + i + n]

        def cc2(name, i=0, n=1):
            o, _ = C2[name]
            return ccol[:, o + i:o + i + n]

        def map1(m):
            if m < 2 * AH:
                b, r = m // 4, 32 * (m % 4)
                return dict(kind="A", q=qkT[r:r + 32, b, :], k=qkT[r:r + 32, 2 + b, :], v=B1_V["A"] + HD * (m // 2),
                            scale=32 ** -0.5, h=m // 2)
            kind, h = ("B", m - 2 * AH) if m < 2 * AH + BH else ("C", m - 2 * AH - BH)
            b0 = 4 if kind == "B" else 10
            r = 64 * (h % 2)
            return dict(kind=kind, q=qkT[r:r + 64, b0 + h // 2, :], k=qkT[r:r + 64, b0 + 3 + h // 2, :],
                        v=B1_V[kind] + HD * h, scale=HD ** -0.5, h=h)

        def map2(m):
            if m < NAH:
                r = 64 * (m % 2)
                return dict(kind="N", q=qkT[r:r + 64, m // 2, :], k=qkT[r:r + 64, 3 + m // 2, :], scale=HD ** -0.5, h=m)
            t = xqk[m % 2]
            return dict(kind="M", q=t[0:MQK, 0:T], k=t[0:MQK, T:2 * T], scale=MQK ** -0.5, h=m - NAH)

        block = ctx.enter_context(nc.Block())

        @block.sync
        def _(sp):
            with sp.Fori(0, DEPTH) as L:
                for t, (kind, j) in enumerate(B1_TILES):
                    sp.wait_ge(tile_done, L * B1_N + (t + 1))
                    dst = slot_at(t)
                    sem = arrived[t % SLOTS]
                    d8 = dst.rearrange("p (k n) -> p k n", k=KD)
                    if kind == "mod":
                        src = a["w_mod"][bass.ds(L, 1), :, j * N:(j + 1) * N].rearrange("l (k p) n -> p (l k) n", p=P)
                        sp.dma_start(d8, src).then_inc(sem, 16)
                    elif kind == "in":
                        w = min(N, IN1 - j * N)
                        src = a["w_in"][bass.ds(L, 1), :, j * N:j * N + w].rearrange("l (k p) n -> p (l k) n", p=P)
                        sp.dma_start(d8[:, :, 0:w], src).then_inc(sem, 16)
                    elif kind == "out":
                        src = a["w_out"][bass.ds(L, 1), :, j * N:(j + 1) * N].rearrange("l (k p) n -> p (l k) n", p=P)
                        sp.dma_start(d8, src).then_inc(sem, 16)
                    elif kind == "up":
                        for half in range(2):
                            o = half * DFF + j * 256
                            src = a["w_up"][bass.ds(L, 1), :, o:o + 256].rearrange("l (k p) n -> p (l k) n", p=P)
                            sp.dma_start(d8[:, :, half * 256:half * 256 + 256], src).then_inc(sem, 16)
                    else:
                        nf = min(4, FCH - 4 * j)
                        src = a["w_down"][bass.ds(L, 1), 4 * j * P:(4 * j + nf) * P, :]
                        sp.dma_start(dst.rearrange("p (f n) -> p f n", f=4)[:, 0:nf, :],
                                     src.rearrange("l (f p) n -> p (l f) n", p=P)).then_inc(sem, 16)
            with sp.Fori(0, DEPTH) as L:
                for t, (kind, j) in enumerate(B2_TILES):
                    sp.wait_ge(tile_done, L * B2_N + (DEPTH * B1_N + t + 1))
                    dst = slot_at(t)
                    sem = arrived[t % SLOTS]
                    d8 = dst.rearrange("p (k n) -> p k n", k=KD)
                    if kind == "in":
                        w = min(N, IN2 - j * N)
                        src = a["w_in_2"][bass.ds(L, 1), :, j * N:j * N + w].rearrange("l (k p) n -> p (l k) n", p=P)
                        sp.dma_start(d8[:, :, 0:w], src).then_inc(sem, 16)
                    elif kind == "out":
                        src = a["w_out_2"][bass.ds(L, 1), :, j * N:(j + 1) * N].rearrange("l (k p) n -> p (l k) n", p=P)
                        sp.dma_start(d8, src).then_inc(sem, 16)
                    else:
                        sp.dma_start(dst[:, 0:1152].rearrange("p (k n) -> p k n", k=2),
                                     a["w_uq_2"][bass.ds(L, 1)].rearrange("l (k p) n -> p (l k) n", p=P)).then_inc(sem, 16)
                        sp.dma_start(dst[:, 1152:1920].rearrange("p (k n) -> p k n", k=1),
                                     a["w_ukv_2"][bass.ds(L, 1)].rearrange("l p n -> p l n")).then_inc(sem, 16)
                        sp.dma_start(dst[:, 1920:2048].rearrange("p (k n) -> p k n", k=KD),
                                     a["w_router_2"][bass.ds(L, 1)].rearrange("l (k p) n -> p (l k) n", p=P)).then_inc(sem, 16)
                        sp.dma_start(dst[:, 2048:2816],
                                     a["conv_w_2"][bass.ds(L, 1)].rearrange("l i n -> l (i n)").to_broadcast([P, 768])
                                     ).then_inc(sem, 16)
                with sp.Fori(0, GROUPS) as g:
                    for j in range(G_TILES):
                        sp.wait_ge(tile_done, L * B2_N + g * G_TILES + (DEPTH * B1_N + B2_HEAD + j + 1))
                        w = (a["w_gate_2"], a["w_up_2"], a["w_down_2"])[j // KD]
                        k = j % KD
                        src = w[bass.ds(L * EXP + g * EG, EG), k * P:(k + 1) * P, :].rearrange("e p n -> p e n")
                        sp.dma_start(slot_at(j).rearrange("p (e n) -> p e n", e=EG), src)\
                          .then_inc(arrived[j % SLOTS], 16)
            sp.wait_ge(sems["b2_layer_added"], DEPTH + 1)
            sp.dma_start(out[0].rearrange("(c p) d -> p c d", p=P), x[:, :, :]).then_inc(sems["out_stored"], 16)
            sp.wait_ge(sems["out_stored"], 16)

        @block.tensor
        def _(pe):
            mm = nc.tensor.matmul
            pe.wait_ge(sems["const_loaded"], 16 * 5)
            pe.sem_inc(tile_done, SLOTS)

            def transpose_8(s, src, name, banks=(4, 5, 6, 7)):
                for j in range(4):
                    for i in range(4):
                        k, c = 2 * j + i // 2, i % 2
                        last = nc.tensor.transpose(ps[banks[j]][:, 128 * i:128 * i + 128], src(k, c), ident)
                    last.then_inc(s.up(name), 1)

            def linear(t, i, lhs, w):
                wt = slot_at(t).rearrange("p (k n) -> p k n", k=KD)
                b = 2 * (i % 2)
                for c in range(2):
                    for k in range(KD):
                        last = mm(ps[b + c][:, 0:w], lhs[:, k, c * P:(c + 1) * P], wt[:, k, 0:w],
                                  start=k == 0, stop=k == KD - 1)
                last.then_inc(tile_done, 1)

            def score(s, pre, mp, m):
                if m >= 2:
                    pe.wait_ge(*s.at(pre + "scores_read", m - 1))
                for c in range(2):
                    last = mm(ps[4 + m % 2][:, c * T:(c + 1) * T], mp["q"][:, c * P:(c + 1) * P], mp["k"],
                              start=True, stop=True)
                last.then_inc(s.up(pre + "scores_done"), 1)

            def flip(s, pre, m, blocks):
                pe.wait_ge(*s.at(pre + "probs_ready", m + 1))
                if m >= 2:
                    pe.wait_ge(*s.at(pre + "probsT_ready", m - 1))
                for i, (c, kc) in enumerate(blocks):
                    last = nc.tensor.transpose(ps[6 + m % 2][:, i * P:(i + 1) * P],
                                               sm[:, m % 3, c * T + kc * P:c * T + (kc + 1) * P], ident)
                last.then_inc(s.up(pre + "probs_flipped"), 1)

            def weigh(s, pre, m, blocks, v):
                pe.wait_ge(*s.at(pre + "probsT_ready", m + 1))
                if m >= 2:
                    pe.wait_ge(*s.at(pre + "out_read", m - 1))
                for i, (c, kc) in enumerate(blocks):
                    first = kc == 0
                    final = i + 1 == len(blocks) or blocks[i + 1][0] != c
                    last = mm(ps[2 + m % 2][:, c * HD:(c + 1) * HD], pT[:, m % 2, i * P:(i + 1) * P], v(kc),
                              start=first, stop=final)
                last.then_inc(s.up(pre + "out_done"), 1)

            with pe.Fori(0, DEPTH) as L:
                s = Count(sems, L, COUNTS, "b1_dve_step")

                def modulation(i):
                    b = i % 2 if i < 4 else 4 + i % 2
                    pe.wait_ge(*s.at("b1_mod_summed", i + 1))
                    if i in (4, 5):
                        pe.wait_ge(*s.at("b1_stream_by_dve", 4))
                        pe.wait_ge(*s.at("b1_stream_by_act", 4))
                    elif i >= 2:
                        pe.wait_ge(*s.at("b1_mod_ready", i - 1))
                    if i // 2 in (2, 5):
                        last = mm(ps[b][:, :], ones, acc[:, i % 2, :], start=True, stop=True)
                    else:
                        for q in range(4):
                            last = mm(ps[b][:, q:q + 1], acc[:, i % 2, q * P:(q + 1) * P], ones[:, 0:1],
                                      start=True, stop=True)
                    last.then_inc(tile_done, 1)

                pe.wait_ge(*s.at("b1_normed", 1))
                transpose_8(s, lambda k, c: xn[:, c, k * P:(k + 1) * P], "b1_stream_flipped")
                for i in range(4):
                    modulation(i)
                pe.wait_ge(*s.at("b1_stream_by_dve", 4))
                pe.wait_ge(*s.at("b1_stream_by_act", 4))
                pe.wait_ge(*s.at("b1_mod_ready", 4))

                def qk_flip(u):
                    if u >= 2:
                        pe.wait_ge(*s.at("b1_qk_ready", u - 1))
                    for i in range(4):
                        b, c = 2 * u + i // 2, i % 2
                        kind, o = ("A", b) if b < 4 else ("B", b - 4) if b < 10 else ("C", b - 10)
                        col = B1_Q[kind] + o * P
                        last = nc.tensor.transpose(ps[6 + u % 2][:, i * P:(i + 1) * P],
                                                   proj1[:, c, col:col + P], ident)
                    last.then_inc(s.up("b1_qk_flipped"), 1)

                for j in range(7):
                    t = B1_AT[("in", j)]
                    pe.wait_ge(*b1_loaded(L, t))
                    if j >= 2:
                        pe.wait_ge(*s.at("b1_proj_by_act", j - 1))
                        pe.wait_ge(*s.at("b1_proj_by_dve", j - 1))
                    linear(t, j, h8, min(N, IN1 - j * N))
                    if j < 6:
                        modulation(4 + j)
                    if j == 4:
                        pe.wait_ge(*s.at("b1_rotated", 1))
                        for u in range(2):
                            qk_flip(u)
                    if j == 5:
                        pe.wait_ge(*s.at("b1_rotated", 2))
                        for u in range(2, 5):
                            qk_flip(u)
                modulation(10)
                modulation(11)
                pe.wait_ge(*s.at("b1_proj_by_act", 6))
                pe.wait_ge(*s.at("b1_proj_by_dve", 6))
                for u in range(5, 8):
                    qk_flip(u)

                pe.wait_ge(*s.at("b1_forget_ready", 1))
                n2 = nlf.rearrange("p (c h) -> p c h", c=2)
                for h in range(CH):
                    o = ps[h // 2][:, (h % 2) * T:(h % 2 + 1) * T]
                    mm(o[:, 0:P], n2[:, 0, h:h + 1].to_broadcast([P, P]), tri[:, 0:P], start=True, stop=True)
                    mm(o[:, P:T], n2[:, 0, h:h + 1].to_broadcast([P, P]), ones, start=True, stop=False)
                    last = mm(o[:, P:T], n2[:, 1, h:h + 1].to_broadcast([P, P]), tri[:, 0:P], start=False, stop=True)
                    if h % 2:
                        last.then_inc(s.up("b1_cumsum_done"), 1)
                mm(ps[3][:, 0:6], tri[:, 0:P], n2[:, 0, :], start=True, stop=True)
                mm(ps[3][:, 6:12], ones, n2[:, 0, :], start=True, stop=False)
                last = mm(ps[3][:, 6:12], tri[:, 0:P], n2[:, 1, :], start=False, stop=True)
                last.then_inc(s.up("b1_cumsum_done"), 1)

                blocks = [(0, 0), (1, 0), (1, 1)]
                pe.wait_ge(*s.at("b1_mod_ready", 12))
                pe.wait_ge(*s.at("b1_qk_ready", 8))
                pe.wait_ge(*s.at("b1_cumsum_read", 4))
                for m in range(2):
                    score(s, "b1_", map1(m), m)
                for m in range(MAPS1 + 1):
                    if m + 2 < MAPS1:
                        score(s, "b1_", map1(m + 2), m + 2)
                    if m < MAPS1:
                        flip(s, "b1_", m, blocks)
                    if m >= 1:
                        v = map1(m - 1)["v"]
                        weigh(s, "b1_", m - 1, blocks, lambda kc: proj1[:, kc, v:v + HD])

                pe.wait_ge(*s.at("b1_out_read", MAPS1))
                pe.wait_ge(*s.at("b1_diff_ready", 1))
                ocol = [0, 128, 768, 896, 1024, 1920, 2048, 2176]
                transpose_8(s, lambda k, c: proj1[:, c, ocol[k]:ocol[k] + P], "b1_heads_flipped")
                pe.wait_ge(*s.at("b1_heads_by_dve", 2))
                pe.wait_ge(*s.at("b1_heads_by_act", 2))
                for j in range(2):
                    t = B1_AT[("out", j)]
                    pe.wait_ge(*b1_loaded(L, t))
                    linear(t, j, h8, N)

                pe.wait_ge(*s.at("b1_normed", 2))
                transpose_8(s, lambda k, c: xn[:, c, k * P:(k + 1) * P], "b1_stream_flipped")
                pe.wait_ge(*s.at("b1_stream_by_dve", 8))
                pe.wait_ge(*s.at("b1_stream_by_act", 8))
                for j in range(UPT):
                    t = B1_AT[("up", j)]
                    pe.wait_ge(*b1_loaded(L, t))
                    wt = slot_at(t).rearrange("p (k n) -> p k n", k=KD)
                    if j >= 2:
                        pe.wait_ge(*s.at("b1_product_ready", j - 1))
                    for half in (1, 0):
                        for f in range(2):
                            for k in range(KD):
                                o = half * 256 + f * P
                                last = mm(ps[2 * (j % 2) + half][:, f * T:(f + 1) * T], wt[:, k, o:o + P], h8[:, k, :],
                                          start=k == 0, stop=k == KD - 1)
                    last.then_inc(tile_done, 1)
                pe.wait_ge(*s.at("b1_product_ready", UPT))
                nd = (FCH + 3) // 4
                for j in range(nd):
                    t = B1_AT[("down", j)]
                    pe.wait_ge(*b1_loaded(L, t))
                    wt = slot_at(t).rearrange("p (f n) -> p f n", f=4)
                    for q in range(min(4, FCH - 4 * j)):
                        f = 4 * j + q
                        for c in range(2):
                            for n in range(2):
                                last = mm(ps[4 + 2 * c + n][:, :], prod[:, f, c * P:(c + 1) * P],
                                          wt[:, q, n * N:(n + 1) * N], start=f == 0, stop=f == FCH - 1)
                    last.then_inc(tile_done, 1 if j < nd - 1 else 1 + B1_N - len(B1_TILES))
                s.end()

            with pe.Fori(0, DEPTH) as L:
                s = Count(sems, L, COUNTS, "b2_dve_step")
                pe.wait_ge(*s.at("b2_normed", 1))
                transpose_8(s, lambda k, c: xn[:, c, k * P:(k + 1) * P], "b2_stream_flipped")
                pe.wait_ge(*s.at("b2_stream_by_dve", 4))
                pe.wait_ge(*s.at("b2_stream_by_act", 4))

                for j in range(5):
                    t = B2_AT[("in", j)]
                    pe.wait_ge(*b2_loaded(L, t))
                    if j >= 2:
                        pe.wait_ge(*s.at("b2_proj_by_act", j - 1))
                        pe.wait_ge(*s.at("b2_proj_by_dve", j - 1))
                    linear(t, j, h8, min(N, IN2 - j * N))
                pe.wait_ge(*s.at("b2_heads_normed", 2))
                for n, u in enumerate((3, 4, 0, 1, 2)):
                    if n >= 1:
                        pe.wait_ge(*s.at("b2_qk_ready", n))
                    nb = 2 if u < 4 else 1
                    for i in range(2 * nb):
                        b, c = 2 * u + i // 2, i % 2
                        col = b * P if b < 6 else CQ2 + (b - 6) * P
                        last = nc.tensor.transpose(ps[6][:, i * P:(i + 1) * P], proj2[:, c, col:col + P], ident)
                    last.then_inc(s.up("b2_qk_flipped"), 1)
                t = B2_AT[("small", 0)]
                pe.wait_ge(*b2_loaded(L, t))
                pe.wait_ge(*s.at("b2_qk_ready", 5))
                pe.wait_ge(*s.at("b2_proj_by_act", 5))
                pe.wait_ge(*s.at("b2_proj_by_dve", 5))
                uq = slot_at(t)[:, 0:1152].rearrange("p (k n) -> p k n", k=2)
                ukv = slot_at(t)[:, 1152:1920]
                router = slot_at(t)[:, 1920:2048].rearrange("p (k n) -> p k n", k=KD)
                for c in range(2):
                    for hf in range(2):
                        for k in range(2):
                            last = mm(ps[2 * hf + c][:, 0:288], cT[:, k, c * P:(c + 1) * P],
                                      uq[:, k, hf * 288:(hf + 1) * 288], start=k == 0, stop=k == 1)
                        last.then_inc(s.up("b2_uq_done"), 1)
                for c in range(2):
                    for hf in range(2):
                        last = mm(ps[4 + 2 * hf + c][:, 0:384], cT[:, 2, c * P:(c + 1) * P],
                                  ukv[:, hf * 384:(hf + 1) * 384], start=True, stop=True)
                        last.then_inc(s.up("b2_kv_done"), 1)
                pe.wait_ge(*s.at("b2_taps_ready", 1))
                pe.wait_ge(*s.at("b2_uq_by_act", 2))
                v0 = [proj2[:, c, CC2:CC2 + 256] for c in range(2)]
                v2 = [cv2[:, c, :] for c in range(2)]
                o = ps[0][:, 0:256]
                mm(o, E[:, 127:255], v0[0], start=True, stop=False)
                mm(o, E[:, 129:257], v2[0], start=False, stop=False)
                mm(o, E[:, 1:129], v2[1], start=False, stop=True)
                o = ps[0][:, 256:512]
                mm(o, E[:, 127:255], v0[1], start=True, stop=False)
                mm(o, E[:, 255:383], v0[0], start=False, stop=False)
                last = mm(o, E[:, 129:257], v2[1], start=False, stop=True)
                last.then_inc(s.up("b2_shifts_done"), 1)

                blocks = [(0, 0), (0, 1), (1, 0), (1, 1)]
                pe.wait_ge(*s.at("b2_kv_by_act", 2))
                pe.wait_ge(*s.at("b2_kv_by_dve", 2))
                pe.wait_ge(*s.at("b2_uq_by_dve", 2))

                def head_flip(m):
                    h = m - NAH
                    if h == 0:
                        pe.wait_ge(*s.at("b2_latent_ready", 1))
                        pe.wait_ge(*s.at("b2_shifts_read", 1))
                    if h >= 2:
                        pe.wait_ge(*s.at("b2_head_ready", h - 1))
                    for i in range(4):
                        src = (qb, kb)[i // 2][:, i % 2, h * MQK:(h + 1) * MQK]
                        last = nc.tensor.transpose(ps[m % 2][0:MQK, i * P:(i + 1) * P], src, ident)
                    last.then_inc(s.up("b2_head_flipped"), 1)

                def score2(m):
                    if m >= NAH:
                        pe.wait_ge(*s.at("b2_head_ready", m - NAH + 1))
                    score(s, "b2_", map2(m), m)

                for m in range(2):
                    score2(m)
                for m in range(MAPS2 + 1):
                    if NAH <= m + 3 < MAPS2:
                        head_flip(m + 3)
                    if m + 2 < MAPS2:
                        score2(m + 2)
                    if m < MAPS2:
                        flip(s, "b2_", m, blocks)
                    if m >= 1:
                        h = m - 1
                        v = (lambda kc: proj2[:, kc, VA2 + HD * h:VA2 + HD * (h + 1)]) if h < NAH else \
                            (lambda kc: vb[:, kc, h - NAH, :])
                        weigh(s, "b2_", h, blocks, v)

                pe.wait_ge(*s.at("b2_mixed_ready", 1))
                ocol = [0, 128, 256, 1152, 1280, 1408, HC2, HC2 + P]
                transpose_8(s, lambda k, c: proj2[:, c, ocol[k]:ocol[k] + P], "b2_heads_flipped")
                pe.wait_ge(*s.at("b2_heads_by_dve", 2))
                pe.wait_ge(*s.at("b2_heads_by_act", 2))
                for j in range(2):
                    tt = B2_AT[("out", j)]
                    pe.wait_ge(*b2_loaded(L, tt))
                    linear(tt, j, h8, N)

                pe.wait_ge(*s.at("b2_normed", 2))
                transpose_8(s, lambda k, c: xn[:, c, k * P:(k + 1) * P], "b2_stream_flipped")
                pe.wait_ge(*s.at("b2_stream_by_dve", 8))
                pe.wait_ge(*s.at("b2_stream_by_act", 8))
                for c in range(2):
                    for k in range(KD):
                        last = mm(ps[0][:, c * EXP:(c + 1) * EXP], h8[:, k, c * P:(c + 1) * P], router[:, k, :],
                                  start=k == 0, stop=k == KD - 1)
                last.then_inc(tile_done, 1 + B2_HEAD - len(B2_TILES))
                pe.wait_ge(*s.at("b2_affinity_ready", 1))
                for c in range(2):
                    last = nc.tensor.transpose(ps[1][0:EXP, c * P:(c + 1) * P], aff[:, c * EXP:(c + 1) * EXP], ident)
                last.then_inc(s.up("b2_affinity_flipped"), 1)
                pe.wait_ge(*s.at("b2_slots_ready", 1))
                mm(ps[0][:, 0:1], ones, ones[:, 0:1], start=True, stop=True)
                for c in range(2):
                    last = nc.tensor.transpose(ps[0][:, c * EXP:(c + 1) * EXP], rcum[0:EXP, c * P:(c + 1) * P],
                                               ident[0:EXP, 0:EXP])
                last.then_inc(s.up("b2_slots_flipped"), 1)
                s.end()

                with pe.Fori(0, GROUPS) as g:
                    s = Count(sems, L * GROUPS + g, COUNTS, "g_dve_step")
                    pe.wait_ge(*s.at("g_chosen", 1))
                    for hf in range(2):
                        for q in range(4):
                            k = 4 * hf + q
                            for c in range(2):
                                last = mm(ps[4 + hf][:, q * P:(q + 1) * P], xn[:, c, k * P:(k + 1) * P],
                                          selP[:, c, :, :].rearrange("p e s -> p (e s)"), start=c == 0, stop=c == 1)
                        last.then_inc(s.up("g_rows_done"), 1)
                    pe.wait_ge(*s.at("g_weighted", 1))
                    for c in range(2):
                        last = nc.tensor.transpose(ps[6][:, c * P:(c + 1) * P],
                                                   selG[:, c, :, :].rearrange("p e s -> p (e s)"), ident)
                    last.then_inc(s.up("g_weights_flipped"), 1)
                    pe.wait_ge(*s.at("g_rows_by_dve", 1))
                    pe.wait_ge(*s.at("g_rows_by_act", 1))

                    def experts(part, lhs, bank):
                        for k in range(KD):
                            j = part * KD + k
                            pe.wait_ge(*g_loaded(L, g, j))
                            wt = slot_at(j).rearrange("p (e n) -> p e n", e=EG)
                            for n in range(2):
                                for e in range(EG):
                                    last = mm(ps[bank + n][e * CAP:(e + 1) * CAP, :],
                                              lhs[:, k, e * CAP:(e + 1) * CAP], wt[:, e, n * N:(n + 1) * N],
                                              start=k == 0, stop=k == KD - 1)
                            last.then_inc(tile_done, 1)

                    experts(0, xsT, 0)
                    experts(1, xsT, 2)
                    pe.wait_ge(*s.at("g_hidden_ready", 2))
                    for hf in range(2):
                        for q in range(4):
                            k = 4 * hf + q
                            last = nc.tensor.transpose(ps[4 + hf][:, q * P:(q + 1) * P], hid[:, k * P:(k + 1) * P], ident)
                        last.then_inc(s.up("g_hidden_flipped"), 1)
                    pe.wait_ge(*s.at("g_weights_ready", 1))
                    pe.wait_ge(*s.at("g_hidden_by_dve", 1))
                    pe.wait_ge(*s.at("g_hidden_by_act", 1))
                    experts(2, hidT, 6)
                    pe.wait_ge(*s.at("g_result_by_act", 1))
                    pe.wait_ge(*s.at("g_result_by_dve", 1))
                    for i in range(4):
                        c, n = i // 2, i % 2
                        if i >= 2:
                            pe.wait_ge(*s.at("g_scatter_added", i - 1))
                        mm(ps[4 + i % 2][:, :], pgT[:, c, :], ysb[:, n * N:(n + 1) * N], start=True, stop=True)\
                            .then_inc(s.up("g_scatter_done"), 1)
                    s.end()

        @block.scalar
        def _(act):
            av = nc.scalar.activation
            act.dma_start(tab[:, :], a["tab"]).then_inc(sems["const_loaded"], 16)
            act.dma_start(x[:, :, :], a["x"][0].rearrange("(c p) d -> p c d", p=P)).then_inc(sems["const_loaded"], 16)
            act.dma_start(cols[:, :], a["cols"]).then_inc(sems["const_loaded"], 16)
            act.dma_start(rows[:, :], a["rows"].to_broadcast([P, NROWS])).then_inc(sems["const_loaded"], 16)
            act.wait_ge(sems["rpb_clear"], 1)
            act.dma_start(rpad[0:84, 48:79], a["rpb"]).then_inc(sems["const_loaded"], 16)
            act.wait_ge(sems["const_loaded"], 16 * 5)
            src = rpad[0:84, :].unsqueeze(1).to_broadcast([84, GRID, P])
            act.dma_start(copies.rearrange("l h c m -> (l h) c m"), src).then_inc(sems["rpb_stored"], 16)
            av(csil, cols[:, 2 * NC1:2 * NC1 + 8], ACT.Silu).then_inc(sems["csil"], 1)
            act.wait_ge(sems["rpb_stored"], 16)

            def norm_act(s, pre):
                for c in range(2):
                    nc.scalar.activation(xn[:, c, :], x[:, c, :], ACT.Square, accum_out=ss[:, c:c + 1])\
                        .then_inc(s.up(pre + "sumsq"), 1)

            def evac_hT(s, pre, which, scale, bias):
                for j in (1, 3):
                    act.wait_ge(*s.at(pre + "stream_flipped", 4 * which + j + 1))
                    for i in range(2):
                        k = 2 * j + i
                        kw = dict(bias=bias(k)) if bias else {}
                        av(h8[:, k, :], ps[4 + j][:, i * T:(i + 1) * T], ACT.Identity, scale=scale(k), **kw)\
                            .then_inc(s.up(pre + "stream_by_act"), 1)

            def exps(s, pre, m):
                act.wait_ge(*s.at(pre + "max_ready", m + 1))
                for c in range(2):
                    v = sm[:, m % 3, c * T:(c + 1) * T]
                    i = av(v, v, ACT.Exp, bias=nmx[:, 2 * m + c:2 * m + c + 1],
                           accum_out=den[:, 2 * m + c:2 * m + c + 1])
                    i.then_inc(s.up(pre + "probs_ready" if c else None), 1)

            def pt_copy(s, pre, m, n):
                act.wait_ge(*s.at(pre + "probs_flipped", m + 1))
                if m >= 2:
                    act.wait_ge(*s.at(pre + "out_done", m - 1))
                av(pT[:, m % 2, 0:n], ps[6 + m % 2][:, 0:n], ACT.Copy).then_inc(s.up(pre + "probsT_ready"), 1)

            with act.Fori(0, DEPTH) as L:
                s = Count(sems, L, COUNTS, "b1_act_step")
                act.wait_ge(sems["b1_layer_added"], L + 1)
                act.dma_start(gates[:, :, :].rearrange("p (i n) m -> p i (n m)", i=2),
                              a["b_mod"].rearrange("l (s d) -> l s d", s=6)[bass.ds(L, 1), 2::3, :]
                              .to_broadcast([P, 2, D])).then_inc(sems["b1_gate_bias"], 16)
                norm_act(s, "b1_")
                act.wait_ge(*s.at("b1_lambda_dots", 1))
                av(lamv[:, 2:4], lamv[:, 0:2], ACT.Exp).then_inc(s.up("b1_lambda_exps"), 1)
                act.wait_ge(*s.at("b1_gain_ready", 1))
                evac_hT(s, "b1_", 0, lambda k: acol[:, k:k + 1], lambda k: modc[:, k:k + 1])
                qt = 0
                for j in range(7):
                    act.wait_ge(tile_done, b1_used(L, B1_AT[("in", j)]))
                    w = min(N, IN1 - j * N)
                    av(proj1[:, 0, j * N:j * N + w], ps[2 * (j % 2)][:, 0:w], ACT.Copy)\
                        .then_inc(s.up("b1_proj_by_act"), 1)
                    for _ in range({4: 2, 5: 3}.get(j, 0)):
                        act.wait_ge(*s.at("b1_qk_flipped", qt + 1))
                        av(qkT[:, 2 * qt:2 * qt + 2, :], ps[6 + qt % 2][:, :].rearrange("p (b t) -> p b t", b=2),
                           ACT.Copy).then_inc(s.up("b1_qk_ready"), 1)
                        qt += 1
                act.wait_ge(*s.at("b1_forget_abs", 1))
                av(fe, fz, ACT.Exp, scale=-1.0).then_inc(s.up(), 1)
                act.wait_ge(*s.own())
                av(fe, fe, ACT.Ln, bias=1.0).then_inc(s.up("b1_forget_log"), 1)
                while qt < 8:
                    act.wait_ge(*s.at("b1_qk_flipped", qt + 1))
                    av(qkT[:, 2 * qt:2 * qt + 2, :], ps[6 + qt % 2][:, :].rearrange("p (b t) -> p b t", b=2),
                       ACT.Copy).then_inc(s.up("b1_qk_ready"), 1)
                    qt += 1
                for m in range(MAPS1 + 1):
                    if m < MAPS1:
                        exps(s, "b1_", m)
                    if m >= 1:
                        pt_copy(s, "b1_", m - 1, 384)
                for j in (1, 3):
                    act.wait_ge(*s.at("b1_heads_flipped", j + 1))
                    av(h8[:, 2 * j:2 * j + 2, :], ps[4 + j][:, :].rearrange("p (b t) -> p b t", b=2), ACT.Copy)\
                        .then_inc(s.up("b1_heads_by_act"), 1)
                act.wait_ge(*s.at("b1_mixer_added", 1))
                norm_act(s, "b1_")
                act.wait_ge(*s.at("b1_gain_ready", 2))
                evac_hT(s, "b1_", 1, lambda k: acol[:, 8 + k:9 + k], lambda k: modc[:, 24 + k:25 + k])
                for j in range(UPT):
                    act.wait_ge(*s.at("b1_conv_done", j + 1))
                    if j >= 2:
                        act.wait_ge(*s.at("b1_product_ready", j - 1))
                    av(pT[:, j % 2, :], sm[:, j % 2, :], ACT.Silu).then_inc(s.up("b1_silu_done"), 1)
                s.end()

            act.wait_ge(sems["b1_layer_added"], DEPTH + 1)
            act.dma_start(gbuf[:, 0:D], a["g_final"].to_broadcast([P, D])).then_inc(sems["fin_g"], 16)
            for c in range(2):
                av(xn[:, c, :], x[:, c, :], ACT.Square, accum_out=ss[:, c:c + 1]).then_inc(sems["fin_sumsq"], 1)

            with act.Fori(0, DEPTH) as L:
                s = Count(sems, L, COUNTS, "b2_act_step")
                act.wait_ge(sems["b2_layer_added"], L + 1)
                for c in range(2):
                    for r in range(2):
                        for h in range(NAH):
                            row = 3 - (2 * c + r) + 7 * h
                            base = copies[bass.ds(L, 1), row:row + 4, :, :]
                            src = base.rearrange("l i c m -> (l i) (c m)")[:, 63:63 + 127 * GRID]\
                                .rearrange("i (c m) -> c i m", m=127)[:, :, 0:GRID]
                            act.dma_start(nbias[r * 64:(r + 1) * 64, h, c, :].rearrange("p (i j) -> p i j", i=4), src)\
                               .then_inc(sems["b2_bias_loaded"], 16)
                norm_act(s, "b2_")
                evac_hT(s, "b2_", 0, lambda k: cc2("norm_mix", k), None)
                for j in range(5):
                    act.wait_ge(tile_done, b2_used(L, B2_AT[("in", j)]))
                    w = min(N, IN2 - j * N)
                    av(proj2[:, 0, j * N:j * N + w], ps[2 * (j % 2)][:, 0:w], ACT.Copy)\
                        .then_inc(s.up("b2_proj_by_act"), 1)
                    if j == 2:
                        act.wait_ge(*s.at("b2_proj_by_dve", 3))
                        act.wait_ge(*s.own())
                        for c in range(2):
                            av(sm[:, 2, 0:256], proj2[:, c, CQ2:CQ2 + 256], ACT.Square,
                               accum_out=ss[:, 14 * c + 12:14 * c + 13])\
                                .then_inc(s.up(), 1)
                            act.wait_ge(*s.own())
                            i = av(sm[:, 2, 0:128], proj2[:, c, CKV2:CKV2 + 128], ACT.Square,
                                   accum_out=ss[:, 14 * c + 13:14 * c + 14])
                            i.then_inc(s.up("b2_compressed_sumsq" if c else None), 1)
                            act.wait_ge(*s.own())
                for n, u in enumerate((3, 4, 0, 1, 2)):
                    act.wait_ge(*s.at("b2_qk_flipped", n + 1))
                    for i in range(2 if u < 4 else 1):
                        b = 2 * u + i
                        dst = qkT[:, b, :] if b < 6 else cT[:, b - 6, :]
                        col = cc2("qn") if b < 3 else cc2("kn") if b < 6 else cc2("cq", b - 6) if b < 8 else cc2("ckv")
                        ins = av(dst, ps[6][:, i * T:(i + 1) * T], ACT.Copy, scale=col)
                        ins.then_inc(s.up("b2_qk_ready" if i == (1 if u < 4 else 0) else None), 1)
                for hf in range(2):
                    act.wait_ge(*s.at("b2_uq_done", hf + 1))
                    av(qb[:, 0, hf * 288:(hf + 1) * 288], ps[2 * hf][:, 0:288], ACT.Copy)\
                        .then_inc(s.up("b2_uq_by_act"), 1)
                for hf in range(2):
                    act.wait_ge(*s.at("b2_kv_done", hf + 1))
                    v = ps[4 + 2 * hf][:, 0:384].rearrange("p (h n) -> p h n", h=3)
                    av(kb[:, 0, hf * 288:(hf + 1) * 288].rearrange("p (h n) -> p h n", h=3)[:, :, 0:64],
                       v[:, :, 0:64], ACT.Copy).then_inc(s.up(), 1)
                    av(vb[:, 0, 3 * hf:3 * hf + 3, :], v[:, :, 64:128], ACT.Copy).then_inc(s.up("b2_kv_by_act"), 1)

                def head_copy(m):
                    h = m - NAH
                    act.wait_ge(*s.at("b2_head_flipped", h + 1))
                    av(xqk[m % 2][0:MQK, :], ps[m % 2][0:MQK, :], ACT.Copy).then_inc(s.up("b2_head_ready"), 1)

                for m in range(MAPS2 + 1):
                    if m < MAPS2:
                        exps(s, "b2_", m)
                    if m >= 1:
                        pt_copy(s, "b2_", m - 1, 512)
                    if NAH <= m + 3 < MAPS2:
                        head_copy(m + 3)
                act.wait_ge(*s.at("b2_out_read", MAPS2))
                act.wait_ge(*s.at("b2_conv_ready", 1))
                act.wait_ge(*s.at("b2_out_done", MAPS2))
                for c in range(2):
                    for q, (o, n) in enumerate(((0, 384), (1152, 384), (HC2, 256))):
                        i = av(pT[:, 0, 0:n], proj2[:, c, o:o + n], ACT.Square, accum_out=ss[:, 3 * c + q:3 * c + q + 1])
                        i.then_inc(s.up("b2_mixed_sumsq" if (c, q) == (1, 2) else None), 1)
                        act.wait_ge(*s.own())
                for j in (1, 3):
                    act.wait_ge(*s.at("b2_heads_flipped", j + 1))
                    for i in range(2):
                        k = 2 * j + i
                        av(h8[:, k, :], ps[4 + j][:, i * T:(i + 1) * T], ACT.Copy, scale=cc2("out_norm", k))\
                            .then_inc(s.up("b2_heads_by_act" if i else None), 1)
                act.wait_ge(*s.at("b2_mixer_added", 1))
                norm_act(s, "b2_")
                evac_hT(s, "b2_", 1, lambda k: cc2("norm_ffn", k), None)
                act.wait_ge(*s.at("b2_logits_ready", 1))
                for c in range(2):
                    i = av(affe[:, c * EXP:(c + 1) * EXP], aff[:, c * EXP:(c + 1) * EXP], ACT.Exp,
                           bias=mx2[:, c:c + 1], accum_out=dn2[:, c:c + 1])
                    i.then_inc(s.up("b2_affinity_exps" if c else None), 1)
                s.end()

                with act.Fori(0, GROUPS) as g:
                    s = Count(sems, L * GROUPS + g, COUNTS, "g_act_step")
                    act.wait_ge(*s.at("g_rows_done", 2))
                    for q in range(4):
                        k = 4 + q
                        i = av(xsT[:, k, :], ps[5][:, q * P:(q + 1) * P], ACT.Copy, scale=cc2("norm_ffn", k))
                        i.then_inc(s.up("g_rows_by_act" if q == 3 else None), 1)
                    act.wait_ge(*s.at("g_weights_flipped", 1))
                    av(pgT[:, :, :], ps[6][:, 0:256].rearrange("p (c t) -> p c t", c=2), ACT.Copy)\
                        .then_inc(s.up("g_weights_ready"), 1)
                    act.wait_ge(tile_done, g_used(L, g, KD - 1))
                    for n in range(2):
                        av(hid[:, n * N:(n + 1) * N], ps[n][:, :], ACT.Silu).then_inc(s.up("g_gate_silu"), 1)
                    act.wait_ge(*s.at("g_hidden_flipped", 2))
                    av(hidT[:, 4:8, :], ps[5][:, :].rearrange("p (k s) -> p k s", k=4), ACT.Copy)\
                        .then_inc(s.up("g_hidden_by_act"), 1)
                    act.wait_ge(tile_done, g_used(L, g, G_TILES - 1))
                    av(ysb[:, 0:N], ps[6][:, :], ACT.Copy).then_inc(s.up("g_result_by_act"), 1)
                    s.end()

        @block.gpsimd
        def _(pool):
            gp = nc.gpsimd

            def inv_root(s, n, inv, eps, name):
                gt = nc.gpsimd.tensor_tensor
                gt(tmp28[:, 0:n], ss[:, 0:n], tb(inv)[:, 0:n], ALU.mult).then_inc(s.up(), 1)
                pool.wait_ge(*s.own())
                gt(tmp28[:, 0:n], tmp28[:, 0:n], tb(eps)[:, 0:n], ALU.add).then_inc(s.up(), 1)
                pool.wait_ge(*s.own())
                gt(rs[:, 0:n], tmp28[:, 0:n], tb("half")[:, 0:n], ALU.pow).then_inc(s.up(name), 1)

            def norm_pool(s, pre, which):
                pool.wait_ge(*s.at(pre + "sumsq", 2 * (which + 1)))
                inv_root(s, 2, "invD", "eps6", pre + "rstd")

            gp.memset(hT[:, 0:P], 0.0).then_inc(sems["rpb_clear"], 1)
            pool.wait_ge(sems["const_loaded"], 16 * 5)
            with pool.Fori(0, DEPTH) as L:
                s = Count(sems, L, COUNTS, "b1_pool_step")
                norm_pool(s, "b1_", 0)
                pool.wait_ge(*s.at("b1_diff_sumsq", 1))
                inv_root(s, 8, "inv64", "eps5", "b1_diff_rstd")
                norm_pool(s, "b1_", 1)
                s.end()
            pool.wait_ge(sems["fin_sumsq"], 2)
            inv_root(Count(sems, None, COUNTS, "once_pool"), 2, "invD", "eps6", "fin_rstd")

            with pool.Fori(0, DEPTH) as L:
                s = Count(sems, L, COUNTS, "b2_pool_step")
                pool.wait_ge(*s.at("b2_bias_loaded", 16 * 4 * NAH))
                cm = tb("colmask").unsqueeze(1).to_broadcast([P, 48, GRID])
                nb = gbuf[:, :].rearrange("p (r j) -> p r j", j=GRID)
                gp.tensor_tensor(nb, nb, cm, ALU.add).then_inc(s.up("b2_bias_ready"), 1)
                norm_pool(s, "b2_", 0)
                pool.wait_ge(*s.at("b2_compressed_sumsq", 1))
                pool.wait_ge(*s.at("b2_head_sumsq", 1))
                inv_root(s, 28, "inv14", "eps6", "b2_head_rstd")
                pool.wait_ge(*s.at("b2_proj_by_act", 5))
                pool.wait_ge(*s.at("b2_proj_by_dve", 5))
                t = B2_AT[("small", 0)]
                pool.wait_ge(*b2_loaded(L, t))
                taps = slot_at(t)[:, 2048:2816].rearrange("p (i n) -> p i n", i=3)

                def tap(i):
                    return taps[:, i, :].unsqueeze(1).to_broadcast([P, 2, 256])

                u, v0 = proj2[:, :, HC2:HC2 + 256], proj2[:, :, CC2:CC2 + 256]
                gp.tensor_tensor(u, u, v0, ALU.mult).then_inc(s.up(), 1)
                pool.wait_ge(*s.own())
                gp.tensor_tensor(cv2[:, :, :], u, tap(2), ALU.mult).then_inc(s.up(), 1)
                gp.tensor_tensor(v0, u, tap(0), ALU.mult).then_inc(s.up(), 1)
                pool.wait_ge(*s.own())
                gp.tensor_tensor(u, u, tap(1), ALU.mult).then_inc(s.up("b2_taps_ready"), 1)
                pool.wait_ge(*s.at("b2_latent_sumsq", 1))
                inv_root(s, 24, "inv96", "eps6", "b2_latent_rstd")
                pool.wait_ge(*s.at("b2_mixed_sumsq", 1))
                inv_root(s, 6, "inv3", "eps6", "b2_mixed_rstd")
                norm_pool(s, "b2_", 1)
                s.end()

        @block.vector
        def _(dve):
            tt, ts, stt = nc.vector.tensor_tensor, nc.vector.tensor_scalar, nc.vector.scalar_tensor_tensor
            cp = nc.vector.tensor_copy
            dve.wait_ge(sems["const_loaded"], 16 * 5)
            dve.wait_ge(sems["csil"], 1)
            nc.vector.memset(pad[:, 0:1], 0.0).then_inc(sems["b1_layer_added"], 1)

            def norm_dve(s, pre, which):
                dve.wait_ge(*s.at(pre + "rstd", which + 1))
                for c in range(2):
                    i = nc.vector.tensor_scalar(xn[:, c, :], x[:, c, :], rs[:, c:c + 1], None, ALU.mult)
                    if c == 1:
                        i.then_inc(s.up(pre + "normed"), 1)
                    else:
                        i.then_inc(s.up(), 1)

            def evac_hT(s, pre, which, scale, bias):
                for j in (0, 2):
                    dve.wait_ge(*s.at(pre + "stream_flipped", 4 * which + j + 1))
                    for i in range(2):
                        k = 2 * j + i
                        src = ps[4 + j][:, i * T:(i + 1) * T]
                        ins = ts(h8[:, k, :], src, scale(k), bias(k), ALU.mult, ALU.add) if bias else \
                            ts(h8[:, k, :], src, scale(k), None, ALU.mult)
                        ins.then_inc(s.up(pre + "stream_by_dve"), 1)

            def settle(s):
                dve.wait_ge(*s.own())
                cp(pad[:, 0:1], tb("half")[:, 0:1]).then_inc(s.up(), 1)

            def rope(s, v, c, g, hw, cos, sin, t1, t2):
                cb = cos.unsqueeze(1).unsqueeze(2).to_broadcast([P, g, 2, hw])
                sn = sin.unsqueeze(1).to_broadcast([P, g, hw])
                tt(t1, v, cb, ALU.mult).then_inc(s.up(), 1)
                tt(t2[:, :, 0, :], v[:, :, 1, :], sn, ALU.mult).then_inc(s.up(), 1)
                tt(t2[:, :, 1, :], v[:, :, 0, :], sn, ALU.mult).then_inc(s.up(), 1)
                dve.wait_ge(*s.own())
                tt(v[:, :, 0, :], t1[:, :, 0, :], t2[:, :, 0, :], ALU.subtract).then_inc(s.up(), 1)
                return tt(v[:, :, 1, :], t1[:, :, 1, :], t2[:, :, 1, :], ALU.add)

            def row_max(s, pre, m):
                dve.wait_ge(*s.own())
                nc.vector.tensor_reduce(nmx[:, 2 * m:2 * m + 2], sm[:, m % 3, :].rearrange("p (c k) -> p c k", c=2),
                                        AX.X, ALU.max, negate=True).then_inc(s.up(pre + "max_ready"), 1)

            def out_norm(s, pre, m, dst):
                dve.wait_ge(*s.at(pre + "out_done", m + 1))
                nc.vector.reciprocal(rden[:, 2 * m:2 * m + 2], den[:, 2 * m:2 * m + 2]).then_inc(s.up(), 1)
                dve.wait_ge(*s.own())
                tt(dst, ps[2 + m % 2][:, 0:2 * HD].rearrange("p (c d) -> p c d", c=2),
                   rden[:, 2 * m:2 * m + 2].unsqueeze(2).to_broadcast([P, 2, HD]), ALU.mult)\
                    .then_inc(s.up(pre + "out_read"), 1)

            with dve.Fori(0, DEPTH) as L:
                s = Count(sems, L, COUNTS, "b1_dve_step")
                cp(ccol[:, 0:NC1], cols[:, bass.ds(L * NC1, NC1)]).then_inc(s.up(), 1)
                cp(crow[:, 0:NR1], rows[:, bass.ds(L * NR1, NR1)]).then_inc(s.up(), 1)
                cp(lcur, tab[:, bass.ds(L * 2 + TAB["lam"][0], 2)]).then_inc(s.up(), 1)
                dve.wait_ge(*s.own())
                lr = crow[:, R1["lam"][0]:R1["lam"][0] + 128].rearrange("p (a b d) -> p a b d", a=2, b=2)
                tt(lamt.rearrange("p (a d) -> p a d", a=2), lr[:, :, 0, :], lr[:, :, 1, :], ALU.mult)\
                    .then_inc(s.up(), 1)
                dve.wait_ge(*s.own())
                nc.vector.tensor_reduce(lamv[:, 0:2], lamt.rearrange("p (a d) -> p a d", a=2), AX.X, ALU.add)\
                    .then_inc(s.up("b1_lambda_dots"), 1)

                def accumulate(i):
                    t = B1_AT[("mod", i)]
                    dve.wait_ge(*b1_loaded(L, t))
                    if i >= 2:
                        dve.wait_ge(tile_done, b1_used(L, B1_AT[("mod", i - 2)]))
                    wt = slot_at(t).rearrange("p (k n) -> p k n", k=KD)
                    ts(acc[:, i % 2, :], wt[:, 0, :], csil[:, 0:1], None, ALU.mult).then_inc(s.up(), 1)
                    for k in range(1, KD):
                        dve.wait_ge(*s.own())
                        stt(acc[:, i % 2, :], wt[:, k, :], csil[:, k:k + 1], acc[:, i % 2, :], ALU.mult, ALU.add)\
                            .then_inc(s.up("b1_mod_summed" if k == KD - 1 else None), 1)

                def mod_out(i):
                    dve.wait_ge(tile_done, b1_used(L, B1_AT[("mod", i)]))
                    b = i % 2 if i < 4 else 4 + i % 2
                    if i // 2 in (2, 5):
                        n = i - 4 if i < 6 else i - 8
                        dve.wait_ge(*s.at("b1_gate_bias", 16))
                        tt(gates[:, n, :], ps[b][:, :], gates[:, n, :], ALU.add).then_inc(s.up("b1_mod_ready"), 1)
                    else:
                        tt(modc[:, 4 * i:4 * i + 4], ps[b][:, 0:4], cc1("b_mod", 4 * i, 4), ALU.add)\
                            .then_inc(s.up("b1_mod_ready"), 1)

                def ab(which, g):
                    dve.wait_ge(*s.own())
                    o = 8 + 24 * which
                    stt(acol[:, 8 * which:8 * which + 8], modc[:, o:o + 8], 1.0, cc1(g, 0, 8), ALU.add, ALU.mult)\
                        .then_inc(s.up("b1_gain_ready"), 1)
                    dve.wait_ge(*s.own())

                accumulate(0)
                norm_dve(s, "b1_", 0)
                for i in range(1, 4):
                    accumulate(i)
                    mod_out(i - 1)
                mod_out(3)
                ab(0, "g_attn")
                dve.wait_ge(*s.at("b1_lambda_exps", 1))
                tt(lamv[:, 0:1], lamv[:, 3:4], lamv[:, 2:3], ALU.subtract).then_inc(s.up(), 1)
                dve.wait_ge(*s.own())
                tt(lamv[:, 0:1], lamv[:, 0:1], lcur[:, 0:1], ALU.add).then_inc(s.up(), 1)
                sg = crow[:, 0:64]
                ts(sg, sg, lcur[:, 1:2], None, ALU.mult).then_inc(s.up(), 1)
                evac_hT(s, "b1_", 0, lambda k: acol[:, k:k + 1], lambda k: modc[:, k:k + 1])

                t768 = sm[:, :, :].rearrange("p a n -> p (a n)")
                for j in range(7):
                    if j < 6:
                        accumulate(4 + j)
                    dve.wait_ge(tile_done, b1_used(L, B1_AT[("in", j)]))
                    w = min(N, IN1 - j * N)
                    cp(proj1[:, 1, j * N:j * N + w], ps[2 * (j % 2) + 1][:, 0:w]).then_inc(s.up("b1_proj_by_dve"), 1)
                    if j < 6:
                        mod_out(4 + j)
                    if j == 5:
                        ab(1, "g_mlp")
                    if j in (1, 3):
                        dve.wait_ge(*s.at("b1_proj_by_act", j + 1))
                        kind, g, hw = ("A", 16, 16) if j == 1 else ("B", 12, 32)
                        for c in range(2):
                            n = g * 2 * hw
                            o = B1_Q[kind]
                            v = proj1[:, c, o:o + n].rearrange("p (g a d) -> p g a d", g=g, a=2)
                            t1 = t768[:, 0:n].rearrange("p (g a d) -> p g a d", g=g, a=2)
                            t2 = t768[:, 768:768 + n].rearrange("p (g a d) -> p g a d", g=g, a=2)
                            dve.wait_ge(*s.own())
                            cs = tb("cos" + kind)[:, c * hw:(c + 1) * hw]
                            sn = tb("sin" + kind)[:, c * hw:(c + 1) * hw]
                            ins = rope(s, v, c, g, hw, cs, sn, t1, t2)
                            ins.then_inc(s.up("b1_rotated" if c else None), 1)
                dve.wait_ge(*s.at("b1_proj_by_act", 7))
                f3 = fz.rearrange("p (c h) -> p c h", c=2)
                fb = crow[:, 64:70].unsqueeze(1).to_broadcast([P, 2, 6])
                dve.wait_ge(*s.own())
                tt(f3, proj1[:, :, B1_F:B1_F + 6], fb, ALU.add).then_inc(s.up(), 1)
                dve.wait_ge(*s.own())
                ts(fa, fz, -1.0, 0.0, ALU.mult, ALU.max).then_inc(s.up(), 1)
                dve.wait_ge(*s.own())
                stt(fz, fa, 2.0, fz, ALU.mult, ALU.add).then_inc(s.up("b1_forget_abs"), 1)
                accumulate(10)
                mod_out(10)
                accumulate(11)
                mod_out(11)
                dve.wait_ge(*s.at("b1_forget_log", 1))
                dve.wait_ge(*s.own())
                tt(nlf, fa, fe, ALU.add).then_inc(s.up("b1_forget_ready"), 1)
                for b in range(3):
                    dve.wait_ge(*s.at("b1_cumsum_done", b + 1))
                    cp(nfrow[:, 2 * b:2 * b + 2, :], ps[b][:, :].rearrange("p (h k) -> p h k", h=2))\
                        .then_inc(s.up("b1_cumsum_read"), 1)
                dve.wait_ge(*s.at("b1_cumsum_done", 4))
                cp(nfq, ps[3][:, 0:12]).then_inc(s.up("b1_cumsum_read"), 1)
                dve.wait_ge(*s.own())

                def mask1(m):
                    mp = map1(m)
                    dve.wait_ge(*s.at("b1_scores_done", m + 1))
                    if m >= 3:
                        dve.wait_ge(*s.at("b1_probs_flipped", m - 2))
                    src = ps[4 + m % 2][:, :].rearrange("p (c k) -> p c k", c=2)
                    dst = sm[:, m % 3, :].rearrange("p (c k) -> p c k", c=2)
                    if mp["kind"] != "C":
                        stt(dst, src, mp["scale"], causal if mp["kind"] == "A" else mult, ALU.mult, ALU.add)\
                            .then_inc(s.up("b1_scores_read"), 1)
                    else:
                        h = mp["h"]
                        stt(dst, src, mp["scale"], nfrow[:, h, :].unsqueeze(1).to_broadcast([P, 2, T]),
                            ALU.mult, ALU.add).then_inc(s.up("b1_scores_read"), 1)
                        dve.wait_ge(*s.own())
                        for c in range(2):
                            stt(dst[:, c, :], dst[:, c, :], nfq[:, 6 * c + h:6 * c + h + 1], causal[:, c, :],
                                ALU.subtract, ALU.add).then_inc(s.up(), 1)
                    row_max(s, "b1_", m)

                def out1(m):
                    mp = map1(m)
                    if mp["kind"] == "A":
                        out_norm(s, "b1_", m, oA[:, m // 2, m % 2, :, :])
                    else:
                        o = B1_Q[mp["kind"]] + HD * mp["h"]
                        out_norm(s, "b1_", m, proj1[:, :, o:o + HD])
                    if m == 2 * AH - 1:
                        dve.wait_ge(*s.own())
                        ev, od = oA[:, :, 0, :, :], oA[:, :, 1, :, :]
                        stt(ev, od, lamv[:, 0:1], ev, ALU.mult, ALU.add).then_inc(s.up(), 1)
                        dve.wait_ge(*s.own())
                        tt(od, ev, ev, ALU.mult).then_inc(s.up(), 1)
                        dve.wait_ge(*s.own())
                        nc.vector.tensor_reduce(ss[:, 0:8].rearrange("p (h c) -> p h c", h=AH), od, AX.X, ALU.add)\
                            .then_inc(s.up("b1_diff_sumsq"), 1)
                    if m == 2 * AH + 2:
                        dve.wait_ge(*s.at("b1_diff_rstd", 1))
                        ev = oA[:, :, 0, :, :]
                        r8 = rs[:, 0:8].rearrange("p (h c) -> p h c", h=AH)
                        tt(ev, ev, r8.unsqueeze(3).to_broadcast([P, AH, 2, HD]), ALU.mult).then_inc(s.up(), 1)
                        dve.wait_ge(*s.own())
                        for c in range(2):
                            dst = proj1[:, c, 0:AH * HD].rearrange("p (h d) -> p h d", h=AH)
                            tt(dst, oA[:, :, 0, c, :], sg.unsqueeze(1).to_broadcast([P, AH, HD]), ALU.mult)\
                                .then_inc(s.up("b1_diff_ready" if c else None), 1)

                mask1(0)
                for m in range(MAPS1 + 2):
                    if m + 1 < MAPS1:
                        mask1(m + 1)
                    if m >= 2:
                        out1(m - 2)
                for j in (0, 2):
                    dve.wait_ge(*s.at("b1_heads_flipped", j + 1))
                    cp(h8[:, 2 * j:2 * j + 2, :], ps[4 + j][:, :].rearrange("p (b t) -> p b t", b=2))\
                        .then_inc(s.up("b1_heads_by_dve"), 1)

                def residual(banks, gate, name):
                    for i in range(4):
                        bank, c, n, tile = banks[i]
                        dve.wait_ge(tile_done, b1_used(L, B1_AT[tile]))
                        tmp = sm[:, i % 3, :]
                        tt(tmp, ps[bank][:, :], gates[:, 2 * gate + n, :], ALU.mult).then_inc(s.up(), 1)
                        dve.wait_ge(*s.own())
                        xv = x[:, c, n * N:(n + 1) * N]
                        tt(xv, xv, tmp, ALU.add).then_inc(s.up(name if i == 3 else None), 1)

                residual([(2 * n + c, c, n, ("out", n)) for n in range(2) for c in range(2)], 0, "b1_mixer_added")
                norm_dve(s, "b1_", 1)
                evac_hT(s, "b1_", 1, lambda k: acol[:, 8 + k:9 + k], lambda k: modc[:, 24 + k:25 + k])

                def conv(j):
                    dve.wait_ge(tile_done, b1_used(L, B1_AT[("up", j)]))
                    if j >= 2:
                        dve.wait_ge(*s.at("b1_silu_done", j - 1))
                    y = sm[:, j % 2, :].rearrange("p (f t) -> p f t", f=2)
                    gp = ps[2 * (j % 2) + 1][:, :].rearrange("p (f t) -> p f t", f=2)
                    dve.wait_ge(*s.own())
                    for f in range(2):
                        ts(y[:, f, :], gp[:, f, :], cc1("conv_w", 2 * FCH + 2 * j + f), cc1("conv_b", 2 * j + f),
                           ALU.mult, ALU.add).then_inc(s.up(), 1)
                    for tap_, sh in ((1, 1), (0, 2)):
                        dve.wait_ge(*s.own())
                        for f in range(2):
                            stt(y[:, f, sh:T], gp[:, f, 0:T - sh], cc1("conv_w", tap_ * FCH + 2 * j + f),
                                y[:, f, sh:T], ALU.mult, ALU.add)\
                                .then_inc(s.up("b1_conv_done" if (tap_, f) == (0, 1) else None), 1)

                def product(j):
                    dve.wait_ge(*s.at("b1_silu_done", j + 1))
                    tt(prod[:, 2 * j:2 * j + 2, :], pT[:, j % 2, :].rearrange("p (f t) -> p f t", f=2),
                       ps[2 * (j % 2)][:, :].rearrange("p (f t) -> p f t", f=2), ALU.mult)\
                        .then_inc(s.up("b1_product_ready"), 1)

                conv(0)
                for j in range(UPT):
                    if j + 1 < UPT:
                        conv(j + 1)
                    product(j)
                end = ("down", (FCH + 3) // 4 - 1)
                residual([(4 + 2 * c + n, c, n, end) for c in range(2) for n in range(2)], 1, "b1_layer_added")
                s.end()

            dve.wait_ge(sems["fin_rstd"], 1)
            dve.wait_ge(sems["fin_g"], 16)
            for c in range(2):
                stt(x[:, c, :], x[:, c, :], rs[:, c:c + 1], gbuf[:, 0:D], ALU.mult, ALU.mult)\
                    .then_inc(sems["once_dve" if c == 0 else "b2_layer_added"], 1)

            with dve.Fori(0, DEPTH) as L:
                s = Count(sems, L, COUNTS, "b2_dve_step")
                cp(ccol[:, 0:NC2], cols[:, bass.ds(L * NC2 + (2 * NC1 + 8), NC2)]).then_inc(s.up(), 1)
                cp(crow[:, 0:NR2], rows[:, bass.ds(L * NR2 + 2 * NR1, NR2)]).then_inc(s.up(), 1)
                norm_dve(s, "b2_", 0)
                evac_hT(s, "b2_", 0, lambda k: cc2("norm_mix", k), None)
                ss14 = ss[:, 0:28].rearrange("p (c h) -> p c h", c=2)
                rs14 = rs[:, 0:28].rearrange("p (c h) -> p c h", c=2)
                t768 = sm[:, 0:2, :].rearrange("p a n -> p (a n)")[:, 0:768]
                for j in range(5):
                    dve.wait_ge(tile_done, b2_used(L, B2_AT[("in", j)]))
                    w = min(N, IN2 - j * N)
                    cp(proj2[:, 1, j * N:j * N + w], ps[2 * (j % 2) + 1][:, 0:w]).then_inc(s.up("b2_proj_by_dve"), 1)
                    if j == 1:
                        dve.wait_ge(*s.at("b2_proj_by_act", 2))
                        for c in range(2):
                            dve.wait_ge(*s.own())
                            v = proj2[:, c, 0:768]
                            tt(t768, v, v, ALU.mult).then_inc(s.up(), 1)
                            dve.wait_ge(*s.own())
                            nc.vector.tensor_reduce(ss14[:, c, 0:12], t768.rearrange("p (h d) -> p h d", h=12),
                                                    AX.X, ALU.add)\
                                .then_inc(s.up("b2_head_sumsq" if c else None), 1)
                    if j == 3:
                        dve.wait_ge(*s.at("b2_head_rstd", 1))
                        for c in range(2):
                            v = proj2[:, c, 0:768].rearrange("p (h d) -> p h d", h=12)
                            tt(v, v, rs14[:, c, 0:12].unsqueeze(2).to_broadcast([P, 12, HD]), ALU.mult)\
                                .then_inc(s.up(), 1)
                            for q, (o, n) in enumerate(((CQ2, 256), (CKV2, 128))):
                                v = proj2[:, c, o:o + n]
                                ts(v, v, rs14[:, c, 12 + q:13 + q], None, ALU.mult)\
                                    .then_inc(s.up("b2_heads_normed" if q else None), 1)
                for hf in range(2):
                    dve.wait_ge(*s.at("b2_uq_done", hf + 3))
                    cp(qb[:, 1, hf * 288:(hf + 1) * 288], ps[2 * hf + 1][:, 0:288]).then_inc(s.up("b2_uq_by_dve"), 1)
                for hf in range(2):
                    dve.wait_ge(*s.at("b2_kv_done", hf + 3))
                    v = ps[5 + 2 * hf][:, 0:384].rearrange("p (h n) -> p h n", h=3)
                    cp(kb[:, 1, hf * 288:(hf + 1) * 288].rearrange("p (h n) -> p h n", h=3)[:, :, 0:64],
                       v[:, :, 0:64]).then_inc(s.up(), 1)
                    cp(vb[:, 1, 3 * hf:3 * hf + 3, :], v[:, :, 64:128]).then_inc(s.up("b2_kv_by_dve"), 1)
                dve.wait_ge(*s.at("b2_kv_by_act", 2))
                dve.wait_ge(*s.at("b2_uq_by_act", 2))

                def k6(t, c):
                    return t[:, c, :].rearrange("p (h n) -> p h n", h=MLH)

                for c in range(2):
                    cp(k6(kb, c)[:, :, 64:96],
                       proj2[:, c, KR2:KR2 + 32].unsqueeze(1).to_broadcast([P, MLH, 32]))\
                        .then_inc(s.up(), 1)
                s12 = ss[:, 0:24].rearrange("p (t c h) -> p t c h", t=2, c=2)
                r12 = rs[:, 0:24].rearrange("p (t c h) -> p t c h", t=2, c=2)
                t576 = sm[:, 0:2, :].rearrange("p a n -> p (a n)")[:, 0:576]
                for q, t in enumerate((qb, kb)):
                    for c in range(2):
                        dve.wait_ge(*s.own())
                        tt(t576, t[:, c, :], t[:, c, :], ALU.mult).then_inc(s.up(), 1)
                        dve.wait_ge(*s.own())
                        nc.vector.tensor_reduce(s12[:, q, c, :], t576.rearrange("p (h d) -> p h d", h=MLH),
                                                AX.X, ALU.add)\
                            .then_inc(s.up("b2_latent_sumsq" if (q, c) == (1, 1) else None), 1)
                dve.wait_ge(*s.at("b2_shifts_done", 1))
                u = proj2[:, :, HC2:HC2 + 256]
                tt(u, ps[0][:, :].rearrange("p (c n) -> p c n", c=2), u, ALU.add).then_inc(s.up("b2_shifts_read"), 1)
                dve.wait_ge(*s.own())
                tt(u, u, proj2[:, :, BC2:BC2 + 256], ALU.mult).then_inc(s.up("b2_conv_ready"), 1)
                dve.wait_ge(*s.at("b2_latent_rstd", 1))
                for q, t in enumerate((qb, kb)):
                    gain = crow[:, 96 * q:96 * q + 96].unsqueeze(1).to_broadcast([P, MLH, MQK])
                    for c in range(2):
                        v = k6(t, c)
                        dve.wait_ge(*s.own())
                        tt(v, v, r12[:, q, c, :].unsqueeze(2).to_broadcast([P, MLH, MQK]), ALU.mult)\
                            .then_inc(s.up(), 1)
                        dve.wait_ge(*s.own())
                        tt(v, v, gain, ALU.mult).then_inc(s.up(), 1)
                        dve.wait_ge(*s.own())
                        vr = v[:, :, 64:96].rearrange("p g (a d) -> p g a d", a=2)
                        t1 = t576[:, 0:192].rearrange("p (g a d) -> p g a d", g=MLH, a=2)
                        t2 = t576[:, 192:384].rearrange("p (g a d) -> p g a d", g=MLH, a=2)
                        ins = rope(s, vr, c, MLH, 16, tb("cosM")[:, c * 16:(c + 1) * 16],
                                   tb("sinM")[:, c * 16:(c + 1) * 16], t1, t2)
                        ins.then_inc(s.up("b2_latent_ready" if (q, c) == (1, 1) else None), 1)
                dve.wait_ge(*s.own())
                dve.wait_ge(*s.at("b2_bias_ready", 1))

                def mask2(m):
                    mp = map2(m)
                    dve.wait_ge(*s.at("b2_scores_done", m + 1))
                    if m >= 3:
                        dve.wait_ge(*s.at("b2_probs_flipped", m - 2))
                    src, dst = ps[4 + m % 2][:, :], sm[:, m % 3, :]
                    if m < NAH:
                        stt(dst.rearrange("p (c k) -> p c k", c=2), src.rearrange("p (c k) -> p c k", c=2),
                            mp["scale"], nbias[:, m, :, :], ALU.mult, ALU.add)\
                            .then_inc(s.up("b2_scores_read"), 1)
                    else:
                        ts(dst, src, mp["scale"], None, ALU.mult).then_inc(s.up("b2_scores_read"), 1)
                    row_max(s, "b2_", m)

                def out2(m):
                    o = HD * m if m < NAH else 1152 + HD * (m - NAH)
                    out_norm(s, "b2_", m, proj2[:, :, o:o + HD])

                mask2(0)
                for m in range(MAPS2 + 2):
                    if m + 1 < MAPS2:
                        mask2(m + 1)
                    if m >= 2:
                        out2(m - 2)
                dve.wait_ge(*s.at("b2_mixed_rstd", 1))
                for c in range(2):
                    for q, (o, n) in enumerate(((0, 384), (1152, 384), (HC2, 256))):
                        v = proj2[:, c, o:o + n]
                        ts(v, v, rs[:, 3 * c + q:3 * c + q + 1], None, ALU.mult)\
                            .then_inc(s.up("b2_mixed_ready" if (c, q) == (1, 2) else None), 1)
                for j in (0, 2):
                    dve.wait_ge(*s.at("b2_heads_flipped", j + 1))
                    for i in range(2):
                        k = 2 * j + i
                        ts(h8[:, k, :], ps[4 + j][:, i * T:(i + 1) * T], cc2("out_norm", k), None, ALU.mult)\
                            .then_inc(s.up("b2_heads_by_dve" if i else None), 1)
                for i in range(4):
                    dve.wait_ge(tile_done, b2_used(L, B2_AT[("out", i // 2)]))
                    c, n = i % 2, i // 2
                    xv = x[:, c, n * N:(n + 1) * N]
                    tt(xv, ps[i][:, :], xv, ALU.add).then_inc(s.up("b2_mixer_added" if i == 3 else None), 1)
                norm_dve(s, "b2_", 1)
                evac_hT(s, "b2_", 1, lambda k: cc2("norm_ffn", k), None)
                dve.wait_ge(tile_done, b2_used(L, B2_AT[("small", 0)]))
                a3 = aff.rearrange("p (c e) -> p c e", c=2)
                e3 = affe.rearrange("p (c e) -> p c e", c=2)
                tt(a3, ps[0][:, 0:32].rearrange("p (c e) -> p c e", c=2),
                   crow[:, 192:208].unsqueeze(1).to_broadcast([P, 2, EXP]), ALU.add)\
                    .then_inc(s.up(), 1)
                dve.wait_ge(*s.own())
                nc.vector.tensor_reduce(mx2, a3, AX.X, ALU.max, negate=True).then_inc(s.up("b2_logits_ready"), 1)
                dve.wait_ge(*s.at("b2_affinity_exps", 1))
                nc.vector.reciprocal(rd2, dn2).then_inc(s.up(), 1)
                dve.wait_ge(*s.own())
                tt(a3, e3, rd2.unsqueeze(2).to_broadcast([P, 2, EXP]), ALU.mult).then_inc(s.up("b2_affinity_ready"), 1)
                dve.wait_ge(*s.at("b2_affinity_flipped", 1))
                work, sel, cum = rscratch[0:EXP, :], rsel[0:EXP, :], rcum[0:EXP, :]
                cp(work, ps[1][0:EXP, 0:T]).then_inc(s.up(), 1)
                for r in range(CAP // 8):
                    settle(s)
                    nc.vector.max(m8[0:EXP, :], work).then_inc(s.up(), 1)
                    settle(s)
                    nc.vector.match_replace(work, m8[0:EXP, :], work, -1.0).then_inc(s.up(), 1)
                dve.wait_ge(*s.own())
                ts(sel, work, 0.0, None, ALU.is_lt).then_inc(s.up(), 1)
                dve.wait_ge(*s.own())
                nc.vector.tensor_tensor_scan(cum, ones[0:EXP, 0:1].to_broadcast([EXP, T]), sel, 0.0,
                                             ALU.mult, ALU.add).then_inc(s.up(), 1)
                dve.wait_ge(*s.own())
                tt(cum, cum, sel, ALU.mult).then_inc(s.up("b2_slots_ready"), 1)
                dve.wait_ge(*s.at("b2_slots_flipped", 1))
                cp(slot, ps[0][:, 0:32]).then_inc(s.up(), 1)
                settle(s)
                s.end()

                with dve.Fori(0, GROUPS) as g:
                    s = Count(sems, L * GROUPS + g, COUNTS, "g_dve_step")
                    s3 = slot.rearrange("p (c e) -> p c e", c=2)
                    io = tb("iota").unsqueeze(1).to_broadcast([P, EG, CAP])
                    for c in range(2):
                        tt(selP[:, c, :, :], s3[:, c, bass.ds(g * EG, EG)].unsqueeze(2).to_broadcast([P, EG, CAP]),
                           io, ALU.is_equal).then_inc(s.up("g_chosen" if c else None), 1)
                    dve.wait_ge(*s.own())
                    for c in range(2):
                        tt(selG[:, c, :, :], selP[:, c, :, :],
                           a3[:, c, bass.ds(g * EG, EG)].unsqueeze(2).to_broadcast([P, EG, CAP]),
                           ALU.mult).then_inc(s.up("g_weighted" if c else None), 1)
                    dve.wait_ge(*s.at("g_rows_done", 1))
                    for q in range(4):
                        ts(xsT[:, q, :], ps[4][:, q * P:(q + 1) * P], cc2("norm_ffn", q), None, ALU.mult)\
                            .then_inc(s.up("g_rows_by_dve" if q == 3 else None), 1)
                    dve.wait_ge(*s.at("g_gate_silu", 2))
                    dve.wait_ge(tile_done, g_used(L, g, 2 * KD - 1))
                    for n in range(2):
                        hv = hid[:, n * N:(n + 1) * N]
                        tt(hv, ps[2 + n][:, :], hv, ALU.mult).then_inc(s.up("g_hidden_ready"), 1)
                    dve.wait_ge(*s.at("g_hidden_flipped", 1))
                    cp(hidT[:, 0:4, :], ps[4][:, :].rearrange("p (k s) -> p k s", k=4)).then_inc(s.up("g_hidden_by_dve"), 1)
                    dve.wait_ge(tile_done, g_used(L, g, G_TILES - 1))
                    cp(ysb[:, N:2 * N], ps[7][:, :]).then_inc(s.up("g_result_by_dve"), 1)
                    for i in range(4):
                        dve.wait_ge(*s.at("g_scatter_done", i + 1))
                        c, n = i // 2, i % 2
                        xv = x[:, c, n * N:(n + 1) * N]
                        tt(xv, ps[4 + i % 2][:, :], xv, ALU.add).then_inc(s.up("g_scatter_added"), 1)
                    s.end()
                cp(pad[:, 0:1], tb("half")[:, 0:1]).then_inc(sems["b2_layer_added"], 1)
        if MISCOUNT:
            raise AssertionError(f"counts: {sorted(set(MISCOUNT))}")


def table():
    t = np.zeros((P, NTAB), np.float32)

    def put(name, v):
        o, n = TAB[name]
        t[:, o:o + n] = v.reshape(v.shape[0], n)

    p = np.arange(P)
    put("E", (np.arange(384)[None, :] == p[:, None] + P).astype(np.float32))
    put("ones", np.ones((P, P), np.float32))
    q = (np.arange(2)[None, :, None] * P + p[:, None, None])
    k = np.arange(T)[None, None, :]
    put("causal", np.where(k <= q, 0.0, NEG))
    n = np.zeros((P, 2, T))
    for window, d in ((128, 1), (512, 4), (2048, 16)):
        n += (k <= q) & ((q - k) % d == 0) & ((q - k) // d <= window // d)
    put("mult", np.where(n > 0, np.log(np.maximum(n, 1)), NEG))
    put("tri", (p[:, None] <= np.arange(T)[None, :]).astype(np.float32))
    c = (p % GRID)[:, None]
    start = np.clip(c - 8, 0, GRID - 16)
    j = np.arange(GRID)[None, :]
    put("colmask", np.where((j >= start) & (j < start + 16), 0.0, NEG))
    pos = (np.arange(2)[None, :] * P + p[:, None]).astype(np.float32)[:, :, None]

    def angles(dim, kind):
        if kind == "M":
            inv = np.float32(10000.0) ** (-np.arange(dim // 2, dtype=np.float32) / np.float32(dim // 2))
        else:
            inv = np.float32(1.0) / (np.float32(10000.0) ** (np.arange(0, dim, 2, dtype=np.float32) / np.float32(dim)))
        ang = (pos * inv.astype(np.float32)[None, None, :]).astype(np.float32)
        for fn, name in ((np.cos, "cos"), (np.sin, "sin")):
            v = np.zeros((P, TAB[name + kind][1]), np.float32)
            v[:, 0:dim] = fn(ang).astype(np.float32).reshape(P, dim)
            put(name + kind, v)

    angles(32, "A")
    angles(64, "B")
    angles(32, "M")
    put("iota", np.tile(np.arange(1, CAP + 1, dtype=np.float32)[None, :], (P, 1)))
    for name, v in (("inv14", ([1 / 64] * 12 + [1 / 256, 1 / 128]) * 2), ("inv3", [1 / 384, 1 / 384, 1 / 256] * 2),
                    ("inv64", [1 / HD] * 8), ("inv96", [1 / MQK] * 24), ("invD", [1 / D] * 2), ("eps5", [1e-5] * 8),
                    ("eps6", [1e-6] * 28), ("half", [-0.5] * 28)):
        put(name, np.tile(np.array(v, np.float32)[None, :], (P, 1)))
    li = [0.8 - 0.6 * math.exp(-0.3 * layer) for layer in range(DEPTH)]
    put("lam", np.tile(np.array([v for x in li for v in (-x, 1.0 - x)], np.float32)[None, :], (P, 1)))
    return t


def kernel(**inputs):
    import numpy as _np
    import concourse.bacc as _bacc
    from concourse.bass_utils import run_bass_kernel_spmd as _run

    i = {k: _np.asarray(v) for k, v in inputs.items()}

    def col(v):
        return v.reshape(-1, P).T

    cols, rows = [], []
    for l in range(DEPTH):
        cols += [col(i[n][l]) for n in ("g_attn", "g_mlp", "b_mod", "conv_w", "conv_b")]
        rows += [i["subln_g"][l], i["forget_bias"][l], i["diff_lambda"][l].reshape(-1)]
    cols.append(col(i["c"]))
    for l in range(DEPTH):
        cols += [col(i[n][l]) for n in ("norm_mix_2", "norm_ffn_2", "out_norm_2", "cq_norm_2", "ckv_norm_2")]
        cols += [_np.concatenate([i[n][l], i[n][l]]).reshape(P, 1) for n in ("q_norm_a_2", "k_norm_a_2")]
        rows += [i["q_norm_b_2"][l], i["k_norm_b_2"][l], i["b_router_2"][l]]
    arrays = {
        "x": i["x"], "tab": table(),
        "cols": _np.ascontiguousarray(_np.concatenate(cols, axis=1)),
        "rows": _np.ascontiguousarray(_np.concatenate(rows).reshape(1, NROWS)),
        "rpb": _np.ascontiguousarray(i["rpb_2"][:, :, 4:11, :].reshape(DEPTH * NAH * 7, 31)),
        "g_final": i["g_final"].reshape(1, D),
    }
    for n in ("w_mod", "b_mod", "w_in", "w_out", "w_up", "w_down", "w_in_2", "w_out_2", "w_uq_2", "w_ukv_2",
              "w_router_2", "conv_w_2"):
        arrays[n] = i[n]
    for n in ("w_gate_2", "w_up_2", "w_down_2"):
        arrays[n] = i[n].reshape(DEPTH * EXP, D, EFF)
    nc = _bacc.Bacc("TRN2", target_bir_lowering=False, num_devices=1)
    aps = {n: nc.dram_tensor("in_" + n, v.shape, F32, kind="ExternalInput").ap() for n, v in arrays.items()}
    out = nc.dram_tensor("out", (1, T, D), F32, kind="ExternalOutput").ap()
    two_blocks(nc, aps, out)
    r = _run(nc, [{"in_" + n: v for n, v in arrays.items()}], core_ids=[0])
    return r.results[0]["out"]
```

```python
import math
import numpy as np
import concourse.bass as bass
from concourse import mybir
from contextlib import ExitStack

F32 = mybir.dt.float32
ALU = mybir.AluOpType
ACT = mybir.ActivationFunctionType
AX = mybir.AxisListType

P = 128
T = 256
NC_ = T // P
D = 1024
KD = D // P
DEPTH = 2
N = 512
HD = 64
AH, BH, CH = 4, 6, 6
IN1 = 3078
DFF = 2816
FCH = DFF // P
UPT = FCH // 2
IN2 = 2336
NAH = 6
MLH, MQK = 6, 96
EXP, CAP, EFF = 16, 32, 1024
EG = 4
GRID = 64
NEG = -1.0e30

B1_Q = {"A": 0, "B": 768, "C": 1920}
B1_K = {"A": 256, "B": 1152, "C": 2304}
B1_V = {"A": 512, "B": 1536, "C": 2688}
B1_F = 3072
QA2, KA2, VA2, CQ2, CKV2, KR2, HC2, BC2, CC2 = 0, 384, 768, 1152, 1408, 1536, 1568, 1824, 2080

SLOTS = 6
TILE = 4096
MOD0, MODT = 0, 12
B1_TILES = (
    [("mod", i) for i in range(4)]
    + [("in", 0)] + [t for j in range(1, 7) for t in (("in", j), ("mod", 3 + j))]
    + [("out", i) for i in range(2)]
    + [t for i in range(UPT) for t in ([("up", i)] + ([("mod", 10 + i // 6)] if i in (3, 6) else []))]
    + [("down", i) for i in range((FCH + 3) // 4)]
)
B1_AT = {t: i for i, t in enumerate(B1_TILES)}
B1_N = -(-len(B1_TILES) // SLOTS) * SLOTS
IN2_ORDER = (2, 3, 0, 1, 4)
B2_TILES = [("in", i) for i in IN2_ORDER[0:4]] + [("small", 0), ("in", IN2_ORDER[4]), ("out", 0), ("out", 1)]
B2_AT = {t: i for i, t in enumerate(B2_TILES)}
B2_HEAD = -(-len(B2_TILES) // SLOTS) * SLOTS
G_TILES = 3 * KD
GROUPS = EXP // EG
B2_N = B2_HEAD + GROUPS * G_TILES
assert G_TILES % SLOTS == 0

TAB = {}


def _tab():
    at = 0
    for name, n in (("E", 384), ("ones", P), ("causal", 512), ("mult", 512), ("tri", T), ("colmask", GRID),
                    ("cosA", 64), ("sinA", 64), ("cosB", 128), ("sinB", 128), ("cosM", 64), ("sinM", 64),
                    ("iota", CAP), ("inv3", 6), ("inv64", 24), ("invC", 4), ("inv96", 24), ("invD", 2), ("eps5", 8), ("eps6", 28),
                    ("half", 28), ("lam", 4), ("rows32", 4), ("rows64", 2)):
        TAB[name] = (at, n)
        at += n
    return at


NTAB = _tab()

C1 = {"g_attn": (0, 8), "g_mlp": (8, 8), "b_mod": (16, 48), "conv_w": (64, 66), "conv_b": (130, 22)}
NC1 = 152
C2 = {"norm_mix": (0, 8), "norm_ffn": (8, 8), "out_norm": (16, 8), "cq": (24, 2), "ckv": (26, 1), "qn": (27, 1),
      "kn": (28, 1)}
NC2 = 29
NCOLS = 2 * NC1 + 8 + 2 * NC2
R1 = {"subln": (0, 64), "fb": (64, 6), "lam": (70, 128)}
NR1 = 198
R2 = {"qnb": (0, 96), "knb": (96, 96), "router": (192, 16)}
NR2 = 208
NROWS = 2 * NR1 + 2 * NR2

MAPS1 = 2 * AH + BH + CH
MAPS2 = NAH + MLH
A0 = BH
B1_COUNT = {
    "b1_gate_bias": 16, "b1_dve_step": 0, "b1_act_step": 0, "b1_pool_step": 0,
    "b1_sumsq": 4, "b1_rstd": 2, "b1_normed": 2, "b1_stream_flipped": 8, "b1_stream_by_dve": 8, "b1_stream_by_act": 8,
    "b1_mod_summed": 12, "b1_mod_ready": 12, "b1_gain_ready": 2,
    "b1_proj_by_act": 7, "b1_proj_by_dve": 7, "b1_rotated": 2, "b1_qk_flipped": 8, "b1_qk_ready": 8,
    "b1_forget_abs": 1, "b1_forget_log": 1, "b1_forget_ready": 1, "b1_cumsum_done": 4, "b1_cumsum_read": 4, "b1_lambda_dots": 1, "b1_lambda_exps": 1,
    "b1_scores_done": MAPS1, "b1_scores_read": MAPS1, "b1_max_ready": MAPS1, "b1_probs_ready": MAPS1, "b1_probs_flipped": MAPS1, "b1_probsT_ready": MAPS1,
    "b1_out_done": MAPS1, "b1_out_read": MAPS1, "b1_diff_sumsq": 1, "b1_diff_rstd": 1, "b1_diff_ready": 1,
    "b1_heads_flipped": 4, "b1_heads_by_dve": 2, "b1_heads_by_act": 2, "b1_mixer_added": 1, "b1_layer_added": 1,
    "b1_conv_done": UPT, "b1_silu_done": UPT, "b1_product_ready": UPT,
}
B2_COUNT = {
    "b2_bias_loaded": 16 * 16, "b2_dve_step": 0, "b2_act_step": 0, "b2_pool_step": 0,
    "b2_sumsq": 4, "b2_rstd": 2, "b2_normed": 2, "b2_stream_flipped": 8, "b2_stream_by_dve": 8, "b2_stream_by_act": 8,
    "b2_proj_by_act": 5, "b2_proj_by_dve": 5, "b2_head_sumsq": 1, "b2_compressed_sumsq": 1, "b2_head_rstd": 1, "b2_heads_normed": 1, "b2_compressed_ready": 1, "b2_compressed_rstd": 1, "b2_logits_done": 1, "b2_qk_flipped": 5, "b2_qk_ready": 5,
    "b2_uq_done": 4, "b2_uq_by_act": 2, "b2_uq_by_dve": 2, "b2_kv_done": 4, "b2_kv_by_act": 2, "b2_kv_by_dve": 2,
    "b2_taps_ready": 1, "b2_shifts_done": 1, "b2_shifts_read": 1, "b2_conv_ready": 1, "b2_latent_sumsq": 2, "b2_latent_rstd": 2, "b2_latent_ready": 1,
    "b2_head_flipped": MLH, "b2_head_ready": MLH,
    "b2_scores_done": MAPS2, "b2_scores_read": MAPS2, "b2_max_ready": MAPS2, "b2_probs_ready": MAPS2, "b2_probs_flipped": MAPS2, "b2_probsT_ready": MAPS2,
    "b2_out_done": MAPS2, "b2_out_read": MAPS2, "b2_mixed_sumsq": 1, "b2_mixed_rstd": 1, "b2_mixed_ready": 1,
    "b2_heads_flipped": 4, "b2_heads_by_dve": 2, "b2_heads_by_act": 2, "b2_mixer_added": 1, "b2_layer_added": 1,
    "b2_logits_ready": 1, "b2_affinity_exps": 1, "b2_affinity_ready": 1, "b2_affinity_flipped": 1, "b2_slots_ready": 1, "b2_slots_flipped": 1, "b2_bias_ready": 1,
}
G_COUNT = {
    "g_dve_step": 5, "g_act_step": 3,
    "g_chosen": 1, "g_weighted": 1, "g_rows_done": 2, "g_rows_by_dve": 1, "g_rows_by_act": 1, "g_weights_flipped": 1, "g_weights_ready": 1,
    "g_gate_silu": 2, "g_hidden_ready": 2, "g_hidden_flipped": 2, "g_hidden_by_dve": 1, "g_hidden_by_act": 1, "g_result_by_act": 1, "g_result_by_dve": 1, "g_scatter_done": 4, "g_scatter_added": 4,
}
B1_COUNT.update({"b1_dve_step": 218, "b1_act_step": 41, "b1_pool_step": 6})
B2_COUNT.update({"b2_dve_step": 94, "b2_act_step": 32, "b2_pool_step": 17})
COUNTS = {**B1_COUNT, **B2_COUNT, **G_COUNT}
ONCE = ("const_loaded", "csil", "rpb_clear", "rpb_loaded", "qk_free",
        "router_loaded", "fin_sumsq", "fin_rstd", "x_final", "out_stored", "once_dve", "once_act", "once_pool")
MISCOUNT = []


class Count:

    def __init__(self, sems, turn, counts, step):
        self.sems, self.turn, self.counts, self.step = sems, turn, counts, step
        self.sent, self.last = {}, None

    def at(self, name, k):
        return self.sems[name], k if self.turn is None else self.turn * self.counts[name] + k

    def up(self, name=None):
        name = name or self.step
        self.sent[name] = self.sent.get(name, 0) + 1
        self.last = (name, self.sent[name])
        return self.sems[name]

    def own(self):
        return self.at(*self.last)

    def end(self):
        for name, n in self.sent.items():
            if n != self.counts[name]:
                MISCOUNT.append((name, n, self.counts[name]))


def two_blocks(nc, a, out):
    ctx = ExitStack()
    with ctx:
        def sb(name, shape):
            return ctx.enter_context(nc.sbuf_tensor(name, shape, F32))

        ring = sb("ring", [P, SLOTS, TILE])
        router = sb("router", [P, DEPTH * KD * EXP])
        x = sb("x", [P, NC_, D])
        hT = sb("hT", [P, 2048])
        tab = sb("tab", [P, NTAB])
        cols = sb("cols", [P, NCOLS])
        rows = sb("rows", [P, NROWS])
        ccol = sb("ccol", [P, NC1])
        crow = sb("crow", [P, NR2])
        wide = sb("wide", [P, 6160])
        qk = sb("qk", [P, 7168])
        sm = sb("sm", [P, 3, N])
        pT = sb("pT", [P, 2, N])
        gbuf = sb("gbuf", [P, 3072])
        sc = sb("sc", [P, 768])
        ps = [ctx.enter_context(nc.psum_tensor(f"ps{i}", [P, N], F32)) for i in range(8)]

        small = {}
        at = [0]

        def sm_(name, n):
            small[name] = sc[:, at[0]:at[0] + n]
            at[0] += n
            return small[name]

        csil = sm_("csil", 8)
        ss = sm_("ss", 28)
        rs = sm_("rs", 28)
        tmp28 = sm_("tmp28", 28)
        ssc = sm_("ssc", 4)
        rsc = sm_("rsc", 4)
        ssl = sm_("ssl", 24)
        rsl = sm_("rsl", 24)
        modc = sm_("modc", 48)
        acol = sm_("acol", 16)
        lamv = sm_("lamv", 4)
        lamt = sm_("lamt", 64)
        fz = sm_("fz", 12)
        fa = sm_("fa", 12)
        fe = sm_("fe", 12)
        nlf = sm_("nlf", 12)
        nfq = sm_("nfq", 12)
        den = sm_("den", 40)
        rden = sm_("rden", 40)
        nmx = sm_("nmx", 40)
        lcur = sm_("lcur", 2)
        aff = sm_("aff", 32)
        affe = sm_("affe", 32)
        slot = sm_("slot", 32)
        mx2 = sm_("mx2", 2)
        dn2 = sm_("dn2", 2)
        rd2 = sm_("rd2", 2)
        m8 = sm_("m8", 8)
        pad = sm_("pad", 1)
        kgain = sm_("kgain", 2)
        assert at[0] <= 768

        def tb(name):
            o, n = TAB[name]
            return tab[:, o:o + n]

        E = tb("E")
        ident = E[:, P:2 * P]
        ones = tb("ones")
        tri = tb("tri")
        causal = tb("causal").rearrange("p (c k) -> p c k", c=2)
        mult = tb("mult").rearrange("p (c k) -> p c k", c=2)
        h8 = hT[:, :].rearrange("p (k t) -> p k t", k=KD)
        xn = wide[:, 0:2048].rearrange("p (c d) -> p c d", c=2)
        proj1 = wide[:, 0:2 * IN1].rearrange("p (c n) -> p c n", c=2)
        proj2 = wide[:, 0:2 * IN2].rearrange("p (c n) -> p c n", c=2)
        prod = wide[:, 0:FCH * T].rearrange("p (f t) -> p f t", f=FCH)
        qT = qk[:, 0:2048].rearrange("p (b t) -> p b t", b=8)
        kT = qk[:, 2048:7168].rearrange("p (b t) -> p b t", b=20)
        kN = qk[:, 4096:5632].rearrange("p (b t) -> p b t", b=NAH)
        gates = gbuf[:, 0:2048].rearrange("p (i n) -> p i n", i=4)
        acc = gbuf[:, 2048:3072].rearrange("p (i n) -> p i n", i=2)
        oA = gbuf[:, 2048:3072].rearrange("p (h m c d) -> p h m c d", h=AH, m=2, c=2)
        nbias = gbuf[:, :].rearrange("p (h c k) -> p h c k", h=NAH, c=2)
        nfrow = hT[:, 0:1536].rearrange("p (h k) -> p h k", h=CH)
        cT = qk[:, 1536:2304].rearrange("p (b t) -> p b t", b=3)
        qb = qk[:, 2304:3456].rearrange("p (c n) -> p c n", c=2)
        kb = qk[:, 5632:6784].rearrange("p (c n) -> p c n", c=2)
        xqk = [qk[:, 3456:3968], hT[:, 1152:1664]]
        vb = wide[:, 4672:5440].rearrange("p (c h d) -> p c h d", c=2, h=MLH)
        cv2 = wide[:, 5440:5952].rearrange("p (c n) -> p c n", c=2)
        xsT = wide[:, 2048:3072].rearrange("p (k s) -> p k s", k=KD)
        hid = wide[:, 3072:4096]
        hidT = wide[:, 4096:5120].rearrange("p (k s) -> p k s", k=KD)
        ysb = wide[:, 5120:6144]
        selP = sm[:, 0, 0:256].rearrange("p (c e s) -> p c e s", c=2, e=EG)
        selG = sm[:, 0, 256:512].rearrange("p (c e s) -> p c e s", c=2, e=EG)
        pgT = sm[:, 1, 0:256].rearrange("p (c t) -> p c t", c=2)
        rscratch = sm[:, 2, 0:256]
        rsel = pT[:, 0, 0:256]
        rcum = pT[:, 0, 256:512]
        gfin = qk[:, 0:D]
        rpad = qk[:, 0:128]

        copies = nc.dram_tensor("bias_copies", [DEPTH, NAH * 7, GRID, P], F32, kind="Internal").ap()

        sems = {}
        for name in (*COUNTS, *ONCE, "tile_done"):
            sems[name] = ctx.enter_context(nc.semaphore(name))
        tile_done = sems.pop("tile_done")
        arrived = [ctx.enter_context(nc.semaphore(f"slot_loaded{i}")) for i in range(SLOTS)]

        def arrivals(tiles):
            seen, at_ = [0] * SLOTS, []
            for t, kind in enumerate(tiles):
                n = 32 if kind[0] == "up" or (tiles is B2_TILES and kind == ("in", 0)) else 48 if kind[0] == "small" else 16
                seen[t % SLOTS] += n
                at_.append(seen[t % SLOTS])
            return at_, seen

        B1_ARR, B1_SEEN = arrivals(B1_TILES)
        B2_ARR, B2_HSEEN = arrivals(B2_TILES)
        B2_SEEN = [h + 16 * GROUPS * G_TILES // SLOTS for h in B2_HSEEN]

        def b1_loaded(L, t):
            i = t % SLOTS
            return arrived[i], L * B1_SEEN[i] + B1_ARR[t]

        def b2_loaded(L, t):
            i = t % SLOTS
            return arrived[i], L * B2_SEEN[i] + (DEPTH * B1_SEEN[i] + B2_ARR[t])

        def g_loaded(L, g, j):
            i = j % SLOTS
            first = DEPTH * B1_SEEN[i] + B2_HSEEN[i] + 16 * (j // SLOTS + 1)
            return arrived[i], L * B2_SEEN[i] + g * (16 * G_TILES // SLOTS) + first

        def b1_used(L, t):
            return L * B1_N + (SLOTS + t + 1)

        def b2_used(L, t):
            return L * B2_N + (DEPTH * B1_N + SLOTS + t + 1)

        def g_used(L, g, j):
            return L * B2_N + g * G_TILES + (DEPTH * B1_N + B2_HEAD + SLOTS + j + 1)

        def slot_at(t):
            return ring[:, t % SLOTS, :]

        def cc1(name, i=0, n=1):
            o, _ = C1[name]
            return ccol[:, o + i:o + i + n]

        def cc2(name, i=0, n=1):
            o, _ = C2[name]
            return ccol[:, o + i:o + i + n]

        def map1(m):
            kind, h = ("B", m) if m < A0 else ("A", m - A0) if m < A0 + 2 * AH else ("C", m - A0 - 2 * AH)
            if kind == "A":
                return dict(kind=kind, q=qT[:, h // 4, :], k=kT[:, h, :], v=B1_V["A"] + HD * (h // 2),
                            scale=32 ** -0.5, h=h // 2, part=h % 2)
            o = 0 if kind == "B" else 3
            return dict(kind=kind, q=qT[:, 2 + o + h // 2, :], k=kT[:, 8 + 2 * o + h, :],
                        v=B1_V[kind] + HD * h, scale=HD ** -0.5, h=h)

        def map2(m):
            if m < NAH:
                return dict(kind="N", q=qT[:, m // 2, :], k=kN[:, m, :], scale=HD ** -0.5, h=m)
            t = xqk[m % 2]
            return dict(kind="M", q=t[0:MQK, 0:T], k=t[0:MQK, T:2 * T], scale=MQK ** -0.5, h=m - NAH)

        block = ctx.enter_context(nc.Block())

        @block.sync
        def _(sp):
            sp.dma_start(cols[:, :], a["cols"]).then_inc(sems["const_loaded"], 16)
            sp.dma_start(x[:, :, :], a["x"][0].rearrange("(c p) d -> p c d", p=P)).then_inc(sems["const_loaded"], 16)
            sp.dma_start(rows[:, :], a["rows"].to_broadcast([P, NROWS])).then_inc(sems["const_loaded"], 16)
            sp.dma_start(tab[:, :], a["tab"]).then_inc(sems["const_loaded"], 16)
            sp.dma_start(router[:, :].rearrange("p (k n) -> p k n", n=EXP),
                         a["w_router_2"].rearrange("l (k p) n -> p (l k) n", p=P)).then_inc(sems["router_loaded"], 16)
            with sp.Fori(0, DEPTH) as L:
                for t, (kind, j) in enumerate(B1_TILES):
                    sp.wait_ge(tile_done, L * B1_N + (t + 1))
                    dst = slot_at(t)
                    sem = arrived[t % SLOTS]
                    d8 = dst.rearrange("p (k n) -> p k n", k=KD)
                    if kind == "mod":
                        src = a["w_mod"][bass.ds(L, 1), :, j * N:(j + 1) * N].rearrange("l (k p) n -> p (l k) n", p=P)
                        sp.dma_start(d8, src).then_inc(sem, 16)
                    elif kind == "in":
                        w = min(N, IN1 - j * N)
                        src = a["w_in"][bass.ds(L, 1), :, j * N:j * N + w].rearrange("l (k p) n -> p (l k) n", p=P)
                        sp.dma_start(d8[:, :, 0:w], src).then_inc(sem, 16)
                    elif kind == "out":
                        src = a["w_out"][bass.ds(L, 1), :, j * N:(j + 1) * N].rearrange("l (k p) n -> p (l k) n", p=P)
                        sp.dma_start(d8, src).then_inc(sem, 16)
                    elif kind == "up":
                        for half in range(2):
                            o = half * DFF + j * 256
                            src = a["w_up"][bass.ds(L, 1), :, o:o + 256].rearrange("l (k p) n -> p (l k) n", p=P)
                            sp.dma_start(d8[:, :, half * 256:half * 256 + 256], src).then_inc(sem, 16)
                    else:
                        nf = min(4, FCH - 4 * j)
                        src = a["w_down"][bass.ds(L, 1), 4 * j * P:(4 * j + nf) * P, :]
                        sp.dma_start(dst.rearrange("p (f n) -> p f n", f=4)[:, 0:nf, :],
                                     src.rearrange("l (f p) n -> p (l f) n", p=P)).then_inc(sem, 16)
            sp.wait_ge(sems["qk_free"], 16)
            with sp.Fori(0, DEPTH) as L:
                for t, (kind, j) in enumerate(B2_TILES):
                    sp.wait_ge(tile_done, L * B2_N + (DEPTH * B1_N + t + 1))
                    dst = slot_at(t)
                    sem = arrived[t % SLOTS]
                    d8 = dst.rearrange("p (k n) -> p k n", k=KD)
                    if kind == "in":
                        w = min(N, IN2 - j * N)
                        src = a["w_in_2"][bass.ds(L, 1), :, j * N:j * N + w].rearrange("l (k p) n -> p (l k) n", p=P)
                        if j == 0:
                            sp.dma_start(d8[:, 4:8, 0:w], src[:, 4:8, :]).then_inc(sem, 16)
                            sp.dma_start(d8[:, 0:4, 0:w], src[:, 0:4, :]).then_inc(sem, 16)
                        else:
                            sp.dma_start(d8[:, :, 0:w], src).then_inc(sem, 16)
                    elif kind == "out":
                        src = a["w_out_2"][bass.ds(L, 1), :, j * N:(j + 1) * N].rearrange("l (k p) n -> p (l k) n", p=P)
                        sp.dma_start(d8, src).then_inc(sem, 16)
                    else:
                        sp.dma_start(dst[:, 0:1152].rearrange("p (k n) -> p k n", k=2),
                                     a["w_uq_2"][bass.ds(L, 1)].rearrange("l (k p) n -> p (l k) n", p=P)).then_inc(sem, 16)
                        sp.dma_start(dst[:, 1152:1920].rearrange("p (k n) -> p k n", k=1),
                                     a["w_ukv_2"][bass.ds(L, 1)].rearrange("l p n -> p l n")).then_inc(sem, 16)
                        sp.dma_start(dst[:, 2048:2816],
                                     a["conv_w_2"][bass.ds(L, 1)].rearrange("l i n -> l (i n)").to_broadcast([P, 768])
                                     ).then_inc(sem, 16)
                rel = copies[bass.ds(L, 1)].rearrange("l (h r) c m -> (l h) r (c m)", h=NAH)
                for c in range(2):
                    for r in range(2):
                        for key_row in range(4):
                            src = rel[:, 3 - (2 * c + r) + key_row, 63:63 + 127 * GRID]\
                                .rearrange("h (c m) -> c h m", m=127)[:, :, 0:GRID]
                            dst = nbias[r * 64:(r + 1) * 64, :, c, key_row * GRID:(key_row + 1) * GRID]
                            sp.dma_start(dst, src).then_inc(sems["b2_bias_loaded"], 16)
                with sp.Fori(0, GROUPS) as g:
                    for j in range(G_TILES):
                        sp.wait_ge(tile_done, L * B2_N + g * G_TILES + (DEPTH * B1_N + B2_HEAD + j + 1))
                        w = (a["w_gate_2"], a["w_up_2"], a["w_down_2"])[j // KD]
                        k = j % KD
                        src = w[bass.ds(L * EXP + g * EG, EG), k * P:(k + 1) * P, :].rearrange("e p n -> p e n")
                        sp.dma_start(slot_at(j).rearrange("p (e n) -> p e n", e=EG), src)\
                          .then_inc(arrived[j % SLOTS], 16)
            sp.wait_ge(sems["b2_layer_added"], DEPTH + 1)
            sp.dma_start(out[0].rearrange("(c p) d -> p c d", p=P), x[:, :, :]).then_inc(sems["out_stored"], 16)
            sp.wait_ge(sems["out_stored"], 16)

        @block.tensor
        def _(pe):
            mm = nc.tensor.matmul
            pe.sem_inc(tile_done, SLOTS)
            pe.wait_ge(sems["const_loaded"], 16 * 4)

            def transpose_8(s, src, name, banks=(4, 5, 6, 7)):
                for j in range(4):
                    for i in range(4):
                        k, c = 2 * j + i // 2, i % 2
                        last = nc.tensor.transpose(ps[banks[j]][:, 128 * i:128 * i + 128], src(k, c), ident)
                    last.then_inc(s.up(name), 1)

            def linear(t, i, lhs, w, used=1):
                wt = slot_at(t).rearrange("p (k n) -> p k n", k=KD)
                b = 2 * (i % 2)
                for c in range(2):
                    for k in range(KD):
                        last = mm(ps[b + c][:, 0:w], lhs[:, k, c * P:(c + 1) * P], wt[:, k, 0:w],
                                  start=k == 0, stop=k == KD - 1)
                last.then_inc(tile_done, used)

            def score(s, pre, mp, m):
                if m >= 2:
                    pe.wait_ge(*s.at(pre + "scores_read", m - 1))
                for c in range(2):
                    last = mm(ps[4 + m % 2][:, c * T:(c + 1) * T], mp["q"][:, c * P:(c + 1) * P], mp["k"],
                              start=True, stop=True)
                last.then_inc(s.up(pre + "scores_done"), 1)

            def flip(s, pre, m, blocks):
                pe.wait_ge(*s.at(pre + "probs_ready", m + 1))
                if m >= 2:
                    pe.wait_ge(*s.at(pre + "probsT_ready", m - 1))
                for i, (c, kc) in enumerate(blocks):
                    last = nc.tensor.transpose(ps[6 + m % 2][:, i * P:(i + 1) * P],
                                               sm[:, m % 3, c * T + kc * P:c * T + (kc + 1) * P], ident)
                last.then_inc(s.up(pre + "probs_flipped"), 1)

            def weigh(s, pre, m, blocks, v):
                pe.wait_ge(*s.at(pre + "probsT_ready", m + 1))
                if m >= 2:
                    pe.wait_ge(*s.at(pre + "out_read", m - 1))
                for i, (c, kc) in enumerate(blocks):
                    first = kc == 0
                    final = i + 1 == len(blocks) or blocks[i + 1][0] != c
                    last = mm(ps[2 + m % 2][:, c * HD:(c + 1) * HD], pT[:, m % 2, i * P:(i + 1) * P], v(kc),
                              start=first, stop=final)
                last.then_inc(s.up(pre + "out_done"), 1)

            with pe.Fori(0, DEPTH) as L:
                s = Count(sems, L, COUNTS, "b1_dve_step")

                def modulation(i):
                    b = i % 2 if i < 4 else 4 + i % 2
                    pe.wait_ge(*s.at("b1_mod_summed", i + 1))
                    if i in (4, 5):
                        pe.wait_ge(*s.at("b1_stream_by_dve", 4))
                        pe.wait_ge(*s.at("b1_stream_by_act", 4))
                    elif i >= 2:
                        pe.wait_ge(*s.at("b1_mod_ready", i - 1))
                    if i // 2 in (2, 5):
                        last = mm(ps[b][:, :], ones, acc[:, i % 2, :], start=True, stop=True)
                    else:
                        for q in range(4):
                            last = mm(ps[b][:, q:q + 1], acc[:, i % 2, q * P:(q + 1) * P], ones[:, 0:1],
                                      start=True, stop=True)
                    last.then_inc(tile_done, 1)

                pe.wait_ge(*s.at("b1_normed", 1))
                transpose_8(s, lambda k, c: xn[:, c, k * P:(k + 1) * P], "b1_stream_flipped")
                for i in range(4):
                    modulation(i)
                pe.wait_ge(*s.at("b1_stream_by_dve", 4))
                pe.wait_ge(*s.at("b1_stream_by_act", 4))
                pe.wait_ge(*s.at("b1_mod_ready", 4))

                def qk_flip(u):
                    if u >= 2:
                        pe.wait_ge(*s.at("b1_qk_ready", u - 1))
                    for i in range(4):
                        b, c = 2 * u + i // 2, i % 2
                        kind, o = ("A", b) if b < 4 else ("B", b - 4) if b < 10 else ("C", b - 10)
                        col = B1_Q[kind] + o * P
                        last = nc.tensor.transpose(ps[6 + u % 2][:, i * P:(i + 1) * P],
                                                   proj1[:, c, col:col + P], ident)
                    last.then_inc(s.up("b1_qk_flipped"), 1)

                for j in range(7):
                    t = B1_AT[("in", j)]
                    pe.wait_ge(*b1_loaded(L, t))
                    if j >= 2:
                        pe.wait_ge(*s.at("b1_proj_by_act", j - 1))
                        pe.wait_ge(*s.at("b1_proj_by_dve", j - 1))
                    linear(t, j, h8, min(N, IN1 - j * N))
                    if j >= 1:
                        modulation(3 + j)
                    if j == 4:
                        pe.wait_ge(*s.at("b1_rotated", 1))
                        for u in range(2):
                            qk_flip(u)
                    if j == 5:
                        pe.wait_ge(*s.at("b1_rotated", 2))
                        for u in range(2, 7):
                            qk_flip(u)
                pe.wait_ge(*s.at("b1_proj_by_act", 6))
                pe.wait_ge(*s.at("b1_proj_by_dve", 6))
                qk_flip(7)

                pe.wait_ge(*s.at("b1_forget_ready", 1))
                n2 = nlf.rearrange("p (c h) -> p c h", c=2)
                for h in range(CH):
                    o = ps[h // 2][:, (h % 2) * T:(h % 2 + 1) * T]
                    mm(o[:, 0:P], n2[:, 0, h:h + 1].to_broadcast([P, P]), tri[:, 0:P], start=True, stop=True)
                    mm(o[:, P:T], n2[:, 0, h:h + 1].to_broadcast([P, P]), ones, start=True, stop=False)
                    last = mm(o[:, P:T], n2[:, 1, h:h + 1].to_broadcast([P, P]), tri[:, 0:P], start=False, stop=True)
                    if h % 2:
                        last.then_inc(s.up("b1_cumsum_done"), 1)
                mm(ps[3][:, 0:6], tri[:, 0:P], n2[:, 0, :], start=True, stop=True)
                mm(ps[3][:, 6:12], ones, n2[:, 0, :], start=True, stop=False)
                last = mm(ps[3][:, 6:12], tri[:, 0:P], n2[:, 1, :], start=False, stop=True)
                last.then_inc(s.up("b1_cumsum_done"), 1)

                blocks = [(0, 0), (1, 0), (1, 1)]
                pe.wait_ge(*s.at("b1_mod_ready", 10))
                pe.wait_ge(*s.at("b1_qk_ready", 8))
                pe.wait_ge(*s.at("b1_cumsum_read", 4))
                for m in range(2):
                    score(s, "b1_", map1(m), m)
                for m in range(MAPS1 + 1):
                    if m + 2 < MAPS1:
                        score(s, "b1_", map1(m + 2), m + 2)
                    if m < MAPS1:
                        flip(s, "b1_", m, blocks)
                    if m >= 1:
                        v = map1(m - 1)["v"]
                        weigh(s, "b1_", m - 1, blocks, lambda kc: proj1[:, kc, v:v + HD])

                pe.wait_ge(*s.at("b1_out_read", MAPS1))
                pe.wait_ge(*s.at("b1_diff_ready", 1))
                ocol = [0, 128, 768, 896, 1024, 1920, 2048, 2176]
                transpose_8(s, lambda k, c: proj1[:, c, ocol[k]:ocol[k] + P], "b1_heads_flipped")
                pe.wait_ge(*s.at("b1_heads_by_dve", 2))
                pe.wait_ge(*s.at("b1_heads_by_act", 2))
                for j in range(2):
                    t = B1_AT[("out", j)]
                    pe.wait_ge(*b1_loaded(L, t))
                    linear(t, j, h8, N)

                pe.wait_ge(*s.at("b1_normed", 2))
                transpose_8(s, lambda k, c: xn[:, c, k * P:(k + 1) * P], "b1_stream_flipped")
                pe.wait_ge(*s.at("b1_stream_by_dve", 8))
                pe.wait_ge(*s.at("b1_stream_by_act", 8))
                for j in range(UPT):
                    t = B1_AT[("up", j)]
                    pe.wait_ge(*b1_loaded(L, t))
                    wt = slot_at(t).rearrange("p (k n) -> p k n", k=KD)
                    if j >= 2:
                        pe.wait_ge(*s.at("b1_product_ready", j - 1))
                    for half in (1, 0):
                        for f in range(2):
                            for k in range(KD):
                                o = half * 256 + f * P
                                last = mm(ps[2 * (j % 2) + half][:, f * T:(f + 1) * T], wt[:, k, o:o + P], h8[:, k, :],
                                          start=k == 0, stop=k == KD - 1)
                    last.then_inc(tile_done, 1)
                    if j in (3, 6):
                        modulation(10 + j // 6)
                pe.wait_ge(*s.at("b1_product_ready", UPT))
                nd = (FCH + 3) // 4
                for j in range(nd):
                    t = B1_AT[("down", j)]
                    pe.wait_ge(*b1_loaded(L, t))
                    wt = slot_at(t).rearrange("p (f n) -> p f n", f=4)
                    for q in range(min(4, FCH - 4 * j)):
                        f = 4 * j + q
                        for c in range(2):
                            for n in range(2):
                                last = mm(ps[4 + 2 * c + n][:, :], prod[:, f, c * P:(c + 1) * P],
                                          wt[:, q, n * N:(n + 1) * N], start=f == 0, stop=f == FCH - 1)
                    last.then_inc(tile_done, 1 if j < nd - 1 else 1 + B1_N - len(B1_TILES))
                s.end()

            with pe.Fori(0, DEPTH) as L:
                s = Count(sems, L, COUNTS, "b2_dve_step")
                pe.wait_ge(*s.at("b2_normed", 1))
                transpose_8(s, lambda k, c: xn[:, c, k * P:(k + 1) * P], "b2_stream_flipped")
                pe.wait_ge(*s.at("b2_stream_by_dve", 4))
                pe.wait_ge(*s.at("b2_stream_by_act", 4))

                def block_flip(n, u):
                    if n >= 2:
                        pe.wait_ge(*s.at("b2_qk_ready", n - 1))
                    nb = 2 if u < 4 else 1
                    for i in range(2 * nb):
                        b, c = 2 * u + i // 2, i % 2
                        col = b * P if b < 6 else CQ2 + (b - 6) * P
                        last = nc.tensor.transpose(ps[6 + n % 2][:, i * P:(i + 1) * P], proj2[:, c, col:col + P], ident)
                    last.then_inc(s.up("b2_qk_flipped"), 1)

                small = slot_at(B2_AT[("small", 0)])
                uq = small[:, 0:1152].rearrange("p (k n) -> p k n", k=2)
                ukv = small[:, 1152:1920]
                for i, j in enumerate(IN2_ORDER):
                    t = B2_AT[("in", j)]
                    pe.wait_ge(*b2_loaded(L, t))
                    if i >= 2:
                        pe.wait_ge(*s.at("b2_proj_by_act", i - 1))
                        pe.wait_ge(*s.at("b2_proj_by_dve", i - 1))
                    linear(t, i, h8, min(N, IN2 - j * N), used=2 if i == 4 else 1)
                    if i == 1:
                        pe.wait_ge(*s.at("b2_compressed_ready", 1))
                        block_flip(0, 3)
                        block_flip(1, 4)
                    if i == 2:
                        pe.wait_ge(*b2_loaded(L, B2_AT[("small", 0)]))
                        pe.wait_ge(*s.at("b2_qk_ready", 2))
                        for c in range(2):
                            for hf in range(2):
                                for k in range(2):
                                    last = mm(ps[4 + 2 * hf + c][:, 0:288], cT[:, k, c * P:(c + 1) * P],
                                              uq[:, k, hf * 288:(hf + 1) * 288], start=k == 0, stop=k == 1)
                                last.then_inc(s.up("b2_uq_done"), 1)
                    if i == 3:
                        pe.wait_ge(*s.at("b2_uq_by_act", 2))
                        pe.wait_ge(*s.at("b2_uq_by_dve", 2))
                        for c in range(2):
                            for hf in range(2):
                                last = mm(ps[4 + 2 * hf + c][:, 0:384], cT[:, 2, c * P:(c + 1) * P],
                                          ukv[:, hf * 384:(hf + 1) * 384], start=True, stop=True)
                                last.then_inc(s.up("b2_kv_done"), 1)
                pe.wait_ge(*s.at("b2_kv_by_act", 2))
                pe.wait_ge(*s.at("b2_kv_by_dve", 2))
                pe.wait_ge(*s.at("b2_heads_normed", 1))
                for n in range(3):
                    block_flip(2 + n, n)
                pe.wait_ge(*s.at("b2_qk_ready", 5))

                def shifts():
                    pe.wait_ge(*s.at("b2_taps_ready", 1))
                    pe.wait_ge(*s.at("b2_proj_by_act", 5))
                    v0 = [proj2[:, c, CC2:CC2 + 256] for c in range(2)]
                    v2 = [cv2[:, c, :] for c in range(2)]
                    o = ps[0][:, 0:256]
                    mm(o, E[:, 127:255], v0[0], start=True, stop=False)
                    mm(o, E[:, 129:257], v2[0], start=False, stop=False)
                    mm(o, E[:, 1:129], v2[1], start=False, stop=True)
                    o = ps[0][:, 256:512]
                    mm(o, E[:, 127:255], v0[1], start=True, stop=False)
                    mm(o, E[:, 255:383], v0[0], start=False, stop=False)
                    last = mm(o, E[:, 129:257], v2[1], start=False, stop=True)
                    last.then_inc(s.up("b2_shifts_done"), 1)

                blocks = [(0, 0), (0, 1), (1, 0), (1, 1)]

                def head_flip(m):
                    h = m - NAH
                    if h == 0:
                        pe.wait_ge(*s.at("b2_latent_ready", 1))
                        pe.wait_ge(*s.at("b2_shifts_read", 1))
                    if h >= 2:
                        pe.wait_ge(*s.at("b2_head_ready", h - 1))
                    for i in range(4):
                        src = (qb, kb)[i // 2][:, i % 2, h * MQK:(h + 1) * MQK]
                        last = nc.tensor.transpose(ps[m % 2][0:MQK, i * P:(i + 1) * P], src, ident)
                    last.then_inc(s.up("b2_head_flipped"), 1)

                def score2(m):
                    if m >= NAH:
                        pe.wait_ge(*s.at("b2_head_ready", m - NAH + 1))
                    score(s, "b2_", map2(m), m)

                for m in range(2):
                    score2(m)
                for m in range(MAPS2 + 1):
                    if m == 2:
                        shifts()
                    if NAH <= m + 3 < MAPS2:
                        head_flip(m + 3)
                    if m + 2 < MAPS2:
                        score2(m + 2)
                    if m < MAPS2:
                        flip(s, "b2_", m, blocks)
                    if m >= 1:
                        h = m - 1
                        v = (lambda kc: proj2[:, kc, VA2 + HD * h:VA2 + HD * (h + 1)]) if h < NAH else \
                            (lambda kc: vb[:, kc, h - NAH, :])
                        weigh(s, "b2_", h, blocks, v)

                pe.wait_ge(*s.at("b2_mixed_ready", 1))
                ocol = [0, 128, 256, 1152, 1280, 1408, HC2, HC2 + P]
                transpose_8(s, lambda k, c: proj2[:, c, ocol[k]:ocol[k] + P], "b2_heads_flipped")
                pe.wait_ge(*s.at("b2_heads_by_dve", 2))
                pe.wait_ge(*s.at("b2_heads_by_act", 2))
                for j in range(2):
                    tt = B2_AT[("out", j)]
                    pe.wait_ge(*b2_loaded(L, tt))
                    linear(tt, j, h8, N, used=1 + j * (B2_HEAD - len(B2_TILES)))

                pe.wait_ge(sems["router_loaded"], 16)
                pe.wait_ge(*s.at("b2_normed", 2))
                transpose_8(s, lambda k, c: xn[:, c, k * P:(k + 1) * P], "b2_stream_flipped")
                pe.wait_ge(*s.at("b2_stream_by_dve", 8))
                pe.wait_ge(*s.at("b2_stream_by_act", 8))
                for c in range(2):
                    for k in range(KD):
                        last = mm(ps[0][:, c * EXP:(c + 1) * EXP], h8[:, k, c * P:(c + 1) * P], router[:, bass.ds(L * KD * EXP + k * EXP, EXP)],
                                  start=k == 0, stop=k == KD - 1)
                last.then_inc(s.up("b2_logits_done"), 1)
                pe.wait_ge(*s.at("b2_affinity_ready", 1))
                for c in range(2):
                    last = nc.tensor.transpose(ps[1][0:EXP, c * P:(c + 1) * P], aff[:, c * EXP:(c + 1) * EXP], ident)
                last.then_inc(s.up("b2_affinity_flipped"), 1)
                pe.wait_ge(*s.at("b2_slots_ready", 1))
                mm(ps[0][:, 0:1], ones, ones[:, 0:1], start=True, stop=True)
                for c in range(2):
                    last = nc.tensor.transpose(ps[0][:, c * EXP:(c + 1) * EXP], rcum[0:EXP, c * P:(c + 1) * P],
                                               ident[0:EXP, 0:EXP])
                last.then_inc(s.up("b2_slots_flipped"), 1)
                s.end()

                with pe.Fori(0, GROUPS) as g:
                    s = Count(sems, L * GROUPS + g, COUNTS, "g_dve_step")
                    pe.wait_ge(*s.at("g_chosen", 1))
                    for hf in range(2):
                        for q in range(4):
                            k = 4 * hf + q
                            for c in range(2):
                                last = mm(ps[4 + hf][:, q * P:(q + 1) * P], xn[:, c, k * P:(k + 1) * P],
                                          selP[:, c, :, :].rearrange("p e s -> p (e s)"), start=c == 0, stop=c == 1)
                        last.then_inc(s.up("g_rows_done"), 1)
                    pe.wait_ge(*s.at("g_weighted", 1))
                    for c in range(2):
                        last = nc.tensor.transpose(ps[6][:, c * P:(c + 1) * P],
                                                   selG[:, c, :, :].rearrange("p e s -> p (e s)"), ident)
                    last.then_inc(s.up("g_weights_flipped"), 1)
                    pe.wait_ge(*s.at("g_rows_by_dve", 1))
                    pe.wait_ge(*s.at("g_rows_by_act", 1))

                    def experts(part, lhs, bank):
                        for k in range(KD):
                            j = part * KD + k
                            pe.wait_ge(*g_loaded(L, g, j))
                            wt = slot_at(j).rearrange("p (e n) -> p e n", e=EG)
                            for n in range(2):
                                for e in range(EG):
                                    last = mm(ps[bank + n][e * CAP:(e + 1) * CAP, :],
                                              lhs[:, k, e * CAP:(e + 1) * CAP], wt[:, e, n * N:(n + 1) * N],
                                              start=k == 0, stop=k == KD - 1)
                            last.then_inc(tile_done, 1)

                    experts(0, xsT, 0)
                    experts(1, xsT, 2)
                    pe.wait_ge(*s.at("g_hidden_ready", 2))
                    for hf in range(2):
                        for q in range(4):
                            k = 4 * hf + q
                            last = nc.tensor.transpose(ps[4 + hf][:, q * P:(q + 1) * P], hid[:, k * P:(k + 1) * P], ident)
                        last.then_inc(s.up("g_hidden_flipped"), 1)
                    pe.wait_ge(*s.at("g_weights_ready", 1))
                    pe.wait_ge(*s.at("g_hidden_by_dve", 1))
                    pe.wait_ge(*s.at("g_hidden_by_act", 1))
                    experts(2, hidT, 6)
                    pe.wait_ge(*s.at("g_result_by_act", 1))
                    pe.wait_ge(*s.at("g_result_by_dve", 1))
                    for i in range(4):
                        c, n = i // 2, i % 2
                        if i >= 2:
                            pe.wait_ge(*s.at("g_scatter_added", i - 1))
                        mm(ps[4 + i % 2][:, :], pgT[:, c, :], ysb[:, n * N:(n + 1) * N], start=True, stop=True)\
                            .then_inc(s.up("g_scatter_done"), 1)
                    s.end()

        @block.scalar
        def _(act):
            av = nc.scalar.activation
            act.wait_ge(sems["rpb_clear"], 1)
            act.dma_start(rpad[0:84, 48:79], a["rpb"]).then_inc(sems["rpb_loaded"], 16)
            act.wait_ge(sems["rpb_loaded"], 16)
            src = rpad[0:84, :].unsqueeze(1).to_broadcast([84, GRID, P])
            act.dma_start(copies.rearrange("l h c m -> (l h) c m"), src).then_inc(sems["qk_free"], 16)
            act.wait_ge(sems["const_loaded"], 16 * 4)
            av(csil, cols[:, 2 * NC1:2 * NC1 + 8], ACT.Silu).then_inc(sems["csil"], 1)

            def norm_act(s, pre):
                for c in range(2):
                    nc.scalar.activation(xn[:, c, :], x[:, c, :], ACT.Square, accum_out=ss[:, c:c + 1])\
                        .then_inc(s.up(pre + "sumsq"), 1)

            def evac_hT(s, pre, which, scale, bias):
                for j in (1, 3):
                    act.wait_ge(*s.at(pre + "stream_flipped", 4 * which + j + 1))
                    for i in range(2):
                        k = 2 * j + i
                        kw = dict(bias=bias(k)) if bias else {}
                        av(h8[:, k, :], ps[4 + j][:, i * T:(i + 1) * T], ACT.Identity, scale=scale(k), **kw)\
                            .then_inc(s.up(pre + "stream_by_act"), 1)

            def exps(s, pre, m):
                act.wait_ge(*s.at(pre + "max_ready", m + 1))
                for c in range(2):
                    v = sm[:, m % 3, c * T:(c + 1) * T]
                    i = av(v, v, ACT.Exp, bias=nmx[:, 2 * m + c:2 * m + c + 1],
                           accum_out=den[:, 2 * m + c:2 * m + c + 1])
                    i.then_inc(s.up(pre + "probs_ready" if c else None), 1)

            def pt_copy(s, pre, m, n):
                act.wait_ge(*s.at(pre + "probs_flipped", m + 1))
                if m >= 2:
                    act.wait_ge(*s.at(pre + "out_done", m - 1))
                av(pT[:, m % 2, 0:n], ps[6 + m % 2][:, 0:n], ACT.Copy).then_inc(s.up(pre + "probsT_ready"), 1)

            with act.Fori(0, DEPTH) as L:
                s = Count(sems, L, COUNTS, "b1_act_step")
                act.wait_ge(sems["b1_layer_added"], L + 1)
                act.dma_start(gates[:, :, :].rearrange("p (i n) m -> p i (n m)", i=2),
                              a["b_mod"].rearrange("l (s d) -> l s d", s=6)[bass.ds(L, 1), 2::3, :]
                              .to_broadcast([P, 2, D])).then_inc(sems["b1_gate_bias"], 16)
                norm_act(s, "b1_")
                act.wait_ge(*s.at("b1_lambda_dots", 1))
                av(lamv[:, 2:4], lamv[:, 0:2], ACT.Exp).then_inc(s.up("b1_lambda_exps"), 1)
                act.wait_ge(*s.at("b1_gain_ready", 1))
                evac_hT(s, "b1_", 0, lambda k: acol[:, k:k + 1], lambda k: modc[:, k:k + 1])

                def qk_store(u):
                    act.wait_ge(*s.at("b1_qk_flipped", u + 1))
                    for i in range(2):
                        b, src = 2 * u + i, ps[6 + u % 2][:, i * T:(i + 1) * T]
                        kind, o, w = ("A", b, 2) if b < 4 else ("B", b - 4, 3) if b < 10 else ("C", b - 10, 3)
                        if o < w:
                            qb0 = {"A": 0, "B": 2, "C": 5}[kind]
                            av(qT[:, qb0 + o, :], src, ACT.Copy).then_inc(s.up(None if i == 0 else "b1_qk_ready"), 1)
                        else:
                            kb0, n, rows_of = {"A": (0, 4, "rows32"), "B": (8, 2, "rows64"), "C": (14, 2, "rows64")}[kind]
                            for e in range(n):
                                av(kT[:, kb0 + n * (o - w) + e, :], src, ACT.Copy, scale=tb(rows_of)[:, e:e + 1])\
                                    .then_inc(s.up("b1_qk_ready" if (i, e) == (1, n - 1) else None), 1)

                act.wait_ge(sems["qk_free"], L * 16 + 16)
                for j in range(7):
                    act.wait_ge(tile_done, b1_used(L, B1_AT[("in", j)]))
                    w = min(N, IN1 - j * N)
                    av(proj1[:, 0, j * N:j * N + w], ps[2 * (j % 2)][:, 0:w], ACT.Copy)\
                        .then_inc(s.up("b1_proj_by_act"), 1)
                    for u in {4: range(2), 5: range(2, 7)}.get(j, ()):
                        qk_store(u)
                act.wait_ge(*s.at("b1_forget_abs", 1))
                av(fe, fz, ACT.Exp, scale=-1.0).then_inc(s.up(), 1)
                act.wait_ge(*s.own())
                av(fe, fe, ACT.Ln, bias=1.0).then_inc(s.up("b1_forget_log"), 1)
                qk_store(7)
                for m in range(MAPS1 + 1):
                    if m < MAPS1:
                        exps(s, "b1_", m)
                    if m >= 1:
                        pt_copy(s, "b1_", m - 1, 384)
                for j in (1, 3):
                    act.wait_ge(*s.at("b1_heads_flipped", j + 1))
                    av(h8[:, 2 * j:2 * j + 2, :], ps[4 + j][:, :].rearrange("p (b t) -> p b t", b=2), ACT.Copy)\
                        .then_inc(s.up("b1_heads_by_act"), 1)
                act.dma_start(gfin, a["g_final"].to_broadcast([P, D])).then_inc(sems["qk_free"], 16)
                act.wait_ge(*s.at("b1_mixer_added", 1))
                norm_act(s, "b1_")
                act.wait_ge(*s.at("b1_gain_ready", 2))
                evac_hT(s, "b1_", 1, lambda k: acol[:, 8 + k:9 + k], lambda k: modc[:, 24 + k:25 + k])
                for j in range(UPT):
                    act.wait_ge(*s.at("b1_conv_done", j + 1))
                    if j >= 2:
                        act.wait_ge(*s.at("b1_product_ready", j - 1))
                    av(pT[:, j % 2, :], sm[:, j % 2, :], ACT.Silu).then_inc(s.up("b1_silu_done"), 1)
                s.end()

            act.wait_ge(sems["b1_layer_added"], DEPTH + 1)
            for c in range(2):
                av(xn[:, c, :], x[:, c, :], ACT.Square, accum_out=ss[:, c:c + 1]).then_inc(sems["fin_sumsq"], 1)

            with act.Fori(0, DEPTH) as L:
                s = Count(sems, L, COUNTS, "b2_act_step")
                act.wait_ge(sems["b2_layer_added"], L + 1)
                norm_act(s, "b2_")
                evac_hT(s, "b2_", 0, lambda k: cc2("norm_mix", k), None)
                def block_store(n, u):
                    act.wait_ge(*s.at("b2_qk_flipped", n + 1))
                    for i in range(2 if u < 4 else 1):
                        b = 2 * u + i
                        final = i == (1 if u < 4 else 0)
                        src = ps[6 + n % 2][:, i * T:(i + 1) * T]
                        if 3 <= b < 6:
                            for e in range(2):
                                av(kN[:, 2 * (b - 3) + e, :], src, ACT.Copy, scale=kgain[:, e:e + 1])\
                                    .then_inc(s.up("b2_qk_ready" if final and e else None), 1)
                            continue
                        dst = qT[:, b, :] if b < 3 else cT[:, b - 6, :]
                        col = cc2("qn") if b < 3 else cc2("cq", b - 6) if b < 8 else cc2("ckv")
                        av(dst, src, ACT.Copy, scale=col).then_inc(s.up("b2_qk_ready" if final else None), 1)

                for i, j in enumerate(IN2_ORDER):
                    act.wait_ge(tile_done, b2_used(L, B2_AT[("in", j)]))
                    w = min(N, IN2 - j * N)
                    av(proj2[:, 0, j * N:j * N + w], ps[2 * (i % 2)][:, 0:w], ACT.Copy)\
                        .then_inc(s.up("b2_proj_by_act"), 1)
                    if i == 0:
                        act.wait_ge(*s.at("b2_proj_by_dve", 1))
                        for c in range(2):
                            for q, (o, n) in enumerate(((CQ2, 256), (CKV2, 128))):
                                act.wait_ge(*s.own())
                                av(sm[:, 2, 0:n], proj2[:, c, o:o + n], ACT.Square,
                                   accum_out=ssc[:, 2 * c + q:2 * c + q + 1])\
                                    .then_inc(s.up("b2_compressed_sumsq" if (c, q) == (1, 1) else None), 1)
                    if i == 1:
                        block_store(0, 3)
                        block_store(1, 4)
                    if i == 2:
                        for hf in range(2):
                            act.wait_ge(*s.at("b2_uq_done", hf + 1))
                            av(qb[:, 0, hf * 288:(hf + 1) * 288], ps[4 + 2 * hf][:, 0:288], ACT.Copy)\
                                .then_inc(s.up("b2_uq_by_act"), 1)
                    if i == 3:
                        for hf in range(2):
                            act.wait_ge(*s.at("b2_kv_done", hf + 1))
                            v = ps[4 + 2 * hf][:, 0:384].rearrange("p (h n) -> p h n", h=3)
                            av(kb[:, 0, hf * 288:(hf + 1) * 288].rearrange("p (h n) -> p h n", h=3)[:, :, 0:64],
                               v[:, :, 0:64], ACT.Copy).then_inc(s.up(), 1)
                            av(vb[:, 0, 3 * hf:3 * hf + 3, :], v[:, :, 64:128], ACT.Copy)\
                                .then_inc(s.up("b2_kv_by_act"), 1)
                for n in range(3):
                    block_store(2 + n, n)

                def head_copy(m):
                    h = m - NAH
                    act.wait_ge(*s.at("b2_head_flipped", h + 1))
                    av(xqk[m % 2][0:MQK, :], ps[m % 2][0:MQK, :], ACT.Copy).then_inc(s.up("b2_head_ready"), 1)

                for m in range(MAPS2 + 1):
                    if m < MAPS2:
                        exps(s, "b2_", m)
                    if m >= 1:
                        pt_copy(s, "b2_", m - 1, 512)
                    if NAH <= m + 3 < MAPS2:
                        head_copy(m + 3)
                act.wait_ge(*s.at("b2_out_read", MAPS2))
                act.wait_ge(*s.at("b2_conv_ready", 1))
                act.wait_ge(*s.at("b2_out_done", MAPS2))
                for c in range(2):
                    for q, (o, n) in enumerate(((0, 384), (1152, 384), (HC2, 256))):
                        i = av(pT[:, 0, 0:n], proj2[:, c, o:o + n], ACT.Square, accum_out=ss[:, 3 * c + q:3 * c + q + 1])
                        i.then_inc(s.up("b2_mixed_sumsq" if (c, q) == (1, 2) else None), 1)
                        act.wait_ge(*s.own())
                for j in (1, 3):
                    act.wait_ge(*s.at("b2_heads_flipped", j + 1))
                    for i in range(2):
                        k = 2 * j + i
                        av(h8[:, k, :], ps[4 + j][:, i * T:(i + 1) * T], ACT.Copy, scale=cc2("out_norm", k))\
                            .then_inc(s.up("b2_heads_by_act" if i else None), 1)
                act.wait_ge(*s.at("b2_mixer_added", 1))
                norm_act(s, "b2_")
                evac_hT(s, "b2_", 1, lambda k: cc2("norm_ffn", k), None)
                act.wait_ge(*s.at("b2_logits_ready", 1))
                for c in range(2):
                    i = av(affe[:, c * EXP:(c + 1) * EXP], aff[:, c * EXP:(c + 1) * EXP], ACT.Exp,
                           bias=mx2[:, c:c + 1], accum_out=dn2[:, c:c + 1])
                    i.then_inc(s.up("b2_affinity_exps" if c else None), 1)
                s.end()

                with act.Fori(0, GROUPS) as g:
                    s = Count(sems, L * GROUPS + g, COUNTS, "g_act_step")
                    act.wait_ge(*s.at("g_rows_done", 2))
                    for q in range(4):
                        k = 4 + q
                        i = av(xsT[:, k, :], ps[5][:, q * P:(q + 1) * P], ACT.Copy, scale=cc2("norm_ffn", k))
                        i.then_inc(s.up("g_rows_by_act" if q == 3 else None), 1)
                    act.wait_ge(*s.at("g_weights_flipped", 1))
                    av(pgT[:, :, :], ps[6][:, 0:256].rearrange("p (c t) -> p c t", c=2), ACT.Copy)\
                        .then_inc(s.up("g_weights_ready"), 1)
                    act.wait_ge(tile_done, g_used(L, g, KD - 1))
                    for n in range(2):
                        av(hid[:, n * N:(n + 1) * N], ps[n][:, :], ACT.Silu).then_inc(s.up("g_gate_silu"), 1)
                    act.wait_ge(*s.at("g_hidden_flipped", 2))
                    av(hidT[:, 4:8, :], ps[5][:, :].rearrange("p (k s) -> p k s", k=4), ACT.Copy)\
                        .then_inc(s.up("g_hidden_by_act"), 1)
                    act.wait_ge(tile_done, g_used(L, g, G_TILES - 1))
                    av(ysb[:, 0:N], ps[6][:, :], ACT.Copy).then_inc(s.up("g_result_by_act"), 1)
                    s.end()

        @block.gpsimd
        def _(pool):
            gp = nc.gpsimd

            def inv_root(s, n, inv, eps, name, src=ss, dst=rs):
                gt = nc.gpsimd.tensor_tensor
                gt(tmp28[:, 0:n], src[:, 0:n], tb(inv)[:, 0:n], ALU.mult).then_inc(s.up(), 1)
                pool.wait_ge(*s.own())
                gt(tmp28[:, 0:n], tmp28[:, 0:n], tb(eps)[:, 0:n], ALU.add).then_inc(s.up(), 1)
                pool.wait_ge(*s.own())
                gt(dst[:, 0:n], tmp28[:, 0:n], tb("half")[:, 0:n], ALU.pow).then_inc(s.up(name), 1)

            def norm_pool(s, pre, which):
                pool.wait_ge(*s.at(pre + "sumsq", 2 * (which + 1)))
                inv_root(s, 2, "invD", "eps6", pre + "rstd")

            gp.memset(rpad, 0.0).then_inc(sems["rpb_clear"], 1)
            pool.wait_ge(sems["const_loaded"], 16 * 4)
            with pool.Fori(0, DEPTH) as L:
                s = Count(sems, L, COUNTS, "b1_pool_step")
                norm_pool(s, "b1_", 0)
                pool.wait_ge(*s.at("b1_diff_sumsq", 1))
                inv_root(s, 8, "inv64", "eps5", "b1_diff_rstd")
                norm_pool(s, "b1_", 1)
                s.end()
            pool.wait_ge(sems["fin_sumsq"], 2)
            inv_root(Count(sems, None, COUNTS, "once_pool"), 2, "invD", "eps6", "fin_rstd")

            with pool.Fori(0, DEPTH) as L:
                s = Count(sems, L, COUNTS, "b2_pool_step")
                norm_pool(s, "b2_", 0)
                pool.wait_ge(*s.at("b2_compressed_sumsq", 1))
                inv_root(s, 4, "invC", "eps6", "b2_compressed_rstd", ssc, rsc)
                pool.wait_ge(*s.at("b2_bias_loaded", 16 * 16))
                cm = tb("colmask").unsqueeze(1).to_broadcast([P, 48, GRID])
                nb = gbuf[:, :].rearrange("p (r j) -> p r j", j=GRID)
                gp.tensor_tensor(nb, nb, cm, ALU.add).then_inc(s.up("b2_bias_ready"), 1)
                pool.wait_ge(*s.at("b2_latent_sumsq", 1))
                inv_root(s, 12, "inv96", "eps6", "b2_latent_rstd", ssl, rsl)
                pool.wait_ge(*s.at("b2_head_sumsq", 1))
                inv_root(s, 24, "inv64", "eps6", "b2_head_rstd")
                pool.wait_ge(*s.at("b2_proj_by_act", 5))
                pool.wait_ge(*s.at("b2_proj_by_dve", 5))
                t = B2_AT[("small", 0)]
                pool.wait_ge(*b2_loaded(L, t))
                taps = slot_at(t)[:, 2048:2816].rearrange("p (i n) -> p i n", i=3)

                def tap(i):
                    return taps[:, i, :].unsqueeze(1).to_broadcast([P, 2, 256])

                pool.wait_ge(*s.at("b2_latent_sumsq", 2))
                inv_root(s, 12, "inv96", "eps6", "b2_latent_rstd", ssl[:, 12:24], rsl[:, 12:24])
                u, v0 = proj2[:, :, HC2:HC2 + 256], proj2[:, :, CC2:CC2 + 256]
                gp.tensor_tensor(u, u, v0, ALU.mult).then_inc(s.up(), 1)
                pool.wait_ge(*s.own())
                gp.tensor_tensor(cv2[:, :, :], u, tap(2), ALU.mult).then_inc(s.up(), 1)
                gp.tensor_tensor(v0, u, tap(0), ALU.mult).then_inc(s.up(), 1)
                pool.wait_ge(*s.own())
                gp.tensor_tensor(u, u, tap(1), ALU.mult).then_inc(s.up("b2_taps_ready"), 1)
                pool.wait_ge(*s.at("b2_mixed_sumsq", 1))
                inv_root(s, 6, "inv3", "eps6", "b2_mixed_rstd")
                norm_pool(s, "b2_", 1)
                s.end()

        @block.vector
        def _(dve):
            tt, ts, stt = nc.vector.tensor_tensor, nc.vector.tensor_scalar, nc.vector.scalar_tensor_tensor
            cp = nc.vector.tensor_copy
            dve.wait_ge(sems["const_loaded"], 16 * 4)
            dve.wait_ge(sems["csil"], 1)
            nc.vector.memset(pad[:, 0:1], 0.0).then_inc(sems["b1_layer_added"], 1)

            def norm_dve(s, pre, which):
                dve.wait_ge(*s.at(pre + "rstd", which + 1))
                for c in range(2):
                    i = nc.vector.tensor_scalar(xn[:, c, :], x[:, c, :], rs[:, c:c + 1], None, ALU.mult)
                    if c == 1:
                        i.then_inc(s.up(pre + "normed"), 1)
                    else:
                        i.then_inc(s.up(), 1)

            def evac_hT(s, pre, which, scale, bias):
                for j in (0, 2):
                    dve.wait_ge(*s.at(pre + "stream_flipped", 4 * which + j + 1))
                    for i in range(2):
                        k = 2 * j + i
                        src = ps[4 + j][:, i * T:(i + 1) * T]
                        ins = ts(h8[:, k, :], src, scale(k), bias(k), ALU.mult, ALU.add) if bias else \
                            ts(h8[:, k, :], src, scale(k), None, ALU.mult)
                        ins.then_inc(s.up(pre + "stream_by_dve"), 1)

            def settle(s):
                dve.wait_ge(*s.own())
                cp(pad[:, 0:1], tb("half")[:, 0:1]).then_inc(s.up(), 1)

            def rope(s, v, c, g, hw, cos, sin, t1, t2):
                cb = cos.unsqueeze(1).unsqueeze(2).to_broadcast([P, g, 2, hw])
                sn = sin.unsqueeze(1).to_broadcast([P, g, hw])
                tt(t1, v, cb, ALU.mult).then_inc(s.up(), 1)
                tt(t2[:, :, 0, :], v[:, :, 1, :], sn, ALU.mult).then_inc(s.up(), 1)
                tt(t2[:, :, 1, :], v[:, :, 0, :], sn, ALU.mult).then_inc(s.up(), 1)
                dve.wait_ge(*s.own())
                tt(v[:, :, 0, :], t1[:, :, 0, :], t2[:, :, 0, :], ALU.subtract).then_inc(s.up(), 1)
                return tt(v[:, :, 1, :], t1[:, :, 1, :], t2[:, :, 1, :], ALU.add)

            def row_max(s, pre, m):
                dve.wait_ge(*s.own())
                nc.vector.tensor_reduce(nmx[:, 2 * m:2 * m + 2], sm[:, m % 3, :].rearrange("p (c k) -> p c k", c=2),
                                        AX.X, ALU.max, negate=True).then_inc(s.up(pre + "max_ready"), 1)

            def out_norm(s, pre, m, dst):
                dve.wait_ge(*s.at(pre + "out_done", m + 1))
                nc.vector.reciprocal(rden[:, 2 * m:2 * m + 2], den[:, 2 * m:2 * m + 2]).then_inc(s.up(), 1)
                dve.wait_ge(*s.own())
                tt(dst, ps[2 + m % 2][:, 0:2 * HD].rearrange("p (c d) -> p c d", c=2),
                   rden[:, 2 * m:2 * m + 2].unsqueeze(2).to_broadcast([P, 2, HD]), ALU.mult)\
                    .then_inc(s.up(pre + "out_read"), 1)

            with dve.Fori(0, DEPTH) as L:
                s = Count(sems, L, COUNTS, "b1_dve_step")
                cp(ccol[:, 0:NC1], cols[:, bass.ds(L * NC1, NC1)]).then_inc(s.up(), 1)
                cp(crow[:, 0:NR1], rows[:, bass.ds(L * NR1, NR1)]).then_inc(s.up(), 1)
                cp(lcur, tab[:, bass.ds(L * 2 + TAB["lam"][0], 2)]).then_inc(s.up(), 1)
                dve.wait_ge(*s.own())
                lr = crow[:, R1["lam"][0]:R1["lam"][0] + 128].rearrange("p (a b d) -> p a b d", a=2, b=2)
                tt(lamt.rearrange("p (a d) -> p a d", a=2), lr[:, :, 0, :], lr[:, :, 1, :], ALU.mult)\
                    .then_inc(s.up(), 1)
                dve.wait_ge(*s.own())
                nc.vector.tensor_reduce(lamv[:, 0:2], lamt.rearrange("p (a d) -> p a d", a=2), AX.X, ALU.add)\
                    .then_inc(s.up("b1_lambda_dots"), 1)

                def accumulate(i):
                    t = B1_AT[("mod", i)]
                    dve.wait_ge(*b1_loaded(L, t))
                    if i >= 2:
                        dve.wait_ge(tile_done, b1_used(L, B1_AT[("mod", i - 2)]))
                    wt = slot_at(t).rearrange("p (k n) -> p k n", k=KD)
                    ts(acc[:, i % 2, :], wt[:, 0, :], csil[:, 0:1], None, ALU.mult).then_inc(s.up(), 1)
                    for k in range(1, KD):
                        dve.wait_ge(*s.own())
                        stt(acc[:, i % 2, :], wt[:, k, :], csil[:, k:k + 1], acc[:, i % 2, :], ALU.mult, ALU.add)\
                            .then_inc(s.up("b1_mod_summed" if k == KD - 1 else None), 1)

                def mod_out(i):
                    dve.wait_ge(tile_done, b1_used(L, B1_AT[("mod", i)]))
                    b = i % 2 if i < 4 else 4 + i % 2
                    if i // 2 in (2, 5):
                        n = i - 4 if i < 6 else i - 8
                        dve.wait_ge(*s.at("b1_gate_bias", 16))
                        tt(gates[:, n, :], ps[b][:, :], gates[:, n, :], ALU.add).then_inc(s.up("b1_mod_ready"), 1)
                    else:
                        tt(modc[:, 4 * i:4 * i + 4], ps[b][:, 0:4], cc1("b_mod", 4 * i, 4), ALU.add)\
                            .then_inc(s.up("b1_mod_ready"), 1)

                def ab(which, g):
                    dve.wait_ge(*s.own())
                    o = 8 + 24 * which
                    stt(acol[:, 8 * which:8 * which + 8], modc[:, o:o + 8], 1.0, cc1(g, 0, 8), ALU.add, ALU.mult)\
                        .then_inc(s.up("b1_gain_ready"), 1)
                    dve.wait_ge(*s.own())

                norm_dve(s, "b1_", 0)
                for i in range(4):
                    accumulate(i)
                    if i >= 1:
                        mod_out(i - 1)
                mod_out(3)
                ab(0, "g_attn")
                dve.wait_ge(*s.at("b1_lambda_exps", 1))
                tt(lamv[:, 0:1], lamv[:, 3:4], lamv[:, 2:3], ALU.subtract).then_inc(s.up(), 1)
                dve.wait_ge(*s.own())
                tt(lamv[:, 0:1], lamv[:, 0:1], lcur[:, 0:1], ALU.add).then_inc(s.up(), 1)
                sg = crow[:, 0:64]
                ts(sg, sg, lcur[:, 1:2], None, ALU.mult).then_inc(s.up(), 1)
                evac_hT(s, "b1_", 0, lambda k: acol[:, k:k + 1], lambda k: modc[:, k:k + 1])

                t768 = sm[:, :, :].rearrange("p a n -> p (a n)")
                for j in range(7):
                    if j >= 1:
                        accumulate(3 + j)
                    dve.wait_ge(tile_done, b1_used(L, B1_AT[("in", j)]))
                    w = min(N, IN1 - j * N)
                    cp(proj1[:, 1, j * N:j * N + w], ps[2 * (j % 2) + 1][:, 0:w]).then_inc(s.up("b1_proj_by_dve"), 1)
                    if j >= 1:
                        mod_out(3 + j)
                    if j == 6:
                        ab(1, "g_mlp")
                    if j in (1, 3):
                        dve.wait_ge(*s.at("b1_proj_by_act", j + 1))
                        kind, g, hw = ("A", 16, 16) if j == 1 else ("B", 12, 32)
                        for c in range(2):
                            n = g * 2 * hw
                            o = B1_Q[kind]
                            v = proj1[:, c, o:o + n].rearrange("p (g a d) -> p g a d", g=g, a=2)
                            t1 = t768[:, 0:n].rearrange("p (g a d) -> p g a d", g=g, a=2)
                            t2 = t768[:, 768:768 + n].rearrange("p (g a d) -> p g a d", g=g, a=2)
                            dve.wait_ge(*s.own())
                            cs = tb("cos" + kind)[:, c * hw:(c + 1) * hw]
                            sn = tb("sin" + kind)[:, c * hw:(c + 1) * hw]
                            ins = rope(s, v, c, g, hw, cs, sn, t1, t2)
                            ins.then_inc(s.up("b1_rotated" if c else None), 1)
                dve.wait_ge(*s.at("b1_proj_by_act", 7))
                f3 = fz.rearrange("p (c h) -> p c h", c=2)
                fb = crow[:, 64:70].unsqueeze(1).to_broadcast([P, 2, 6])
                dve.wait_ge(*s.own())
                tt(f3, proj1[:, :, B1_F:B1_F + 6], fb, ALU.add).then_inc(s.up(), 1)
                dve.wait_ge(*s.own())
                ts(fa, fz, -1.0, 0.0, ALU.mult, ALU.max).then_inc(s.up(), 1)
                dve.wait_ge(*s.own())
                stt(fz, fa, 2.0, fz, ALU.mult, ALU.add).then_inc(s.up("b1_forget_abs"), 1)
                dve.wait_ge(*s.at("b1_forget_log", 1))
                dve.wait_ge(*s.own())
                tt(nlf, fa, fe, ALU.add).then_inc(s.up("b1_forget_ready"), 1)
                for b in range(3):
                    dve.wait_ge(*s.at("b1_cumsum_done", b + 1))
                    cp(nfrow[:, 2 * b:2 * b + 2, :], ps[b][:, :].rearrange("p (h k) -> p h k", h=2))\
                        .then_inc(s.up("b1_cumsum_read"), 1)
                dve.wait_ge(*s.at("b1_cumsum_done", 4))
                cp(nfq, ps[3][:, 0:12]).then_inc(s.up("b1_cumsum_read"), 1)
                dve.wait_ge(*s.own())

                def mask1(m):
                    mp = map1(m)
                    dve.wait_ge(*s.at("b1_scores_done", m + 1))
                    if m >= 3:
                        dve.wait_ge(*s.at("b1_probs_flipped", m - 2))
                    src = ps[4 + m % 2][:, :].rearrange("p (c k) -> p c k", c=2)
                    dst = sm[:, m % 3, :].rearrange("p (c k) -> p c k", c=2)
                    if mp["kind"] != "C":
                        stt(dst, src, mp["scale"], causal if mp["kind"] == "A" else mult, ALU.mult, ALU.add)\
                            .then_inc(s.up("b1_scores_read"), 1)
                    else:
                        h = mp["h"]
                        stt(dst, src, mp["scale"], nfrow[:, h, :].unsqueeze(1).to_broadcast([P, 2, T]),
                            ALU.mult, ALU.add).then_inc(s.up("b1_scores_read"), 1)
                        dve.wait_ge(*s.own())
                        for c in range(2):
                            stt(dst[:, c, :], dst[:, c, :], nfq[:, 6 * c + h:6 * c + h + 1], causal[:, c, :],
                                ALU.subtract, ALU.add).then_inc(s.up(), 1)
                    row_max(s, "b1_", m)

                def out1(m):
                    mp = map1(m)
                    if mp["kind"] == "A":
                        out_norm(s, "b1_", m, oA[:, mp["h"], mp["part"], :, :])
                    else:
                        o = B1_Q[mp["kind"]] + HD * mp["h"]
                        out_norm(s, "b1_", m, proj1[:, :, o:o + HD])
                    if m == A0 + 2 * AH - 1:
                        dve.wait_ge(*s.own())
                        ev, od = oA[:, :, 0, :, :], oA[:, :, 1, :, :]
                        stt(ev, od, lamv[:, 0:1], ev, ALU.mult, ALU.add).then_inc(s.up(), 1)
                        dve.wait_ge(*s.own())
                        tt(od, ev, ev, ALU.mult).then_inc(s.up(), 1)
                        dve.wait_ge(*s.own())
                        nc.vector.tensor_reduce(ss[:, 0:8].rearrange("p (h c) -> p h c", h=AH), od, AX.X, ALU.add)\
                            .then_inc(s.up("b1_diff_sumsq"), 1)
                    if m == A0 + 2 * AH + 2:
                        dve.wait_ge(*s.at("b1_diff_rstd", 1))
                        ev = oA[:, :, 0, :, :]
                        r8 = rs[:, 0:8].rearrange("p (h c) -> p h c", h=AH)
                        tt(ev, ev, r8.unsqueeze(3).to_broadcast([P, AH, 2, HD]), ALU.mult).then_inc(s.up(), 1)
                        dve.wait_ge(*s.own())
                        for c in range(2):
                            dst = proj1[:, c, 0:AH * HD].rearrange("p (h d) -> p h d", h=AH)
                            tt(dst, oA[:, :, 0, c, :], sg.unsqueeze(1).to_broadcast([P, AH, HD]), ALU.mult)\
                                .then_inc(s.up("b1_diff_ready" if c else None), 1)

                mask1(0)
                for m in range(MAPS1 + 2):
                    if m + 1 < MAPS1:
                        mask1(m + 1)
                    if m >= 2:
                        out1(m - 2)
                for j in (0, 2):
                    dve.wait_ge(*s.at("b1_heads_flipped", j + 1))
                    cp(h8[:, 2 * j:2 * j + 2, :], ps[4 + j][:, :].rearrange("p (b t) -> p b t", b=2))\
                        .then_inc(s.up("b1_heads_by_dve"), 1)

                def residual(banks, gate, name):
                    for i in range(4):
                        bank, c, n, tile = banks[i]
                        dve.wait_ge(tile_done, b1_used(L, B1_AT[tile]))
                        tmp = sm[:, i % 3, :]
                        tt(tmp, ps[bank][:, :], gates[:, 2 * gate + n, :], ALU.mult).then_inc(s.up(), 1)
                        dve.wait_ge(*s.own())
                        xv = x[:, c, n * N:(n + 1) * N]
                        tt(xv, xv, tmp, ALU.add).then_inc(s.up(name if i == 3 else None), 1)

                residual([(2 * n + c, c, n, ("out", n)) for n in range(2) for c in range(2)], 0, "b1_mixer_added")
                norm_dve(s, "b1_", 1)
                evac_hT(s, "b1_", 1, lambda k: acol[:, 8 + k:9 + k], lambda k: modc[:, 24 + k:25 + k])

                def conv(j):
                    dve.wait_ge(tile_done, b1_used(L, B1_AT[("up", j)]))
                    if j >= 2:
                        dve.wait_ge(*s.at("b1_silu_done", j - 1))
                    y = sm[:, j % 2, :].rearrange("p (f t) -> p f t", f=2)
                    gp = ps[2 * (j % 2) + 1][:, :].rearrange("p (f t) -> p f t", f=2)
                    dve.wait_ge(*s.own())
                    for f in range(2):
                        ts(y[:, f, :], gp[:, f, :], cc1("conv_w", 2 * FCH + 2 * j + f), cc1("conv_b", 2 * j + f),
                           ALU.mult, ALU.add).then_inc(s.up(), 1)
                    for tap_, sh in ((1, 1), (0, 2)):
                        dve.wait_ge(*s.own())
                        for f in range(2):
                            stt(y[:, f, sh:T], gp[:, f, 0:T - sh], cc1("conv_w", tap_ * FCH + 2 * j + f),
                                y[:, f, sh:T], ALU.mult, ALU.add)\
                                .then_inc(s.up("b1_conv_done" if (tap_, f) == (0, 1) else None), 1)

                def product(j):
                    dve.wait_ge(*s.at("b1_silu_done", j + 1))
                    tt(prod[:, 2 * j:2 * j + 2, :], pT[:, j % 2, :].rearrange("p (f t) -> p f t", f=2),
                       ps[2 * (j % 2)][:, :].rearrange("p (f t) -> p f t", f=2), ALU.mult)\
                        .then_inc(s.up("b1_product_ready"), 1)

                for j in range(UPT):
                    conv(j)
                    product(j)
                    if j in (2, 5):
                        accumulate(10 + j // 5)
                    if j in (4, 7):
                        mod_out(10 + j // 7)
                end = ("down", (FCH + 3) // 4 - 1)
                residual([(4 + 2 * c + n, c, n, end) for c in range(2) for n in range(2)], 1, "b1_layer_added")
                s.end()

            dve.wait_ge(sems["fin_rstd"], 1)
            dve.wait_ge(sems["qk_free"], 16 * (DEPTH + 1))
            for c in range(2):
                stt(x[:, c, :], x[:, c, :], rs[:, c:c + 1], gfin, ALU.mult, ALU.mult)\
                    .then_inc(sems["once_dve" if c == 0 else "b2_layer_added"], 1)

            with dve.Fori(0, DEPTH) as L:
                s = Count(sems, L, COUNTS, "b2_dve_step")
                cp(ccol[:, 0:NC2], cols[:, bass.ds(L * NC2 + (2 * NC1 + 8), NC2)]).then_inc(s.up(), 1)
                cp(crow[:, 0:NR2], rows[:, bass.ds(L * NR2 + 2 * NR1, NR2)]).then_inc(s.up(), 1)
                dve.wait_ge(*s.own())
                ts(kgain, tb("rows64"), cc2("kn"), None, ALU.mult).then_inc(s.up(), 1)
                norm_dve(s, "b2_", 0)
                evac_hT(s, "b2_", 0, lambda k: cc2("norm_mix", k), None)
                t768 = sm[:, 0:2, :].rearrange("p a n -> p (a n)")[:, 0:768]
                s12 = ssl.rearrange("p (t c h) -> p t c h", t=2, c=2)
                r12 = rsl.rearrange("p (t c h) -> p t c h", t=2, c=2)

                def k6(t, c):
                    return t[:, c, :].rearrange("p (h n) -> p h n", h=MLH)

                def latent_squares(q, t, scratch):
                    for c in range(2):
                        dve.wait_ge(*s.own())
                        tt(scratch, t[:, c, :], t[:, c, :], ALU.mult).then_inc(s.up(), 1)
                        dve.wait_ge(*s.own())
                        nc.vector.tensor_reduce(s12[:, q, c, :], scratch.rearrange("p (h d) -> p h d", h=MLH),
                                                AX.X, ALU.add)\
                            .then_inc(s.up("b2_latent_sumsq" if c else None), 1)

                def latent_norm(q, t, c, scratch):
                    dve.wait_ge(*s.at("b2_latent_rstd", q + 1))
                    gain = crow[:, 96 * q:96 * q + 96].unsqueeze(1).to_broadcast([P, MLH, MQK])
                    v = k6(t, c)
                    dve.wait_ge(*s.own())
                    tt(v, v, r12[:, q, c, :].unsqueeze(2).to_broadcast([P, MLH, MQK]), ALU.mult).then_inc(s.up(), 1)
                    dve.wait_ge(*s.own())
                    tt(v, v, gain, ALU.mult).then_inc(s.up(), 1)
                    dve.wait_ge(*s.own())
                    vr = v[:, :, 64:96].rearrange("p g (a d) -> p g a d", a=2)
                    t1 = scratch[:, 0:192].rearrange("p (g a d) -> p g a d", g=MLH, a=2)
                    t2 = scratch[:, 192:384].rearrange("p (g a d) -> p g a d", g=MLH, a=2)
                    ins = rope(s, vr, c, MLH, 16, tb("cosM")[:, c * 16:(c + 1) * 16],
                               tb("sinM")[:, c * 16:(c + 1) * 16], t1, t2)
                    ins.then_inc(s.up("b2_latent_ready" if (q, c) == (1, 1) else None), 1)

                for i, j in enumerate(IN2_ORDER):
                    dve.wait_ge(tile_done, b2_used(L, B2_AT[("in", j)]))
                    w = min(N, IN2 - j * N)
                    cp(proj2[:, 1, j * N:j * N + w], ps[2 * (i % 2) + 1][:, 0:w]).then_inc(s.up("b2_proj_by_dve"), 1)
                    if i == 0:
                        dve.wait_ge(*s.at("b2_compressed_rstd", 1))
                        for c in range(2):
                            for q, (o, n) in enumerate(((CQ2, 256), (CKV2, 128))):
                                v = proj2[:, c, o:o + n]
                                ts(v, v, rsc[:, 2 * c + q:2 * c + q + 1], None, ALU.mult)\
                                    .then_inc(s.up("b2_compressed_ready" if (c, q) == (1, 1) else None), 1)
                    if i == 2:
                        for hf in range(2):
                            dve.wait_ge(*s.at("b2_uq_done", hf + 3))
                            cp(qb[:, 1, hf * 288:(hf + 1) * 288], ps[5 + 2 * hf][:, 0:288])\
                                .then_inc(s.up("b2_uq_by_dve"), 1)
                        dve.wait_ge(*s.at("b2_uq_by_act", 2))
                        latent_squares(0, qb, t768[:, 0:576])
                        for c in range(2):
                            latent_norm(0, qb, c, t768[:, 0:576])
                    if i == 3:
                        dve.wait_ge(*s.at("b2_proj_by_act", 4))
                        for c in range(2):
                            dve.wait_ge(*s.own())
                            v = proj2[:, c, 0:768]
                            tt(t768, v, v, ALU.mult).then_inc(s.up(), 1)
                            dve.wait_ge(*s.own())
                            nc.vector.tensor_reduce(ss[:, 12 * c:12 * c + 12],
                                                    t768.rearrange("p (h d) -> p h d", h=12), AX.X, ALU.add)\
                                .then_inc(s.up("b2_head_sumsq" if c else None), 1)
                        for hf in range(2):
                            dve.wait_ge(*s.at("b2_kv_done", hf + 3))
                            v = ps[5 + 2 * hf][:, 0:384].rearrange("p (h n) -> p h n", h=3)
                            cp(kb[:, 1, hf * 288:(hf + 1) * 288].rearrange("p (h n) -> p h n", h=3)[:, :, 0:64],
                               v[:, :, 0:64]).then_inc(s.up(), 1)
                            cp(vb[:, 1, 3 * hf:3 * hf + 3, :], v[:, :, 64:128]).then_inc(s.up("b2_kv_by_dve"), 1)
                        dve.wait_ge(*s.at("b2_head_rstd", 1))
                        for c in range(2):
                            v = proj2[:, c, 0:768].rearrange("p (h d) -> p h d", h=12)
                            tt(v, v, rs[:, 12 * c:12 * c + 12].unsqueeze(2).to_broadcast([P, 12, HD]), ALU.mult)\
                                .then_inc(s.up("b2_heads_normed" if c else None), 1)
                dve.wait_ge(*s.at("b2_kv_by_act", 2))
                for c in range(2):
                    cp(k6(kb, c)[:, :, 64:96],
                       proj2[:, c, KR2:KR2 + 32].unsqueeze(1).to_broadcast([P, MLH, 32]))\
                        .then_inc(s.up(), 1)
                latent_squares(1, kb, hT[:, 0:576])
                dve.wait_ge(*s.at("b2_bias_ready", 1))

                def mask2(m):
                    mp = map2(m)
                    dve.wait_ge(*s.at("b2_scores_done", m + 1))
                    if m >= 3:
                        dve.wait_ge(*s.at("b2_probs_flipped", m - 2))
                    src, dst = ps[4 + m % 2][:, :], sm[:, m % 3, :]
                    if m < NAH:
                        stt(dst.rearrange("p (c k) -> p c k", c=2), src.rearrange("p (c k) -> p c k", c=2),
                            mp["scale"], nbias[:, m, :, :], ALU.mult, ALU.add)\
                            .then_inc(s.up("b2_scores_read"), 1)
                    else:
                        ts(dst, src, mp["scale"], None, ALU.mult).then_inc(s.up("b2_scores_read"), 1)
                    row_max(s, "b2_", m)

                def out2(m):
                    o = HD * m if m < NAH else 1152 + HD * (m - NAH)
                    out_norm(s, "b2_", m, proj2[:, :, o:o + HD])

                mask2(0)
                for m in range(MAPS2 + 2):
                    if m + 1 < MAPS2:
                        mask2(m + 1)
                    if m < 2:
                        latent_norm(1, kb, m, hT[:, 0:576])
                    if m == 2:
                        dve.wait_ge(*s.at("b2_shifts_done", 1))
                        u = proj2[:, :, HC2:HC2 + 256]
                        tt(u, ps[0][:, :].rearrange("p (c n) -> p c n", c=2), u, ALU.add)\
                            .then_inc(s.up("b2_shifts_read"), 1)
                        dve.wait_ge(*s.own())
                        tt(u, u, proj2[:, :, BC2:BC2 + 256], ALU.mult).then_inc(s.up("b2_conv_ready"), 1)
                    if m >= 2:
                        out2(m - 2)
                dve.wait_ge(*s.at("b2_mixed_rstd", 1))
                for c in range(2):
                    for q, (o, n) in enumerate(((0, 384), (1152, 384), (HC2, 256))):
                        v = proj2[:, c, o:o + n]
                        ts(v, v, rs[:, 3 * c + q:3 * c + q + 1], None, ALU.mult)\
                            .then_inc(s.up("b2_mixed_ready" if (c, q) == (1, 2) else None), 1)
                for j in (0, 2):
                    dve.wait_ge(*s.at("b2_heads_flipped", j + 1))
                    for i in range(2):
                        k = 2 * j + i
                        ts(h8[:, k, :], ps[4 + j][:, i * T:(i + 1) * T], cc2("out_norm", k), None, ALU.mult)\
                            .then_inc(s.up("b2_heads_by_dve" if i else None), 1)
                for i in range(4):
                    dve.wait_ge(tile_done, b2_used(L, B2_AT[("out", i // 2)]))
                    c, n = i % 2, i // 2
                    xv = x[:, c, n * N:(n + 1) * N]
                    tt(xv, ps[i][:, :], xv, ALU.add).then_inc(s.up("b2_mixer_added" if i == 3 else None), 1)
                norm_dve(s, "b2_", 1)
                evac_hT(s, "b2_", 1, lambda k: cc2("norm_ffn", k), None)
                dve.wait_ge(*s.at("b2_logits_done", 1))
                a3 = aff.rearrange("p (c e) -> p c e", c=2)
                e3 = affe.rearrange("p (c e) -> p c e", c=2)
                tt(a3, ps[0][:, 0:32].rearrange("p (c e) -> p c e", c=2),
                   crow[:, 192:208].unsqueeze(1).to_broadcast([P, 2, EXP]), ALU.add)\
                    .then_inc(s.up(), 1)
                dve.wait_ge(*s.own())
                nc.vector.tensor_reduce(mx2, a3, AX.X, ALU.max, negate=True).then_inc(s.up("b2_logits_ready"), 1)
                dve.wait_ge(*s.at("b2_affinity_exps", 1))
                nc.vector.reciprocal(rd2, dn2).then_inc(s.up(), 1)
                dve.wait_ge(*s.own())
                tt(a3, e3, rd2.unsqueeze(2).to_broadcast([P, 2, EXP]), ALU.mult).then_inc(s.up("b2_affinity_ready"), 1)
                dve.wait_ge(*s.at("b2_affinity_flipped", 1))
                work, sel, cum = rscratch[0:EXP, :], rsel[0:EXP, :], rcum[0:EXP, :]
                cp(work, ps[1][0:EXP, 0:T]).then_inc(s.up(), 1)
                for r in range(CAP // 8):
                    settle(s)
                    nc.vector.max(m8[0:EXP, :], work).then_inc(s.up(), 1)
                    settle(s)
                    nc.vector.match_replace(work, m8[0:EXP, :], work, -1.0).then_inc(s.up(), 1)
                dve.wait_ge(*s.own())
                ts(sel, work, 0.0, None, ALU.is_lt).then_inc(s.up(), 1)
                dve.wait_ge(*s.own())
                nc.vector.tensor_tensor_scan(cum, ones[0:EXP, 0:1].to_broadcast([EXP, T]), sel, 0.0,
                                             ALU.mult, ALU.add).then_inc(s.up(), 1)
                dve.wait_ge(*s.own())
                tt(cum, cum, sel, ALU.mult).then_inc(s.up("b2_slots_ready"), 1)
                dve.wait_ge(*s.at("b2_slots_flipped", 1))
                cp(slot, ps[0][:, 0:32]).then_inc(s.up(), 1)
                settle(s)
                s.end()

                with dve.Fori(0, GROUPS) as g:
                    s = Count(sems, L * GROUPS + g, COUNTS, "g_dve_step")
                    s3 = slot.rearrange("p (c e) -> p c e", c=2)
                    io = tb("iota").unsqueeze(1).to_broadcast([P, EG, CAP])
                    for c in range(2):
                        tt(selP[:, c, :, :], s3[:, c, bass.ds(g * EG, EG)].unsqueeze(2).to_broadcast([P, EG, CAP]),
                           io, ALU.is_equal).then_inc(s.up("g_chosen" if c else None), 1)
                    dve.wait_ge(*s.own())
                    for c in range(2):
                        tt(selG[:, c, :, :], selP[:, c, :, :],
                           a3[:, c, bass.ds(g * EG, EG)].unsqueeze(2).to_broadcast([P, EG, CAP]),
                           ALU.mult).then_inc(s.up("g_weighted" if c else None), 1)
                    dve.wait_ge(*s.at("g_rows_done", 1))
                    for q in range(4):
                        ts(xsT[:, q, :], ps[4][:, q * P:(q + 1) * P], cc2("norm_ffn", q), None, ALU.mult)\
                            .then_inc(s.up("g_rows_by_dve" if q == 3 else None), 1)
                    dve.wait_ge(*s.at("g_gate_silu", 2))
                    dve.wait_ge(tile_done, g_used(L, g, 2 * KD - 1))
                    for n in range(2):
                        hv = hid[:, n * N:(n + 1) * N]
                        tt(hv, ps[2 + n][:, :], hv, ALU.mult).then_inc(s.up("g_hidden_ready"), 1)
                    dve.wait_ge(*s.at("g_hidden_flipped", 1))
                    cp(hidT[:, 0:4, :], ps[4][:, :].rearrange("p (k s) -> p k s", k=4)).then_inc(s.up("g_hidden_by_dve"), 1)
                    dve.wait_ge(tile_done, g_used(L, g, G_TILES - 1))
                    cp(ysb[:, N:2 * N], ps[7][:, :]).then_inc(s.up("g_result_by_dve"), 1)
                    for i in range(4):
                        dve.wait_ge(*s.at("g_scatter_done", i + 1))
                        c, n = i // 2, i % 2
                        xv = x[:, c, n * N:(n + 1) * N]
                        tt(xv, ps[4 + i % 2][:, :], xv, ALU.add).then_inc(s.up("g_scatter_added"), 1)
                    s.end()
                cp(pad[:, 0:1], tb("half")[:, 0:1]).then_inc(sems["b2_layer_added"], 1)
        if MISCOUNT:
            raise AssertionError(f"counts: {sorted(set(MISCOUNT))}")


def table():
    t = np.zeros((P, NTAB), np.float32)

    def put(name, v):
        o, n = TAB[name]
        t[:, o:o + n] = v.reshape(v.shape[0], n)

    p = np.arange(P)
    put("E", (np.arange(384)[None, :] == p[:, None] + P).astype(np.float32))
    put("ones", np.ones((P, P), np.float32))
    q = (np.arange(2)[None, :, None] * P + p[:, None, None])
    k = np.arange(T)[None, None, :]
    put("causal", np.where(k <= q, 0.0, NEG))
    n = np.zeros((P, 2, T))
    for window, d in ((128, 1), (512, 4), (2048, 16)):
        n += (k <= q) & ((q - k) % d == 0) & ((q - k) // d <= window // d)
    put("mult", np.where(n > 0, np.log(np.maximum(n, 1)), NEG))
    put("tri", (p[:, None] <= np.arange(T)[None, :]).astype(np.float32))
    c = (p % GRID)[:, None]
    start = np.clip(c - 8, 0, GRID - 16)
    j = np.arange(GRID)[None, :]
    put("colmask", np.where((j >= start) & (j < start + 16), 0.0, NEG))
    pos = (np.arange(2)[None, :] * P + p[:, None]).astype(np.float32)[:, :, None]

    def angles(dim, kind):
        if kind == "M":
            inv = np.float32(10000.0) ** (-np.arange(dim // 2, dtype=np.float32) / np.float32(dim // 2))
        else:
            inv = np.float32(1.0) / (np.float32(10000.0) ** (np.arange(0, dim, 2, dtype=np.float32) / np.float32(dim)))
        ang = (pos * inv.astype(np.float32)[None, None, :]).astype(np.float32)
        for fn, name in ((np.cos, "cos"), (np.sin, "sin")):
            v = np.zeros((P, TAB[name + kind][1]), np.float32)
            v[:, 0:dim] = fn(ang).astype(np.float32).reshape(P, dim)
            put(name + kind, v)

    angles(32, "A")
    angles(64, "B")
    angles(32, "M")
    put("iota", np.tile(np.arange(1, CAP + 1, dtype=np.float32)[None, :], (P, 1)))
    for name, v in (("invC", [1 / 256, 1 / 128] * 2), ("inv3", [1 / 384, 1 / 384, 1 / 256] * 2),
                    ("inv64", [1 / HD] * 24), ("inv96", [1 / MQK] * 24), ("invD", [1 / D] * 2), ("eps5", [1e-5] * 8),
                    ("eps6", [1e-6] * 28), ("half", [-0.5] * 28)):
        put(name, np.tile(np.array(v, np.float32)[None, :], (P, 1)))
    put("rows32", (p[:, None] // 32 == np.arange(4)[None, :]).astype(np.float32))
    put("rows64", (p[:, None] // 64 == np.arange(2)[None, :]).astype(np.float32))
    li = [0.8 - 0.6 * math.exp(-0.3 * layer) for layer in range(DEPTH)]
    put("lam", np.tile(np.array([v for x in li for v in (-x, 1.0 - x)], np.float32)[None, :], (P, 1)))
    return t


def kernel(**inputs):
    import numpy as _np
    import concourse.bacc as _bacc
    from concourse.bass_utils import run_bass_kernel_spmd as _run

    i = {k: _np.asarray(v) for k, v in inputs.items()}

    def col(v):
        return v.reshape(-1, P).T

    cols, rows = [], []
    for l in range(DEPTH):
        cols += [col(i[n][l]) for n in ("g_attn", "g_mlp", "b_mod", "conv_w", "conv_b")]
        rows += [i["subln_g"][l], i["forget_bias"][l], i["diff_lambda"][l].reshape(-1)]
    cols.append(col(i["c"]))
    for l in range(DEPTH):
        cols += [col(i[n][l]) for n in ("norm_mix_2", "norm_ffn_2", "out_norm_2", "cq_norm_2", "ckv_norm_2")]
        cols += [_np.concatenate([i[n][l], i[n][l]]).reshape(P, 1) for n in ("q_norm_a_2", "k_norm_a_2")]
        rows += [i["q_norm_b_2"][l], i["k_norm_b_2"][l], i["b_router_2"][l]]
    arrays = {
        "x": i["x"], "tab": table(),
        "cols": _np.ascontiguousarray(_np.concatenate(cols, axis=1)),
        "rows": _np.ascontiguousarray(_np.concatenate(rows).reshape(1, NROWS)),
        "rpb": _np.ascontiguousarray(i["rpb_2"][:, :, 4:11, :].reshape(DEPTH * NAH * 7, 31)),
        "g_final": i["g_final"].reshape(1, D),
    }
    for n in ("w_mod", "b_mod", "w_in", "w_out", "w_up", "w_down", "w_in_2", "w_out_2", "w_uq_2", "w_ukv_2",
              "w_router_2", "conv_w_2"):
        arrays[n] = i[n]
    for n in ("w_gate_2", "w_up_2", "w_down_2"):
        arrays[n] = i[n].reshape(DEPTH * EXP, D, EFF)
    nc = _bacc.Bacc("TRN2", target_bir_lowering=False, num_devices=1)
    aps = {n: nc.dram_tensor("in_" + n, v.shape, F32, kind="ExternalInput").ap() for n, v in arrays.items()}
    out = nc.dram_tensor("out", (1, T, D), F32, kind="ExternalOutput").ap()
    two_blocks(nc, aps, out)
    r = _run(nc, [{"in_" + n: v for n, v in arrays.items()}], core_ids=[0])
    return r.results[0]["out"]
```

```python
import math
import numpy as np
import concourse.bass as bass
from concourse import mybir
from contextlib import ExitStack

F32 = mybir.dt.float32
ALU = mybir.AluOpType
ACT = mybir.ActivationFunctionType
AX = mybir.AxisListType

P = 128
T = 256
NC_ = T // P
D = 1024
KD = D // P
DEPTH = 2
N = 512
HD = 64
AH, BH, CH = 4, 6, 6
IN1 = 3078
DFF = 2816
FCH = DFF // P
UPT = FCH // 2
IN2 = 2336
NAH = 6
MLH, MQK = 6, 96
EXP, CAP, EFF = 16, 32, 1024
EG = 4
GRID = 64
NEG = -1.0e30

B1_Q = {"A": 0, "B": 768, "C": 1920}
B1_K = {"A": 256, "B": 1152, "C": 2304}
B1_V = {"A": 512, "B": 1536, "C": 2688}
B1_F = 3072
QA2, KA2, VA2, CQ2, CKV2, KR2, HC2, BC2, CC2 = 0, 384, 768, 1152, 1408, 1536, 1568, 1824, 2080

CAUSAL_KEYS = ((0, P), (P, T))
ALL_KEYS = ((0, T), (T, T))

SLOTS = 6
TILE = 4096
IN1_ORDER = (0, 1, 6, 2, 3, 4, 5)
MOD_AT = {0: 4, 1: 5, 3: 6, 4: 7, 5: 8, 6: 9}
FLIPS_AT = {3: (0, 1), 4: (2, 3), 5: (4,), 6: (5, 6)}
B1_TILES = (
    [("mod", i) for i in range(4)]
    + [t for i, j in enumerate(IN1_ORDER) for t in [("in", j)] + ([("mod", MOD_AT[i])] if i in MOD_AT else [])]
    + [("out", i) for i in range(2)]
    + [t for i in range(UPT) for t in ([("up", i)] + ([("mod", 10 + i // 6)] if i in (3, 6) else []))]
    + [("down", i) for i in range((FCH + 3) // 4)]
)
B1_AT = {t: i for i, t in enumerate(B1_TILES)}
B1_N = -(-len(B1_TILES) // SLOTS) * SLOTS
IN2_ORDER = (2, 3, 0, 1, 4)
B2_TILES = [("in", i) for i in IN2_ORDER[0:4]] + [("small", 0), ("in", IN2_ORDER[4]), ("out", 0), ("out", 1)]
B2_AT = {t: i for i, t in enumerate(B2_TILES)}
B2_HEAD = -(-len(B2_TILES) // SLOTS) * SLOTS
G_TILES = 3 * KD
GROUPS = EXP // EG
B2_N = B2_HEAD + GROUPS * G_TILES
assert G_TILES % SLOTS == 0

TAB = {}


def _tab():
    at = 0
    for name, n in (("E", 384), ("ones", P), ("causal", 384), ("mult", 384), ("tri", T), ("colmask", GRID),
                    ("cosA", 64), ("sinA", 64), ("cosB", 128), ("sinB", 128), ("cosM", 64), ("sinM", 64),
                    ("iota", CAP), ("invN", 6), ("inv64", 24), ("invC", 4), ("inv96", 24), ("invD", 2), ("eps5", 8),
                    ("eps6", 28),
                    ("half", 28), ("lam", 4), ("rows32", 4), ("rows64", 2)):
        TAB[name] = (at, n)
        at += n
    return at


NTAB = _tab()

C1 = {"g_attn": (0, 8), "g_mlp": (8, 8), "b_mod": (16, 48), "conv_w": (64, 66), "conv_b": (130, 22)}
NC1 = 152
C2 = {"norm_mix": (0, 8), "norm_ffn": (8, 8), "out_norm": (16, 8), "cq": (24, 2), "ckv": (26, 1), "qn": (27, 1),
      "kn": (28, 1)}
NC2 = 29
NCOLS = 2 * NC1 + 8 + 2 * NC2
R1 = {"subln": (0, 64), "fb": (64, 6), "lam": (70, 128)}
NR1 = 198
R2 = {"qnb": (0, 96), "knb": (96, 96), "router": (192, 16)}
NR2 = 208
NROWS = 2 * NR1 + 2 * NR2

MAPS1 = 2 * AH + BH + CH
MAPS2 = NAH + MLH
MIXED = ((0, 384), (HC2, 256), (1152, 384))
A0 = BH
B1_COUNT = {
    "b1_gate_bias": 16, "b1_forget_bias": CH, "b1_dve_step": 222, "b1_act_step": 41, "b1_pool_step": 28, "b1_sumsq": 4, "b1_rstd": 4,
    "b1_normed": 4, "b1_half_out_done": 2, "b1_half_mixer_added": 1, "b1_half_layer_added": 1, "b1_down_done": 3,
    "b1_stream_flipped": 8, "b1_stream_by_dve": 8, "b1_stream_by_act": 8, "b1_mod_summed": 12, "b1_mod_ready": 12,
    "b1_gain_ready": 2, "b1_proj_by_act": 7, "b1_proj_by_dve": 7, "b1_rotated": 2, "b1_qk_flipped": 8,
    "b1_qk_ready": 8, "b1_forget_abs": 1, "b1_forget_log": 1, "b1_forget_ready": 1, "b1_cumsum_done": 4,
    "b1_cumsum_read": 4, "b1_lambda_dots": 1, "b1_lambda_exps": 1, "b1_scores_done": MAPS1, "b1_scores_read": MAPS1,
    "b1_max_ready": MAPS1, "b1_probs_ready": MAPS1, "b1_probs_flipped": MAPS1, "b1_probsT_ready": MAPS1,
    "b1_out_done": MAPS1, "b1_out_read": MAPS1, "b1_diff_sumsq": 1, "b1_diff_rstd": 1, "b1_diff_ready": 1,
    "b1_heads_flipped": 4, "b1_heads_by_dve": 2, "b1_heads_by_act": 2, "b1_mixer_added": 1, "b1_layer_added": 1,
    "b1_conv_done": UPT, "b1_silu_done": UPT, "b1_product_ready": UPT,
}
B2_COUNT = {
    "b2_bias_loaded": 16 * 16, "b2_dve_step": 91, "b2_act_step": 31, "b2_pool_step": 23, "b2_sumsq": 4,
    "b2_rstd": 4, "b2_normed": 4, "b2_half_out_done": 2, "b2_half_mixer_added": 1, "b2_half_layer_added": 1,
    "b2_stream_flipped": 8, "b2_stream_by_dve": 8, "b2_stream_by_act": 8, "b2_proj_by_act": 5, "b2_proj_by_dve": 5,
    "b2_head_sumsq": 1, "b2_compressed_sumsq": 1, "b2_head_rstd": 1, "b2_heads_normed": 1, "b2_compressed_ready": 1,
    "b2_compressed_rstd": 1, "b2_logits_done": 1, "b2_qk_flipped": 5, "b2_qk_ready": 5, "b2_uq_done": 4,
    "b2_uq_by_act": 2, "b2_uq_by_dve": 2, "b2_kv_done": 4, "b2_kv_by_act": 2, "b2_kv_by_dve": 2, "b2_taps_ready": 1,
    "b2_shifts_done": 1, "b2_shifts_read": 1, "b2_conv_ready": 1, "b2_latent_sumsq": 2, "b2_latent_rstd": 2,
    "b2_latent_ready": 1, "b2_head_flipped": MLH, "b2_head_ready": MLH, "b2_scores_done": MAPS2,
    "b2_scores_read": MAPS2, "b2_max_ready": MAPS2, "b2_probs_ready": MAPS2, "b2_probs_flipped": MAPS2,
    "b2_probsT_ready": MAPS2, "b2_out_done": MAPS2, "b2_out_read": MAPS2, "b2_mixed_sumsq": 2, "b2_mixed_rstd": 2,
    "b2_mixed_ready": 1, "b2_heads_flipped": 4, "b2_heads_by_dve": 2, "b2_heads_by_act": 2, "b2_mixer_added": 1,
    "b2_layer_added": 1, "b2_logits_ready": 1, "b2_affinity_exps": 1, "b2_affinity_ready": 1,
    "b2_affinity_flipped": 1, "b2_slots_ready": 1, "b2_slots_flipped": 1, "b2_bias_ready": 1,
}
G_COUNT = {
    "g_dve_step": 5, "g_act_step": 3, "g_chosen": 1, "g_weighted": 1, "g_rows_done": 2, "g_rows_by_dve": 1,
    "g_rows_by_act": 1, "g_weights_flipped": 1, "g_weights_ready": 1, "g_gate_silu": 2, "g_hidden_ready": 2,
    "g_hidden_flipped": 2, "g_hidden_by_dve": 1, "g_hidden_by_act": 1, "g_result_by_act": 1, "g_result_by_dve": 1,
    "g_scatter_done": 4, "g_scatter_added": 4,
}
COUNTS = {**B1_COUNT, **B2_COUNT, **G_COUNT}
ONCE = ("const_loaded", "csil", "rpb_clear", "rpb_loaded", "qk_free",
        "router_loaded", "fin_sumsq", "fin_rstd", "out_stored", "once_pool")
MISCOUNT = []


class Count:

    def __init__(self, sems, turn, counts, step):
        self.sems, self.turn, self.counts, self.step = sems, turn, counts, step
        self.sent, self.last = {}, None

    def at(self, name, k):
        return self.sems[name], k if self.turn is None else self.turn * self.counts[name] + k

    def up(self, name=None):
        name = name or self.step
        self.sent[name] = self.sent.get(name, 0) + 1
        self.last = (name, self.sent[name])
        return self.sems[name]

    def own(self):
        return self.at(*self.last)

    def end(self):
        for name, n in self.sent.items():
            if n != self.counts[name]:
                MISCOUNT.append((name, n, self.counts[name]))


def two_blocks(nc, a, out):
    ctx = ExitStack()
    with ctx:
        def sb(name, shape):
            return ctx.enter_context(nc.sbuf_tensor(name, shape, F32))

        ring = sb("ring", [P, SLOTS, TILE])
        router = sb("router", [P, DEPTH * KD * EXP])
        x = sb("x", [P, NC_, D])
        hT = sb("hT", [P, 2048])
        tab = sb("tab", [P, NTAB])
        cols = sb("cols", [P, NCOLS])
        rows = sb("rows", [P, NROWS])
        ccol = sb("ccol", [P, NC1])
        crow = sb("crow", [P, NR2])
        wide = sb("wide", [P, 6160])
        qk = sb("qk", [P, 7168])
        sm = sb("sm", [P, 3, N])
        pT = sb("pT", [P, 2, N])
        gbuf = sb("gbuf", [P, 3072])
        sc = sb("sc", [P, 768])
        ps = [ctx.enter_context(nc.psum_tensor(f"ps{i}", [P, N], F32)) for i in range(8)]

        small = {}
        at = [0]

        def sm_(name, n):
            small[name] = sc[:, at[0]:at[0] + n]
            at[0] += n
            return small[name]

        csil = sm_("csil", 8)
        ss = sm_("ss", 28)
        rs = sm_("rs", 28)
        tmp28 = sm_("tmp28", 28)
        ssc = sm_("ssc", 4)
        rsc = sm_("rsc", 4)
        ssm = sm_("ssm", 6)
        rsm = [sm_("rsm0", 6), sm_("rsm1", 6)]
        tmpm = [sm_("tmpm0", 6), sm_("tmpm1", 6)]
        ssl = sm_("ssl", 24)
        rsl = sm_("rsl", 24)
        modc = sm_("modc", 48)
        acol = sm_("acol", 16)
        lamv = sm_("lamv", 4)
        lamt = sm_("lamt", 64)
        fz = sm_("fz", 12)
        fa = sm_("fa", 12)
        fe = sm_("fe", 12)
        nlf = sm_("nlf", 12)
        nfq = sm_("nfq", 12)
        den = sm_("den", 40)
        rden = sm_("rden", 40)
        nmx = sm_("nmx", 40)
        lcur = sm_("lcur", 2)
        aff = sm_("aff", 32)
        affe = sm_("affe", 32)
        slot = sm_("slot", 32)
        mx2 = sm_("mx2", 2)
        dn2 = sm_("dn2", 2)
        rd2 = sm_("rd2", 2)
        m8 = sm_("m8", 8)
        pad = sm_("pad", 1)
        kgain = sm_("kgain", 2)
        assert at[0] <= 768

        def tb(name):
            o, n = TAB[name]
            return tab[:, o:o + n]

        E = tb("E")
        ident = E[:, P:2 * P]
        ones = tb("ones")
        tri = tb("tri")
        causal, mult = tb("causal"), tb("mult")
        h8 = hT[:, :].rearrange("p (k t) -> p k t", k=KD)
        xn = wide[:, 0:2048].rearrange("p (c d) -> p c d", c=2)
        proj1 = wide[:, 0:2 * IN1].rearrange("p (c n) -> p c n", c=2)
        proj2 = wide[:, 0:2 * IN2].rearrange("p (c n) -> p c n", c=2)
        prod = wide[:, 0:FCH * T].rearrange("p (f t) -> p f t", f=FCH)
        qT = qk[:, 0:2048].rearrange("p (b t) -> p b t", b=8)
        kT = qk[:, 2048:7168].rearrange("p (b t) -> p b t", b=20)
        kN = qk[:, 4096:5632].rearrange("p (b t) -> p b t", b=NAH)
        gates = gbuf[:, 0:2048].rearrange("p (i n) -> p i n", i=4)
        acc = gbuf[:, 2048:3072].rearrange("p (i n) -> p i n", i=2)
        oA = gbuf[:, 2048:3072].rearrange("p (h m c d) -> p h m c d", h=AH, m=2, c=2)
        nbias = gbuf[:, :].rearrange("p (h c k) -> p h c k", h=NAH, c=2)
        fbias = [qk[:, o + (P + T) * i:o + (P + T) * (i + 1)] for o, k in ((4096, 4), (512, 2)) for i in range(k)]
        nfrow = hT[:, 0:1536].rearrange("p (h k) -> p h k", h=CH)
        cT = qk[:, 1536:2304].rearrange("p (b t) -> p b t", b=3)
        qb = qk[:, 2304:3456].rearrange("p (c n) -> p c n", c=2)
        kb = qk[:, 5632:6784].rearrange("p (c n) -> p c n", c=2)
        xqk = [qk[:, 3456:3968], hT[:, 1152:1664]]
        vb = wide[:, 4672:5440].rearrange("p (c h d) -> p c h d", c=2, h=MLH)
        cv2 = wide[:, 5440:5952].rearrange("p (c n) -> p c n", c=2)
        xsT = wide[:, 2048:3072].rearrange("p (k s) -> p k s", k=KD)
        hid = wide[:, 3072:4096]
        hidT = wide[:, 4096:5120].rearrange("p (k s) -> p k s", k=KD)
        ysb = wide[:, 5120:6144]
        selP = sm[:, 0, 0:256].rearrange("p (c e s) -> p c e s", c=2, e=EG)
        selG = sm[:, 0, 256:512].rearrange("p (c e s) -> p c e s", c=2, e=EG)
        pgT = sm[:, 1, 0:256].rearrange("p (c t) -> p c t", c=2)
        rscratch = sm[:, 2, 0:256]
        rsel = pT[:, 0, 0:256]
        rcum = pT[:, 0, 256:512]
        gfin = qk[:, 0:D]
        rpad = qk[:, 0:128]

        copies = nc.dram_tensor("bias_copies", [DEPTH, NAH * 7, GRID, P], F32, kind="Internal").ap()

        sems = {}
        for name in (*COUNTS, *ONCE, "tile_done"):
            sems[name] = ctx.enter_context(nc.semaphore(name))
        tile_done = sems.pop("tile_done")
        arrived = [ctx.enter_context(nc.semaphore(f"slot_loaded{i}")) for i in range(SLOTS)]

        def arrivals(tiles):
            seen, at_ = [0] * SLOTS, []
            for t, kind in enumerate(tiles):
                two = kind[0] == "up" or (tiles is B2_TILES and kind == ("in", 0))
                n = 32 if two else 48 if kind[0] == "small" else 16
                seen[t % SLOTS] += n
                at_.append(seen[t % SLOTS])
            return at_, seen

        B1_ARR, B1_SEEN = arrivals(B1_TILES)
        B2_ARR, B2_HSEEN = arrivals(B2_TILES)
        B2_SEEN = [h + 16 * GROUPS * G_TILES // SLOTS for h in B2_HSEEN]

        def b1_loaded(L, t):
            i = t % SLOTS
            return arrived[i], L * B1_SEEN[i] + B1_ARR[t]

        def b2_loaded(L, t):
            i = t % SLOTS
            return arrived[i], L * B2_SEEN[i] + (DEPTH * B1_SEEN[i] + B2_ARR[t])

        def g_loaded(L, g, j):
            i = j % SLOTS
            first = DEPTH * B1_SEEN[i] + B2_HSEEN[i] + 16 * (j // SLOTS + 1)
            return arrived[i], L * B2_SEEN[i] + g * (16 * G_TILES // SLOTS) + first

        def b1_used(L, t):
            return L * B1_N + (SLOTS + t + 1)

        def b2_used(L, t):
            return L * B2_N + (DEPTH * B1_N + SLOTS + t + 1)

        def g_used(L, g, j):
            return L * B2_N + g * G_TILES + (DEPTH * B1_N + B2_HEAD + SLOTS + j + 1)

        def slot_at(t):
            return ring[:, t % SLOTS, :]

        def cc1(name, i=0, n=1):
            o, _ = C1[name]
            return ccol[:, o + i:o + i + n]

        def cc2(name, i=0, n=1):
            o, _ = C2[name]
            return ccol[:, o + i:o + i + n]

        def map1(m):
            kind, h = ("B", m) if m < A0 else ("A", m - A0) if m < A0 + 2 * AH else ("C", m - A0 - 2 * AH)
            if kind == "A":
                return dict(kind=kind, q=qT[:, h // 4, :], k=kT[:, h, :], v=B1_V["A"] + HD * (h // 2),
                            scale=32 ** -0.5, h=h // 2, part=h % 2)
            o = 0 if kind == "B" else 3
            return dict(kind=kind, q=qT[:, 2 + o + h // 2, :], k=kT[:, 8 + 2 * o + h, :],
                        v=B1_V[kind] + HD * h, scale=HD ** -0.5, h=h)

        def map2(m):
            if m < NAH:
                return dict(kind="N", q=qT[:, m // 2, :], k=kN[:, m, :], scale=HD ** -0.5, h=m)
            t = xqk[m % 2]
            return dict(kind="M", q=t[0:MQK, 0:T], k=t[0:MQK, T:2 * T], scale=MQK ** -0.5, h=m - NAH)

        block = ctx.enter_context(nc.Block())

        @block.sync
        def _(sp):
            sp.dma_start(cols[:, :], a["cols"]).then_inc(sems["const_loaded"], 16)
            sp.dma_start(x[:, :, :], a["x"][0].rearrange("(c p) d -> p c d", p=P)).then_inc(sems["const_loaded"], 16)
            sp.dma_start(rows[:, :], a["rows"].to_broadcast([P, NROWS])).then_inc(sems["const_loaded"], 16)
            sp.dma_start(tab[:, :], a["tab"]).then_inc(sems["const_loaded"], 16)
            sp.dma_start(router[:, :].rearrange("p (k n) -> p k n", n=EXP),
                         a["w_router_2"].rearrange("l (k p) n -> p (l k) n", p=P)).then_inc(sems["router_loaded"], 16)
            with sp.Fori(0, DEPTH) as L:
                for t, (kind, j) in enumerate(B1_TILES):
                    sp.wait_ge(tile_done, L * B1_N + (t + 1))
                    dst = slot_at(t)
                    sem = arrived[t % SLOTS]
                    d8 = dst.rearrange("p (k n) -> p k n", k=KD)
                    if kind == "mod":
                        src = a["w_mod"][bass.ds(L, 1), :, j * N:(j + 1) * N].rearrange("l (k p) n -> p (l k) n", p=P)
                        sp.dma_start(d8, src).then_inc(sem, 16)
                    elif kind == "in":
                        w = min(N, IN1 - j * N)
                        src = a["w_in"][bass.ds(L, 1), :, j * N:j * N + w].rearrange("l (k p) n -> p (l k) n", p=P)
                        sp.dma_start(d8[:, :, 0:w], src).then_inc(sem, 16)
                    elif kind == "out":
                        src = a["w_out"][bass.ds(L, 1), :, j * N:(j + 1) * N].rearrange("l (k p) n -> p (l k) n", p=P)
                        sp.dma_start(d8, src).then_inc(sem, 16)
                    elif kind == "up":
                        for half in range(2):
                            o = half * DFF + j * 256
                            src = a["w_up"][bass.ds(L, 1), :, o:o + 256].rearrange("l (k p) n -> p (l k) n", p=P)
                            sp.dma_start(d8[:, :, half * 256:half * 256 + 256], src).then_inc(sem, 16)
                    else:
                        nf = min(4, FCH - 4 * j)
                        src = a["w_down"][bass.ds(L, 1), 4 * j * P:(4 * j + nf) * P, :]
                        sp.dma_start(dst.rearrange("p (f n) -> p f n", f=4)[:, 0:nf, :],
                                     src.rearrange("l (f p) n -> p (l f) n", p=P)).then_inc(sem, 16)
            sp.wait_ge(sems["qk_free"], 16)
            with sp.Fori(0, DEPTH) as L:
                for t, (kind, j) in enumerate(B2_TILES):
                    sp.wait_ge(tile_done, L * B2_N + (DEPTH * B1_N + t + 1))
                    dst = slot_at(t)
                    sem = arrived[t % SLOTS]
                    d8 = dst.rearrange("p (k n) -> p k n", k=KD)
                    if kind == "in":
                        w = min(N, IN2 - j * N)
                        src = a["w_in_2"][bass.ds(L, 1), :, j * N:j * N + w].rearrange("l (k p) n -> p (l k) n", p=P)
                        if j == 0:
                            sp.dma_start(d8[:, 4:8, 0:w], src[:, 4:8, :]).then_inc(sem, 16)
                            sp.dma_start(d8[:, 0:4, 0:w], src[:, 0:4, :]).then_inc(sem, 16)
                        else:
                            sp.dma_start(d8[:, :, 0:w], src).then_inc(sem, 16)
                    elif kind == "out":
                        src = a["w_out_2"][bass.ds(L, 1), :, j * N:(j + 1) * N].rearrange("l (k p) n -> p (l k) n", p=P)
                        sp.dma_start(d8, src).then_inc(sem, 16)
                    else:
                        sp.dma_start(dst[:, 0:1152].rearrange("p (k n) -> p k n", k=2),
                                     a["w_uq_2"][bass.ds(L, 1)].rearrange("l (k p) n -> p (l k) n", p=P))\
                            .then_inc(sem, 16)
                        sp.dma_start(dst[:, 1152:1920].rearrange("p (k n) -> p k n", k=1),
                                     a["w_ukv_2"][bass.ds(L, 1)].rearrange("l p n -> p l n")).then_inc(sem, 16)
                        sp.dma_start(dst[:, 2048:2816],
                                     a["conv_w_2"][bass.ds(L, 1)].rearrange("l i n -> l (i n)").to_broadcast([P, 768])
                                     ).then_inc(sem, 16)
                rel = copies[bass.ds(L, 1)].rearrange("l (h r) c m -> (l h) r (c m)", h=NAH)
                for c in range(2):
                    for r in range(2):
                        for key_row in range(4):
                            src = rel[:, 3 - (2 * c + r) + key_row, 63:63 + 127 * GRID]\
                                .rearrange("h (c m) -> c h m", m=127)[:, :, 0:GRID]
                            dst = nbias[r * 64:(r + 1) * 64, :, c, key_row * GRID:(key_row + 1) * GRID]
                            sp.dma_start(dst, src).then_inc(sems["b2_bias_loaded"], 16)
                with sp.Fori(0, GROUPS) as g:
                    for j in range(G_TILES):
                        sp.wait_ge(tile_done, L * B2_N + g * G_TILES + (DEPTH * B1_N + B2_HEAD + j + 1))
                        w = (a["w_gate_2"], a["w_up_2"], a["w_down_2"])[j // KD]
                        k = j % KD
                        src = w[bass.ds(L * EXP + g * EG, EG), k * P:(k + 1) * P, :].rearrange("e p n -> p e n")
                        sp.dma_start(slot_at(j).rearrange("p (e n) -> p e n", e=EG), src)\
                          .then_inc(arrived[j % SLOTS], 16)
            sp.wait_ge(sems["b2_layer_added"], DEPTH + 1)
            sp.dma_start(out[0].rearrange("(c p) d -> p c d", p=P), x[:, :, :]).then_inc(sems["out_stored"], 16)
            sp.wait_ge(sems["out_stored"], 16)

        @block.tensor
        def _(pe):
            mm = nc.tensor.matmul
            pe.sem_inc(tile_done, SLOTS)
            pe.wait_ge(sems["const_loaded"], 16 * 4)

            def transpose_chunk(c, src, j):
                for k in (2 * j, 2 * j + 1):
                    o = (2 * (k % 2) + c) * P
                    last = nc.tensor.transpose(ps[4 + j][:, o:o + P], src(k, c), ident)
                return last

            def transpose_8(s, src, name):
                for j in range(4):
                    transpose_chunk(0, src, j)
                for j in range(4):
                    transpose_chunk(1, src, j).then_inc(s.up(name), 1)

            def transpose_stream(s, pre, which):
                for c in range(2):
                    pe.wait_ge(*s.at(pre + "normed", 2 * which + c + 1))
                    for j in range(4):
                        last = transpose_chunk(c, lambda k, c: xn[:, c, k * P:(k + 1) * P], j)
                        if c == 1:
                            last.then_inc(s.up(pre + "stream_flipped"), 1)

            def linear(t, i, lhs, w, used=1, half=None):
                wt = slot_at(t).rearrange("p (k n) -> p k n", k=KD)
                b = 2 * (i % 2)
                for c in range(2):
                    for k in range(KD):
                        last = mm(ps[b + c][:, 0:w], lhs[:, k, c * P:(c + 1) * P], wt[:, k, 0:w],
                                  start=k == 0, stop=k == KD - 1)
                    if c == 0 and half:
                        last.then_inc(half, 1)
                last.then_inc(tile_done, used)

            def score(s, pre, mp, m, keys):
                if m >= 2:
                    pe.wait_ge(*s.at(pre + "scores_read", m - 1))
                for c in range(2):
                    o, n = keys[c]
                    last = mm(ps[4 + m % 2][:, o:o + n], mp["q"][:, c * P:(c + 1) * P], mp["k"][:, 0:n],
                              start=True, stop=True)
                last.then_inc(s.up(pre + "scores_done"), 1)

            def flip(s, pre, m, blocks):
                pe.wait_ge(*s.at(pre + "probs_ready", m + 1))
                if m >= 2:
                    pe.wait_ge(*s.at(pre + "probsT_ready", m - 1))
                for i, (c, kc) in enumerate(blocks):
                    last = nc.tensor.transpose(ps[6 + m % 2][:, i * P:(i + 1) * P],
                                               sm[:, m % 3, i * P:(i + 1) * P], ident)
                last.then_inc(s.up(pre + "probs_flipped"), 1)

            def weigh(s, pre, m, blocks, v):
                pe.wait_ge(*s.at(pre + "probsT_ready", m + 1))
                if m >= 2:
                    pe.wait_ge(*s.at(pre + "out_read", m - 1))
                for i, (c, kc) in enumerate(blocks):
                    first = kc == 0
                    final = i + 1 == len(blocks) or blocks[i + 1][0] != c
                    last = mm(ps[2 + m % 2][:, c * HD:(c + 1) * HD], pT[:, m % 2, i * P:(i + 1) * P], v(kc),
                              start=first, stop=final)
                last.then_inc(s.up(pre + "out_done"), 1)

            with pe.Fori(0, DEPTH) as L:
                s = Count(sems, L, COUNTS, "b1_dve_step")

                def modulation(i):
                    b = i % 2 if i < 4 else 4 + i % 2
                    pe.wait_ge(*s.at("b1_mod_summed", i + 1))
                    if i in (4, 5):
                        pe.wait_ge(*s.at("b1_stream_by_dve", 4))
                        pe.wait_ge(*s.at("b1_stream_by_act", 4))
                    elif i >= 2:
                        pe.wait_ge(*s.at("b1_mod_ready", i - 1))
                    if i // 2 in (2, 5):
                        last = mm(ps[b][:, :], ones, acc[:, i % 2, :], start=True, stop=True)
                    else:
                        for q in range(4):
                            last = mm(ps[b][:, q:q + 1], acc[:, i % 2, q * P:(q + 1) * P], ones[:, 0:1],
                                      start=True, stop=True)
                    last.then_inc(tile_done, 1)

                transpose_stream(s, "b1_", 0)
                for i in range(4):
                    modulation(i)
                pe.wait_ge(*s.at("b1_stream_by_dve", 4))
                pe.wait_ge(*s.at("b1_stream_by_act", 4))
                pe.wait_ge(*s.at("b1_mod_ready", 4))

                def qk_flip(u):
                    if u >= 2:
                        pe.wait_ge(*s.at("b1_qk_ready", u - 1))
                    for i in range(4):
                        b, c = 2 * u + i // 2, i % 2
                        kind, o = ("A", b) if b < 4 else ("B", b - 4) if b < 10 else ("C", b - 10)
                        col = B1_Q[kind] + o * P
                        last = nc.tensor.transpose(ps[6 + u % 2][:, i * P:(i + 1) * P],
                                                   proj1[:, c, col:col + P], ident)
                    last.then_inc(s.up("b1_qk_flipped"), 1)

                for i, j in enumerate(IN1_ORDER):
                    t = B1_AT[("in", j)]
                    pe.wait_ge(*b1_loaded(L, t))
                    if i >= 2:
                        pe.wait_ge(*s.at("b1_proj_by_act", i - 1))
                        pe.wait_ge(*s.at("b1_proj_by_dve", i - 1))
                    linear(t, i, h8, min(N, IN1 - j * N))
                    if i in MOD_AT:
                        modulation(MOD_AT[i])
                    if i in (3, 4):
                        pe.wait_ge(*s.at("b1_rotated", i - 2))
                    if i == 6:
                        pe.wait_ge(*s.at("b1_proj_by_act", 6))
                        pe.wait_ge(*s.at("b1_proj_by_dve", 6))
                    for u in FLIPS_AT.get(i, ()):
                        qk_flip(u)
                pe.wait_ge(*s.at("b1_proj_by_act", 7))
                pe.wait_ge(*s.at("b1_proj_by_dve", 7))
                qk_flip(7)

                def cumsum(first, n):
                    n2 = nlf.rearrange("p (c h) -> p c h", c=2)
                    for h in range(first, first + n):
                        o = ps[h // 2 % 2][:, (h % 2) * T:(h % 2 + 1) * T]
                        mm(o[:, 0:P], n2[:, 0, h:h + 1].to_broadcast([P, P]), tri[:, 0:P], start=True, stop=True)
                        mm(o[:, P:T], n2[:, 0, h:h + 1].to_broadcast([P, P]), ones, start=True, stop=False)
                        last = mm(o[:, P:T], n2[:, 1, h:h + 1].to_broadcast([P, P]), tri[:, 0:P],
                                  start=False, stop=True)
                        if h % 2:
                            last.then_inc(s.up("b1_cumsum_done"), 1)
                    if first + n == CH:
                        mm(ps[1][:, 0:6], tri[:, 0:P], n2[:, 0, :], start=True, stop=True)
                        mm(ps[1][:, 6:12], ones, n2[:, 0, :], start=True, stop=False)
                        last = mm(ps[1][:, 6:12], tri[:, 0:P], n2[:, 1, :], start=False, stop=True)
                        last.then_inc(s.up("b1_cumsum_done"), 1)

                blocks = [(0, 0), (1, 0), (1, 1)]
                pe.wait_ge(*s.at("b1_mod_ready", 10))
                pe.wait_ge(*s.at("b1_qk_ready", 7))
                for m in range(2):
                    score(s, "b1_", map1(m), m, CAUSAL_KEYS)
                for m in range(MAPS1 + 1):
                    if m == 2:
                        pe.wait_ge(*s.at("b1_forget_ready", 1))
                        cumsum(0, 4)
                    if m == 4:
                        pe.wait_ge(*s.at("b1_cumsum_read", 2))
                        cumsum(4, 2)
                    if m + 2 == A0 + 2 * AH:
                        pe.wait_ge(*s.at("b1_qk_ready", 8))
                    if m + 2 < MAPS1:
                        score(s, "b1_", map1(m + 2), m + 2, CAUSAL_KEYS)
                    if m < MAPS1:
                        flip(s, "b1_", m, blocks)
                    if m >= 1:
                        v = map1(m - 1)["v"]
                        weigh(s, "b1_", m - 1, blocks, lambda kc: proj1[:, kc, v:v + HD])

                pe.wait_ge(*s.at("b1_out_read", MAPS1))
                pe.wait_ge(*s.at("b1_diff_ready", 1))
                ocol = [0, 128, 768, 896, 1024, 1920, 2048, 2176]
                transpose_8(s, lambda k, c: proj1[:, c, ocol[k]:ocol[k] + P], "b1_heads_flipped")
                pe.wait_ge(*s.at("b1_heads_by_dve", 2))
                pe.wait_ge(*s.at("b1_heads_by_act", 2))
                for j in range(2):
                    t = B1_AT[("out", j)]
                    pe.wait_ge(*b1_loaded(L, t))
                    linear(t, j, h8, N, half=s.up("b1_half_out_done"))

                transpose_stream(s, "b1_", 1)
                pe.wait_ge(*s.at("b1_stream_by_dve", 8))
                pe.wait_ge(*s.at("b1_stream_by_act", 8))
                for j in range(UPT):
                    t = B1_AT[("up", j)]
                    pe.wait_ge(*b1_loaded(L, t))
                    wt = slot_at(t).rearrange("p (k n) -> p k n", k=KD)
                    if j >= 2:
                        pe.wait_ge(*s.at("b1_product_ready", j - 1))
                    for half in (1, 0):
                        for f in range(2):
                            for k in range(KD):
                                o = half * 256 + f * P
                                last = mm(ps[2 * (j % 2) + half][:, f * T:(f + 1) * T], wt[:, k, o:o + P], h8[:, k, :],
                                          start=k == 0, stop=k == KD - 1)
                    last.then_inc(tile_done, 1)
                    if j in (3, 6):
                        modulation(10 + j // 6)
                pe.wait_ge(*s.at("b1_product_ready", UPT))
                nd = (FCH + 3) // 4
                for j in range(nd):
                    t = B1_AT[("down", j)]
                    pe.wait_ge(*b1_loaded(L, t))
                    wt = slot_at(t).rearrange("p (f n) -> p f n", f=4)

                    def down(q, c, n):
                        f = 4 * j + q
                        return mm(ps[4 + 2 * c + n][:, :], prod[:, f, c * P:(c + 1) * P],
                                  wt[:, q, n * N:(n + 1) * N], start=f == 0, stop=f == FCH - 1)

                    if j < nd - 1:
                        for q in range(4):
                            for c in range(2):
                                for n in range(2):
                                    last = down(q, c, n)
                    else:
                        for c in range(2):
                            for n in range(2):
                                for q in range(FCH - 4 * j):
                                    last = down(q, c, n)
                                if (c, n) != (1, 1):
                                    last.then_inc(s.up("b1_down_done"), 1)
                    last.then_inc(tile_done, 1 if j < nd - 1 else 1 + B1_N - len(B1_TILES))
                s.end()

            with pe.Fori(0, DEPTH) as L:
                s = Count(sems, L, COUNTS, "b2_dve_step")
                transpose_stream(s, "b2_", 0)
                pe.wait_ge(*s.at("b2_stream_by_dve", 4))
                pe.wait_ge(*s.at("b2_stream_by_act", 4))

                def block_flip(n, u):
                    if n >= 2:
                        pe.wait_ge(*s.at("b2_qk_ready", n - 1))
                    nb = 2 if u < 4 else 1
                    for i in range(2 * nb):
                        b, c = 2 * u + i // 2, i % 2
                        col = b * P if b < 6 else CQ2 + (b - 6) * P
                        last = nc.tensor.transpose(ps[6 + n % 2][:, i * P:(i + 1) * P], proj2[:, c, col:col + P], ident)
                    last.then_inc(s.up("b2_qk_flipped"), 1)

                small = slot_at(B2_AT[("small", 0)])
                uq = small[:, 0:1152].rearrange("p (k n) -> p k n", k=2)
                ukv = small[:, 1152:1920]
                for i, j in enumerate(IN2_ORDER):
                    t = B2_AT[("in", j)]
                    pe.wait_ge(*b2_loaded(L, t))
                    if i >= 2:
                        pe.wait_ge(*s.at("b2_proj_by_act", i - 1))
                        pe.wait_ge(*s.at("b2_proj_by_dve", i - 1))
                    linear(t, i, h8, min(N, IN2 - j * N), used=2 if i == 4 else 1)
                    if i == 1:
                        pe.wait_ge(*s.at("b2_compressed_ready", 1))
                        block_flip(0, 3)
                        block_flip(1, 4)
                    if i == 2:
                        pe.wait_ge(*b2_loaded(L, B2_AT[("small", 0)]))
                        pe.wait_ge(*s.at("b2_qk_ready", 2))
                        for c in range(2):
                            for hf in range(2):
                                for k in range(2):
                                    last = mm(ps[4 + 2 * hf + c][:, 0:288], cT[:, k, c * P:(c + 1) * P],
                                              uq[:, k, hf * 288:(hf + 1) * 288], start=k == 0, stop=k == 1)
                                last.then_inc(s.up("b2_uq_done"), 1)
                        pe.wait_ge(*s.at("b2_uq_by_act", 2))
                        pe.wait_ge(*s.at("b2_uq_by_dve", 2))
                        for c in range(2):
                            for hf in range(2):
                                last = mm(ps[4 + 2 * hf + c][:, 0:384], cT[:, 2, c * P:(c + 1) * P],
                                          ukv[:, hf * 384:(hf + 1) * 384], start=True, stop=True)
                                last.then_inc(s.up("b2_kv_done"), 1)
                pe.wait_ge(*s.at("b2_kv_by_act", 2))
                pe.wait_ge(*s.at("b2_kv_by_dve", 2))
                pe.wait_ge(*s.at("b2_heads_normed", 1))
                for n in range(3):
                    block_flip(2 + n, n)
                pe.wait_ge(*s.at("b2_qk_ready", 5))

                def shifts():
                    pe.wait_ge(*s.at("b2_taps_ready", 1))
                    pe.wait_ge(*s.at("b2_proj_by_act", 5))
                    v0 = [proj2[:, c, CC2:CC2 + 256] for c in range(2)]
                    v2 = [cv2[:, c, :] for c in range(2)]
                    o = ps[0][:, 0:256]
                    mm(o, E[:, 127:255], v0[0], start=True, stop=False)
                    mm(o, E[:, 129:257], v2[0], start=False, stop=False)
                    mm(o, E[:, 1:129], v2[1], start=False, stop=True)
                    o = ps[0][:, 256:512]
                    mm(o, E[:, 127:255], v0[1], start=True, stop=False)
                    mm(o, E[:, 255:383], v0[0], start=False, stop=False)
                    last = mm(o, E[:, 129:257], v2[1], start=False, stop=True)
                    last.then_inc(s.up("b2_shifts_done"), 1)

                blocks = [(0, 0), (0, 1), (1, 0), (1, 1)]

                def head_flip(m):
                    h = m - NAH
                    if h == 0:
                        pe.wait_ge(*s.at("b2_latent_ready", 1))
                        pe.wait_ge(*s.at("b2_shifts_read", 1))
                    if h >= 2:
                        pe.wait_ge(*s.at("b2_head_ready", h - 1))
                    for i in range(4):
                        src = (qb, kb)[i // 2][:, i % 2, h * MQK:(h + 1) * MQK]
                        last = nc.tensor.transpose(ps[m % 2][0:MQK, i * P:(i + 1) * P], src, ident)
                    last.then_inc(s.up("b2_head_flipped"), 1)

                def score2(m):
                    if m >= NAH:
                        pe.wait_ge(*s.at("b2_head_ready", m - NAH + 1))
                    score(s, "b2_", map2(m), m, ALL_KEYS)

                for m in range(2):
                    score2(m)
                for m in range(MAPS2 + 1):
                    if m == 2:
                        shifts()
                    if NAH <= m + 3 < MAPS2:
                        head_flip(m + 3)
                    if m + 2 < MAPS2:
                        score2(m + 2)
                    if m < MAPS2:
                        flip(s, "b2_", m, blocks)
                    if m >= 1:
                        h = m - 1
                        v = (lambda kc: proj2[:, kc, VA2 + HD * h:VA2 + HD * (h + 1)]) if h < NAH else \
                            (lambda kc: vb[:, kc, h - NAH, :])
                        weigh(s, "b2_", h, blocks, v)

                pe.wait_ge(*s.at("b2_mixed_ready", 1))
                ocol = [0, 128, 256, 1152, 1280, 1408, HC2, HC2 + P]
                transpose_8(s, lambda k, c: proj2[:, c, ocol[k]:ocol[k] + P], "b2_heads_flipped")
                pe.wait_ge(*s.at("b2_heads_by_dve", 2))
                pe.wait_ge(*s.at("b2_heads_by_act", 2))
                for j in range(2):
                    tt = B2_AT[("out", j)]
                    pe.wait_ge(*b2_loaded(L, tt))
                    linear(tt, j, h8, N, used=1 + j * (B2_HEAD - len(B2_TILES)), half=s.up("b2_half_out_done"))

                pe.wait_ge(sems["router_loaded"], 16)
                transpose_stream(s, "b2_", 1)
                pe.wait_ge(*s.at("b2_stream_by_dve", 8))
                pe.wait_ge(*s.at("b2_stream_by_act", 8))
                for c in range(2):
                    for k in range(KD):
                        last = mm(ps[0][:, c * EXP:(c + 1) * EXP], h8[:, k, c * P:(c + 1) * P],
                                  router[:, bass.ds(L * KD * EXP + k * EXP, EXP)],
                                  start=k == 0, stop=k == KD - 1)
                last.then_inc(s.up("b2_logits_done"), 1)
                pe.wait_ge(*s.at("b2_affinity_ready", 1))
                for c in range(2):
                    last = nc.tensor.transpose(ps[1][0:EXP, c * P:(c + 1) * P], aff[:, c * EXP:(c + 1) * EXP], ident)
                last.then_inc(s.up("b2_affinity_flipped"), 1)
                pe.wait_ge(*s.at("b2_slots_ready", 1))
                mm(ps[0][:, 0:1], ones, ones[:, 0:1], start=True, stop=True)
                for c in range(2):
                    last = nc.tensor.transpose(ps[0][:, c * EXP:(c + 1) * EXP], rcum[0:EXP, c * P:(c + 1) * P],
                                               ident[0:EXP, 0:EXP])
                last.then_inc(s.up("b2_slots_flipped"), 1)
                s.end()

                with pe.Fori(0, GROUPS) as g:
                    s = Count(sems, L * GROUPS + g, COUNTS, "g_dve_step")
                    pe.wait_ge(*s.at("g_chosen", 1))
                    for hf in range(2):
                        for q in range(4):
                            k = 4 * hf + q
                            for c in range(2):
                                last = mm(ps[4 + hf][:, q * P:(q + 1) * P], xn[:, c, k * P:(k + 1) * P],
                                          selP[:, c, :, :].rearrange("p e s -> p (e s)"), start=c == 0, stop=c == 1)
                        last.then_inc(s.up("g_rows_done"), 1)
                    pe.wait_ge(*s.at("g_weighted", 1))
                    for c in range(2):
                        last = nc.tensor.transpose(ps[6][:, c * P:(c + 1) * P],
                                                   selG[:, c, :, :].rearrange("p e s -> p (e s)"), ident)
                    last.then_inc(s.up("g_weights_flipped"), 1)
                    pe.wait_ge(*s.at("g_rows_by_dve", 1))
                    pe.wait_ge(*s.at("g_rows_by_act", 1))

                    def experts(part, lhs, bank):
                        for k in range(KD):
                            j = part * KD + k
                            pe.wait_ge(*g_loaded(L, g, j))
                            wt = slot_at(j).rearrange("p (e n) -> p e n", e=EG)
                            for n in range(2):
                                for e in range(EG):
                                    last = mm(ps[bank + n][e * CAP:(e + 1) * CAP, :],
                                              lhs[:, k, e * CAP:(e + 1) * CAP], wt[:, e, n * N:(n + 1) * N],
                                              start=k == 0, stop=k == KD - 1)
                            last.then_inc(tile_done, 1)

                    experts(0, xsT, 0)
                    experts(1, xsT, 2)
                    pe.wait_ge(*s.at("g_hidden_ready", 2))
                    for hf in range(2):
                        for q in range(4):
                            k = 4 * hf + q
                            last = nc.tensor.transpose(ps[4 + hf][:, q * P:(q + 1) * P],
                                                       hid[:, k * P:(k + 1) * P], ident)
                        last.then_inc(s.up("g_hidden_flipped"), 1)
                    pe.wait_ge(*s.at("g_weights_ready", 1))
                    pe.wait_ge(*s.at("g_hidden_by_dve", 1))
                    pe.wait_ge(*s.at("g_hidden_by_act", 1))
                    experts(2, hidT, 6)
                    pe.wait_ge(*s.at("g_result_by_act", 1))
                    pe.wait_ge(*s.at("g_result_by_dve", 1))
                    for i in range(4):
                        c, n = i // 2, i % 2
                        if i >= 2:
                            pe.wait_ge(*s.at("g_scatter_added", i - 1))
                        mm(ps[4 + i % 2][:, :], pgT[:, c, :], ysb[:, n * N:(n + 1) * N], start=True, stop=True)\
                            .then_inc(s.up("g_scatter_done"), 1)
                    s.end()

        @block.scalar
        def _(act):
            av = nc.scalar.activation
            act.wait_ge(sems["rpb_clear"], 1)
            act.dma_start(rpad[0:84, 48:79], a["rpb"]).then_inc(sems["rpb_loaded"], 16)
            act.wait_ge(sems["rpb_loaded"], 16)
            src = rpad[0:84, :].unsqueeze(1).to_broadcast([84, GRID, P])
            act.wait_ge(sems["const_loaded"], 16 * 4)
            av(csil, cols[:, 2 * NC1:2 * NC1 + 8], ACT.Silu).then_inc(sems["csil"], 1)
            act.dma_start(copies.rearrange("l h c m -> (l h) c m"), src).then_inc(sems["qk_free"], 16)

            def norm_act(s, pre, added=None):
                for c in range(2):
                    if added:
                        act.wait_ge(*s.at(added[c], 1))
                    nc.scalar.activation(xn[:, c, :], x[:, c, :], ACT.Square, accum_out=ss[:, c:c + 1])\
                        .then_inc(s.up(pre + "sumsq"), 1)

            def evac_hT(s, pre, which, scale, bias):
                for j in (1, 3):
                    act.wait_ge(*s.at(pre + "stream_flipped", 4 * which + j + 1))
                    for i in range(2):
                        k = 2 * j + i
                        kw = dict(bias=bias(k)) if bias else {}
                        av(h8[:, k, :], ps[4 + j][:, i * T:(i + 1) * T], ACT.Identity, scale=scale(k), **kw)\
                            .then_inc(s.up(pre + "stream_by_act"), 1)

            def exps(s, pre, m, keys):
                act.wait_ge(*s.at(pre + "max_ready", m + 1))
                for c in range(2):
                    v = sm[:, m % 3, keys[c][0]:keys[c][0] + keys[c][1]]
                    i = av(v, v, ACT.Exp, bias=nmx[:, 2 * m + c:2 * m + c + 1],
                           accum_out=den[:, 2 * m + c:2 * m + c + 1])
                    i.then_inc(s.up(pre + "probs_ready" if c else None), 1)

            def pt_copy(s, pre, m, n):
                act.wait_ge(*s.at(pre + "probs_flipped", m + 1))
                if m >= 2:
                    act.wait_ge(*s.at(pre + "out_done", m - 1))
                av(pT[:, m % 2, 0:n], ps[6 + m % 2][:, 0:n], ACT.Copy).then_inc(s.up(pre + "probsT_ready"), 1)

            with act.Fori(0, DEPTH) as L:
                s = Count(sems, L, COUNTS, "b1_act_step")
                for c, added in enumerate(("b1_half_layer_added", "b1_layer_added")):
                    act.wait_ge(sems[added], L + 1)
                    av(xn[:, c, :], x[:, c, :], ACT.Square, accum_out=ss[:, c:c + 1]).then_inc(s.up("b1_sumsq"), 1)
                act.dma_start(gates[:, :, :].rearrange("p (i n) m -> p i (n m)", i=2),
                              a["b_mod"].rearrange("l (s d) -> l s d", s=6)[bass.ds(L, 1), 2::3, :]
                              .to_broadcast([P, 2, D])).then_inc(sems["b1_gate_bias"], 16)
                act.wait_ge(*s.at("b1_lambda_dots", 1))
                av(lamv[:, 2:4], lamv[:, 0:2], ACT.Exp).then_inc(s.up("b1_lambda_exps"), 1)
                act.wait_ge(*s.at("b1_gain_ready", 1))
                evac_hT(s, "b1_", 0, lambda k: acol[:, k:k + 1], lambda k: modc[:, k:k + 1])

                def qk_store(u):
                    act.wait_ge(*s.at("b1_qk_flipped", u + 1))
                    for i in range(2):
                        b, src = 2 * u + i, ps[6 + u % 2][:, i * T:(i + 1) * T]
                        kind, o, w = ("A", b, 2) if b < 4 else ("B", b - 4, 3) if b < 10 else ("C", b - 10, 3)
                        if o < w:
                            qb0 = {"A": 0, "B": 2, "C": 5}[kind]
                            av(qT[:, qb0 + o, :], src, ACT.Copy).then_inc(s.up(None if i == 0 else "b1_qk_ready"), 1)
                        else:
                            kb0, n, rows_of = {"A": (0, 4, "rows32"), "B": (8, 2, "rows64"), "C": (14, 2, "rows64")}[kind]
                            for e in range(n):
                                av(kT[:, kb0 + n * (o - w) + e, :], src, ACT.Copy, scale=tb(rows_of)[:, e:e + 1])\
                                    .then_inc(s.up("b1_qk_ready" if (i, e) == (1, n - 1) else None), 1)

                for i, j in enumerate(IN1_ORDER):
                    act.wait_ge(tile_done, b1_used(L, B1_AT[("in", j)]))
                    w = min(N, IN1 - j * N)
                    av(proj1[:, 0, j * N:j * N + w], ps[2 * (i % 2)][:, 0:w], ACT.Copy)\
                        .then_inc(s.up("b1_proj_by_act"), 1)
                    if i == 3:
                        act.wait_ge(*s.at("b1_forget_abs", 1))
                        av(fe, fz, ACT.Exp, scale=-1.0).then_inc(s.up(), 1)
                        act.wait_ge(*s.own())
                        av(fe, fe, ACT.Ln, bias=1.0).then_inc(s.up("b1_forget_log"), 1)
                    if i == 3:
                        act.wait_ge(sems["qk_free"], L * 16 + 16)
                    for u in FLIPS_AT.get(i, ()):
                        qk_store(u)
                qk_store(7)
                for m in range(MAPS1 + 1):
                    if m < MAPS1:
                        exps(s, "b1_", m, CAUSAL_KEYS)
                    if m >= 1:
                        pt_copy(s, "b1_", m - 1, 384)
                for j in (1, 3):
                    act.wait_ge(*s.at("b1_heads_flipped", j + 1))
                    av(h8[:, 2 * j:2 * j + 2, :], ps[4 + j][:, :].rearrange("p (b t) -> p b t", b=2), ACT.Copy)\
                        .then_inc(s.up("b1_heads_by_act"), 1)
                act.dma_start(gfin, a["g_final"].to_broadcast([P, D])).then_inc(sems["qk_free"], 16)
                norm_act(s, "b1_", ("b1_half_mixer_added", "b1_mixer_added"))
                act.wait_ge(*s.at("b1_gain_ready", 2))
                evac_hT(s, "b1_", 1, lambda k: acol[:, 8 + k:9 + k], lambda k: modc[:, 24 + k:25 + k])
                for j in range(UPT):
                    act.wait_ge(*s.at("b1_conv_done", j + 1))
                    if j >= 2:
                        act.wait_ge(*s.at("b1_product_ready", j - 1))
                    av(pT[:, j % 2, :], sm[:, j % 2, :], ACT.Silu).then_inc(s.up("b1_silu_done"), 1)
                s.end()

            for c, added in enumerate(("b1_half_layer_added", "b1_layer_added")):
                act.wait_ge(sems[added], DEPTH + 1)
                av(xn[:, c, :], x[:, c, :], ACT.Square, accum_out=ss[:, c:c + 1]).then_inc(sems["fin_sumsq"], 1)

            with act.Fori(0, DEPTH) as L:
                s = Count(sems, L, COUNTS, "b2_act_step")
                for c, added in enumerate(("b2_half_layer_added", "b2_layer_added")):
                    act.wait_ge(sems[added], L + 1)
                    av(xn[:, c, :], x[:, c, :], ACT.Square, accum_out=ss[:, c:c + 1]).then_inc(s.up("b2_sumsq"), 1)
                evac_hT(s, "b2_", 0, lambda k: cc2("norm_mix", k), None)
                def block_store(n, u):
                    act.wait_ge(*s.at("b2_qk_flipped", n + 1))
                    for i in range(2 if u < 4 else 1):
                        b = 2 * u + i
                        final = i == (1 if u < 4 else 0)
                        src = ps[6 + n % 2][:, i * T:(i + 1) * T]
                        if 3 <= b < 6:
                            for e in range(2):
                                av(kN[:, 2 * (b - 3) + e, :], src, ACT.Copy, scale=kgain[:, e:e + 1])\
                                    .then_inc(s.up("b2_qk_ready" if final and e else None), 1)
                            continue
                        dst = qT[:, b, :] if b < 3 else cT[:, b - 6, :]
                        col = cc2("qn") if b < 3 else cc2("cq", b - 6) if b < 8 else cc2("ckv")
                        av(dst, src, ACT.Copy, scale=col).then_inc(s.up("b2_qk_ready" if final else None), 1)

                for i, j in enumerate(IN2_ORDER):
                    act.wait_ge(tile_done, b2_used(L, B2_AT[("in", j)]))
                    w = min(N, IN2 - j * N)
                    av(proj2[:, 0, j * N:j * N + w], ps[2 * (i % 2)][:, 0:w], ACT.Copy)\
                        .then_inc(s.up("b2_proj_by_act"), 1)
                    if i == 0:
                        act.wait_ge(*s.at("b2_proj_by_dve", 1))
                        for c in range(2):
                            for q, (o, n) in enumerate(((CQ2, 256), (CKV2, 128))):
                                act.wait_ge(*s.own())
                                av(sm[:, 2, 0:n], proj2[:, c, o:o + n], ACT.Square,
                                   accum_out=ssc[:, 2 * c + q:2 * c + q + 1])\
                                    .then_inc(s.up("b2_compressed_sumsq" if (c, q) == (1, 1) else None), 1)
                    if i == 1:
                        block_store(0, 3)
                        block_store(1, 4)
                    if i == 2:
                        for hf in range(2):
                            act.wait_ge(*s.at("b2_uq_done", hf + 1))
                            av(qb[:, 0, hf * 288:(hf + 1) * 288], ps[4 + 2 * hf][:, 0:288], ACT.Copy)\
                                .then_inc(s.up("b2_uq_by_act"), 1)
                        for hf in range(2):
                            act.wait_ge(*s.at("b2_kv_done", hf + 1))
                            v = ps[4 + 2 * hf][:, 0:384].rearrange("p (h n) -> p h n", h=3)
                            av(kb[:, 0, hf * 288:(hf + 1) * 288].rearrange("p (h n) -> p h n", h=3)[:, :, 0:64],
                               v[:, :, 0:64], ACT.Copy).then_inc(s.up(), 1)
                            av(vb[:, 0, 3 * hf:3 * hf + 3, :], v[:, :, 64:128], ACT.Copy)\
                                .then_inc(s.up("b2_kv_by_act"), 1)
                for n in range(3):
                    block_store(2 + n, n)

                def head_copy(m):
                    h = m - NAH
                    act.wait_ge(*s.at("b2_head_flipped", h + 1))
                    av(xqk[m % 2][0:MQK, :], ps[m % 2][0:MQK, :], ACT.Copy).then_inc(s.up("b2_head_ready"), 1)

                def mixed_squares(parts):
                    for q in parts:
                        o, n = MIXED[q]
                        for c in range(2):
                            act.wait_ge(*s.own())
                            av(hT[:, 576:576 + n], proj2[:, c, o:o + n], ACT.Square,
                               accum_out=ssm[:, 3 * c + q:3 * c + q + 1])\
                                .then_inc(s.up("b2_mixed_sumsq" if q and c else None), 1)

                for m in range(MAPS2 + 1):
                    if m == NAH + 3:
                        act.wait_ge(*s.at("b2_out_read", NAH))
                        act.wait_ge(*s.at("b2_conv_ready", 1))
                        mixed_squares((0, 1))
                    if m < MAPS2:
                        exps(s, "b2_", m, ALL_KEYS)
                    if m >= 1:
                        pt_copy(s, "b2_", m - 1, 512)
                    if NAH <= m + 3 < MAPS2:
                        head_copy(m + 3)
                act.wait_ge(*s.at("b2_out_read", MAPS2))
                mixed_squares((2,))
                for j in (1, 3):
                    act.wait_ge(*s.at("b2_heads_flipped", j + 1))
                    for i in range(2):
                        k = 2 * j + i
                        av(h8[:, k, :], ps[4 + j][:, i * T:(i + 1) * T], ACT.Copy, scale=cc2("out_norm", k))\
                            .then_inc(s.up("b2_heads_by_act" if i else None), 1)
                norm_act(s, "b2_", ("b2_half_mixer_added", "b2_mixer_added"))
                evac_hT(s, "b2_", 1, lambda k: cc2("norm_ffn", k), None)
                act.wait_ge(*s.at("b2_logits_ready", 1))
                for c in range(2):
                    i = av(affe[:, c * EXP:(c + 1) * EXP], aff[:, c * EXP:(c + 1) * EXP], ACT.Exp,
                           bias=mx2[:, c:c + 1], accum_out=dn2[:, c:c + 1])
                    i.then_inc(s.up("b2_affinity_exps" if c else None), 1)
                s.end()

                with act.Fori(0, GROUPS) as g:
                    s = Count(sems, L * GROUPS + g, COUNTS, "g_act_step")
                    act.wait_ge(*s.at("g_rows_done", 2))
                    for q in range(4):
                        k = 4 + q
                        i = av(xsT[:, k, :], ps[5][:, q * P:(q + 1) * P], ACT.Copy, scale=cc2("norm_ffn", k))
                        i.then_inc(s.up("g_rows_by_act" if q == 3 else None), 1)
                    act.wait_ge(*s.at("g_weights_flipped", 1))
                    av(pgT[:, :, :], ps[6][:, 0:256].rearrange("p (c t) -> p c t", c=2), ACT.Copy)\
                        .then_inc(s.up("g_weights_ready"), 1)
                    act.wait_ge(tile_done, g_used(L, g, KD - 1))
                    for n in range(2):
                        av(hid[:, n * N:(n + 1) * N], ps[n][:, :], ACT.Silu).then_inc(s.up("g_gate_silu"), 1)
                    act.wait_ge(*s.at("g_hidden_flipped", 2))
                    av(hidT[:, 4:8, :], ps[5][:, :].rearrange("p (k s) -> p k s", k=4), ACT.Copy)\
                        .then_inc(s.up("g_hidden_by_act"), 1)
                    act.wait_ge(tile_done, g_used(L, g, G_TILES - 1))
                    av(ysb[:, 0:N], ps[6][:, :], ACT.Copy).then_inc(s.up("g_result_by_act"), 1)
                    s.end()

        @block.gpsimd
        def _(pool):
            gp = nc.gpsimd

            def inv_root(s, n, inv, eps, name, src=ss, dst=rs, tmp=tmp28):
                gt = nc.gpsimd.tensor_tensor
                gt(tmp[:, 0:n], src[:, 0:n], tb(inv)[:, 0:n], ALU.mult).then_inc(s.up(), 1)
                pool.wait_ge(*s.own())
                gt(tmp[:, 0:n], tmp[:, 0:n], tb(eps)[:, 0:n], ALU.add).then_inc(s.up(), 1)
                pool.wait_ge(*s.own())
                gt(dst[:, 0:n], tmp[:, 0:n], tb("half")[:, 0:n], ALU.pow).then_inc(s.up(name), 1)

            def norm_pool(s, pre, which):
                for c in range(2):
                    pool.wait_ge(*s.at(pre + "sumsq", 2 * which + c + 1))
                    inv_root(s, 1, "invD", "eps6", pre + "rstd", ss[:, c:c + 1], rs[:, c:c + 1],
                             tmp28[:, c:c + 1])

            gp.memset(rpad, 0.0).then_inc(sems["rpb_clear"], 1)
            pool.wait_ge(sems["const_loaded"], 16 * 4)
            with pool.Fori(0, DEPTH) as L:
                s = Count(sems, L, COUNTS, "b1_pool_step")
                norm_pool(s, "b1_", 0)
                pool.wait_ge(*s.at("b1_cumsum_read", 4))
                pool.wait_ge(*s.at("b1_scores_done", BH))
                for h in range(CH):
                    for c, (o, n) in enumerate(CAUSAL_KEYS):
                        gp.tensor_tensor(fbias[h][:, o:o + n], causal[:, o:o + n],
                                         nfq[:, 6 * c + h:6 * c + h + 1].to_broadcast([P, n]), ALU.subtract)\
                            .then_inc(s.up(), 1)
                    pool.wait_ge(*s.own())
                    for c, (o, n) in enumerate(CAUSAL_KEYS):
                        gp.tensor_tensor(fbias[h][:, o:o + n], fbias[h][:, o:o + n], nfrow[:, h, 0:n], ALU.add)\
                            .then_inc(s.up("b1_forget_bias" if c else None), 1)
                pool.wait_ge(*s.at("b1_diff_sumsq", 1))
                inv_root(s, 8, "inv64", "eps5", "b1_diff_rstd")
                norm_pool(s, "b1_", 1)
                s.end()
            s = Count(sems, None, COUNTS, "once_pool")
            for c in range(2):
                pool.wait_ge(sems["fin_sumsq"], c + 1)
                inv_root(s, 1, "invD", "eps6", "fin_rstd", ss[:, c:c + 1], rs[:, c:c + 1],
                             tmp28[:, c:c + 1])

            with pool.Fori(0, DEPTH) as L:
                s = Count(sems, L, COUNTS, "b2_pool_step")
                norm_pool(s, "b2_", 0)
                pool.wait_ge(*s.at("b2_compressed_sumsq", 1))
                inv_root(s, 4, "invC", "eps6", "b2_compressed_rstd", ssc, rsc)
                pool.wait_ge(*s.at("b2_bias_loaded", 16 * 16))
                cm = tb("colmask").unsqueeze(1).to_broadcast([P, 48, GRID])
                nb = gbuf[:, :].rearrange("p (r j) -> p r j", j=GRID)
                gp.tensor_tensor(nb, nb, cm, ALU.add).then_inc(s.up("b2_bias_ready"), 1)
                for q in range(2):
                    pool.wait_ge(*s.at("b2_latent_sumsq", q + 1))
                    inv_root(s, 12, "inv96", "eps6", "b2_latent_rstd", ssl[:, 12 * q:12 * q + 12],
                             rsl[:, 12 * q:12 * q + 12], tmp28[:, 12 * q:12 * q + 12])
                pool.wait_ge(*s.own())
                pool.wait_ge(*s.at("b2_head_sumsq", 1))
                inv_root(s, 24, "inv64", "eps6", "b2_head_rstd")
                pool.wait_ge(*s.at("b2_proj_by_act", 5))
                pool.wait_ge(*s.at("b2_proj_by_dve", 5))
                t = B2_AT[("small", 0)]
                pool.wait_ge(*b2_loaded(L, t))
                taps = slot_at(t)[:, 2048:2816].rearrange("p (i n) -> p i n", i=3)

                def tap(i):
                    return taps[:, i, :].unsqueeze(1).to_broadcast([P, 2, 256])

                u, v0 = proj2[:, :, HC2:HC2 + 256], proj2[:, :, CC2:CC2 + 256]
                gp.tensor_tensor(u, u, v0, ALU.mult).then_inc(s.up(), 1)
                pool.wait_ge(*s.own())
                gp.tensor_tensor(cv2[:, :, :], u, tap(2), ALU.mult).then_inc(s.up(), 1)
                gp.tensor_tensor(v0, u, tap(0), ALU.mult).then_inc(s.up(), 1)
                pool.wait_ge(*s.own())
                gp.tensor_tensor(u, u, tap(1), ALU.mult).then_inc(s.up("b2_taps_ready"), 1)
                for i in range(2):
                    pool.wait_ge(*s.at("b2_mixed_sumsq", i + 1))
                    inv_root(s, 6, "invN", "eps6", "b2_mixed_rstd", ssm, rsm[i], tmpm[i])
                norm_pool(s, "b2_", 1)
                s.end()

        @block.vector
        def _(dve):
            tt, ts, stt = nc.vector.tensor_tensor, nc.vector.tensor_scalar, nc.vector.scalar_tensor_tensor
            cp = nc.vector.tensor_copy
            dve.wait_ge(sems["const_loaded"], 16 * 4)
            dve.wait_ge(sems["csil"], 1)
            nc.vector.memset(pad[:, 0:1], 0.0).then_inc(sems["b1_half_layer_added"], 1)
            nc.vector.memset(ssm, 0.0).then_inc(sems["b1_layer_added"], 1)

            def norm_dve(s, pre, which):
                for c in range(2):
                    dve.wait_ge(*s.at(pre + "rstd", 2 * which + c + 1))
                    nc.vector.tensor_scalar(xn[:, c, :], x[:, c, :], rs[:, c:c + 1], None, ALU.mult)\
                        .then_inc(s.up(pre + "normed"), 1)

            def evac_hT(s, pre, which, scale, bias):
                for j in (0, 2):
                    dve.wait_ge(*s.at(pre + "stream_flipped", 4 * which + j + 1))
                    for i in range(2):
                        k = 2 * j + i
                        src = ps[4 + j][:, i * T:(i + 1) * T]
                        ins = ts(h8[:, k, :], src, scale(k), bias(k), ALU.mult, ALU.add) if bias else \
                            ts(h8[:, k, :], src, scale(k), None, ALU.mult)
                        ins.then_inc(s.up(pre + "stream_by_dve"), 1)

            def settle(s):
                dve.wait_ge(*s.own())
                cp(pad[:, 0:1], tb("half")[:, 0:1]).then_inc(s.up(), 1)

            def rope(s, v, c, g, hw, cos, sin, t1, t2):
                cb = cos.unsqueeze(1).unsqueeze(2).to_broadcast([P, g, 2, hw])
                sn = sin.unsqueeze(1).to_broadcast([P, g, hw])
                tt(t1, v, cb, ALU.mult).then_inc(s.up(), 1)
                tt(t2[:, :, 0, :], v[:, :, 1, :], sn, ALU.mult).then_inc(s.up(), 1)
                tt(t2[:, :, 1, :], v[:, :, 0, :], sn, ALU.mult).then_inc(s.up(), 1)
                dve.wait_ge(*s.own())
                tt(v[:, :, 0, :], t1[:, :, 0, :], t2[:, :, 0, :], ALU.subtract).then_inc(s.up(), 1)
                return tt(v[:, :, 1, :], t1[:, :, 1, :], t2[:, :, 1, :], ALU.add)

            def row_max(s, pre, m):
                dve.wait_ge(*s.own())
                nc.vector.tensor_reduce(nmx[:, 2 * m:2 * m + 2], sm[:, m % 3, :].rearrange("p (c k) -> p c k", c=2),
                                        AX.X, ALU.max, negate=True).then_inc(s.up(pre + "max_ready"), 1)

            def out_norm(s, pre, m, dst):
                dve.wait_ge(*s.at(pre + "out_done", m + 1))
                nc.vector.reciprocal(rden[:, 2 * m:2 * m + 2], den[:, 2 * m:2 * m + 2]).then_inc(s.up(), 1)
                dve.wait_ge(*s.own())
                tt(dst, ps[2 + m % 2][:, 0:2 * HD].rearrange("p (c d) -> p c d", c=2),
                   rden[:, 2 * m:2 * m + 2].unsqueeze(2).to_broadcast([P, 2, HD]), ALU.mult)\
                    .then_inc(s.up(pre + "out_read"), 1)

            with dve.Fori(0, DEPTH) as L:
                s = Count(sems, L, COUNTS, "b1_dve_step")
                cp(ccol[:, 0:NC1], cols[:, bass.ds(L * NC1, NC1)]).then_inc(s.up(), 1)
                cp(crow[:, 0:NR1], rows[:, bass.ds(L * NR1, NR1)]).then_inc(s.up(), 1)
                cp(lcur, tab[:, bass.ds(L * 2 + TAB["lam"][0], 2)]).then_inc(s.up(), 1)
                dve.wait_ge(*s.own())
                lr = crow[:, R1["lam"][0]:R1["lam"][0] + 128].rearrange("p (a b d) -> p a b d", a=2, b=2)
                tt(lamt.rearrange("p (a d) -> p a d", a=2), lr[:, :, 0, :], lr[:, :, 1, :], ALU.mult)\
                    .then_inc(s.up(), 1)
                dve.wait_ge(*s.own())
                nc.vector.tensor_reduce(lamv[:, 0:2], lamt.rearrange("p (a d) -> p a d", a=2), AX.X, ALU.add)\
                    .then_inc(s.up("b1_lambda_dots"), 1)

                def accumulate(i):
                    t = B1_AT[("mod", i)]
                    dve.wait_ge(*b1_loaded(L, t))
                    if i >= 2:
                        dve.wait_ge(tile_done, b1_used(L, B1_AT[("mod", i - 2)]))
                    wt = slot_at(t).rearrange("p (k n) -> p k n", k=KD)
                    ts(acc[:, i % 2, :], wt[:, 0, :], csil[:, 0:1], None, ALU.mult).then_inc(s.up(), 1)
                    for k in range(1, KD):
                        dve.wait_ge(*s.own())
                        stt(acc[:, i % 2, :], wt[:, k, :], csil[:, k:k + 1], acc[:, i % 2, :], ALU.mult, ALU.add)\
                            .then_inc(s.up("b1_mod_summed" if k == KD - 1 else None), 1)

                def mod_out(i):
                    dve.wait_ge(tile_done, b1_used(L, B1_AT[("mod", i)]))
                    b = i % 2 if i < 4 else 4 + i % 2
                    if i // 2 in (2, 5):
                        n = i - 4 if i < 6 else i - 8
                        dve.wait_ge(*s.at("b1_gate_bias", 16))
                        tt(gates[:, n, :], ps[b][:, :], gates[:, n, :], ALU.add).then_inc(s.up("b1_mod_ready"), 1)
                    else:
                        tt(modc[:, 4 * i:4 * i + 4], ps[b][:, 0:4], cc1("b_mod", 4 * i, 4), ALU.add)\
                            .then_inc(s.up("b1_mod_ready"), 1)

                def ab(which, g):
                    dve.wait_ge(*s.own())
                    o = 8 + 24 * which
                    stt(acol[:, 8 * which:8 * which + 8], modc[:, o:o + 8], 1.0, cc1(g, 0, 8), ALU.add, ALU.mult)\
                        .then_inc(s.up("b1_gain_ready"), 1)
                    dve.wait_ge(*s.own())

                for i in range(4):
                    accumulate(i)
                    if i == 0:
                        norm_dve(s, "b1_", 0)
                    if i >= 1:
                        mod_out(i - 1)
                mod_out(3)
                ab(0, "g_attn")
                dve.wait_ge(*s.at("b1_lambda_exps", 1))
                tt(lamv[:, 0:1], lamv[:, 3:4], lamv[:, 2:3], ALU.subtract).then_inc(s.up(), 1)
                dve.wait_ge(*s.own())
                tt(lamv[:, 0:1], lamv[:, 0:1], lcur[:, 0:1], ALU.add).then_inc(s.up(), 1)
                sg = crow[:, 0:64]
                ts(sg, sg, lcur[:, 1:2], None, ALU.mult).then_inc(s.up(), 1)
                evac_hT(s, "b1_", 0, lambda k: acol[:, k:k + 1], lambda k: modc[:, k:k + 1])

                t768 = sm[:, :, :].rearrange("p a n -> p (a n)")
                def rotate(kind, g, hw):
                    for c in range(2):
                        n = g * 2 * hw
                        o = B1_Q[kind]
                        v = proj1[:, c, o:o + n].rearrange("p (g a d) -> p g a d", g=g, a=2)
                        t1 = t768[:, 0:n].rearrange("p (g a d) -> p g a d", g=g, a=2)
                        t2 = t768[:, 768:768 + n].rearrange("p (g a d) -> p g a d", g=g, a=2)
                        dve.wait_ge(*s.own())
                        cs = tb("cos" + kind)[:, c * hw:(c + 1) * hw]
                        sn = tb("sin" + kind)[:, c * hw:(c + 1) * hw]
                        ins = rope(s, v, c, g, hw, cs, sn, t1, t2)
                        ins.then_inc(s.up("b1_rotated" if c else None), 1)

                for i, j in enumerate(IN1_ORDER):
                    if i in MOD_AT:
                        accumulate(MOD_AT[i])
                    dve.wait_ge(tile_done, b1_used(L, B1_AT[("in", j)]))
                    w = min(N, IN1 - j * N)
                    cp(proj1[:, 1, j * N:j * N + w], ps[2 * (i % 2) + 1][:, 0:w]).then_inc(s.up("b1_proj_by_dve"), 1)
                    if i in MOD_AT:
                        mod_out(MOD_AT[i])
                    if i == 1:
                        dve.wait_ge(*s.at("b1_proj_by_act", 2))
                        rotate("A", 16, 16)
                    if i == 2:
                        dve.wait_ge(*s.at("b1_proj_by_act", 3))
                        f3 = fz.rearrange("p (c h) -> p c h", c=2)
                        fb = crow[:, 64:70].unsqueeze(1).to_broadcast([P, 2, 6])
                        dve.wait_ge(*s.own())
                        tt(f3, proj1[:, :, B1_F:B1_F + 6], fb, ALU.add).then_inc(s.up(), 1)
                        dve.wait_ge(*s.own())
                        ts(fa, fz, -1.0, 0.0, ALU.mult, ALU.max).then_inc(s.up(), 1)
                        dve.wait_ge(*s.own())
                        stt(fz, fa, 2.0, fz, ALU.mult, ALU.add).then_inc(s.up("b1_forget_abs"), 1)
                    if i == 3:
                        dve.wait_ge(*s.at("b1_proj_by_act", 4))
                        rotate("B", 12, 32)
                        dve.wait_ge(*s.at("b1_forget_log", 1))
                        tt(nlf, fa, fe, ALU.add).then_inc(s.up("b1_forget_ready"), 1)
                ab(1, "g_mlp")

                def cumsum_read(b):
                    dve.wait_ge(*s.at("b1_cumsum_done", b + 1))
                    cp(nfrow[:, 2 * b:2 * b + 2, :], ps[b % 2][:, :].rearrange("p (h k) -> p h k", h=2))\
                        .then_inc(s.up("b1_cumsum_read"), 1)
                    if b == 2:
                        dve.wait_ge(*s.at("b1_cumsum_done", 4))
                        cp(nfq, ps[1][:, 0:12]).then_inc(s.up("b1_cumsum_read"), 1)

                def mask1(m):
                    mp = map1(m)
                    dve.wait_ge(*s.at("b1_scores_done", m + 1))
                    if m >= 3:
                        dve.wait_ge(*s.at("b1_probs_flipped", m - 2))
                    src, dst = ps[4 + m % 2][:, 0:P + T], sm[:, m % 3, 0:P + T]
                    bias = causal if mp["kind"] == "A" else mult
                    if mp["kind"] == "C":
                        dve.wait_ge(*s.at("b1_forget_bias", mp["h"] + 1))
                        bias = fbias[mp["h"]]
                    stt(dst, src, mp["scale"], bias, ALU.mult, ALU.add).then_inc(s.up("b1_scores_read"), 1)
                    dve.wait_ge(*s.own())
                    for c, (o, n) in enumerate(CAUSAL_KEYS):
                        nc.vector.tensor_reduce(nmx[:, 2 * m + c:2 * m + c + 1], dst[:, o:o + n], AX.X, ALU.max,
                                                negate=True).then_inc(s.up("b1_max_ready" if c else None), 1)

                def out1(m):
                    mp = map1(m)
                    if mp["kind"] == "A":
                        out_norm(s, "b1_", m, oA[:, mp["h"], mp["part"], :, :])
                    else:
                        o = B1_Q[mp["kind"]] + HD * mp["h"]
                        out_norm(s, "b1_", m, proj1[:, :, o:o + HD])
                    if m == A0 + 2 * AH - 1:
                        dve.wait_ge(*s.own())
                        ev, od = oA[:, :, 0, :, :], oA[:, :, 1, :, :]
                        stt(ev, od, lamv[:, 0:1], ev, ALU.mult, ALU.add).then_inc(s.up(), 1)
                        dve.wait_ge(*s.own())
                        tt(od, ev, ev, ALU.mult).then_inc(s.up(), 1)
                        dve.wait_ge(*s.own())
                        nc.vector.tensor_reduce(ss[:, 0:8].rearrange("p (h c) -> p h c", h=AH), od, AX.X, ALU.add)\
                            .then_inc(s.up("b1_diff_sumsq"), 1)
                    if m == A0 + 2 * AH + 2:
                        dve.wait_ge(*s.at("b1_diff_rstd", 1))
                        ev = oA[:, :, 0, :, :]
                        r8 = rs[:, 0:8].rearrange("p (h c) -> p h c", h=AH)
                        tt(ev, ev, r8.unsqueeze(3).to_broadcast([P, AH, 2, HD]), ALU.mult).then_inc(s.up(), 1)
                        dve.wait_ge(*s.own())
                        for c in range(2):
                            dst = proj1[:, c, 0:AH * HD].rearrange("p (h d) -> p h d", h=AH)
                            tt(dst, oA[:, :, 0, c, :], sg.unsqueeze(1).to_broadcast([P, AH, HD]), ALU.mult)\
                                .then_inc(s.up("b1_diff_ready" if c else None), 1)

                mask1(0)
                for m in range(MAPS1 + 2):
                    if m + 1 < MAPS1:
                        mask1(m + 1)
                    if m in (2, 3):
                        cumsum_read(m - 2)
                    if m == 5:
                        cumsum_read(2)
                    if m >= 2:
                        out1(m - 2)
                for j in (0, 2):
                    dve.wait_ge(*s.at("b1_heads_flipped", j + 1))
                    cp(h8[:, 2 * j:2 * j + 2, :], ps[4 + j][:, :].rearrange("p (b t) -> p b t", b=2))\
                        .then_inc(s.up("b1_heads_by_dve"), 1)

                def residual(bank, c, n, gate, name, i):
                    tmp = sm[:, i % 3, :]
                    tt(tmp, ps[bank][:, :], gates[:, 2 * gate + n, :], ALU.mult).then_inc(s.up(), 1)
                    dve.wait_ge(*s.own())
                    xv = x[:, c, n * N:(n + 1) * N]
                    tt(xv, xv, tmp, ALU.add).then_inc(s.up(name), 1)

                for n in range(2):
                    dve.wait_ge(*s.at("b1_half_out_done", n + 1))
                    residual(2 * n, 0, n, 0, "b1_half_mixer_added" if n else None, 2 * n)
                    dve.wait_ge(tile_done, b1_used(L, B1_AT[("out", n)]))
                    residual(2 * n + 1, 1, n, 0, "b1_mixer_added" if n else None, 2 * n + 1)
                norm_dve(s, "b1_", 1)
                evac_hT(s, "b1_", 1, lambda k: acol[:, 8 + k:9 + k], lambda k: modc[:, 24 + k:25 + k])

                def conv(j):
                    dve.wait_ge(tile_done, b1_used(L, B1_AT[("up", j)]))
                    if j >= 2:
                        dve.wait_ge(*s.at("b1_silu_done", j - 1))
                    y = sm[:, j % 2, :].rearrange("p (f t) -> p f t", f=2)
                    gp = ps[2 * (j % 2) + 1][:, :].rearrange("p (f t) -> p f t", f=2)
                    dve.wait_ge(*s.own())
                    for f in range(2):
                        ts(y[:, f, :], gp[:, f, :], cc1("conv_w", 2 * FCH + 2 * j + f), cc1("conv_b", 2 * j + f),
                           ALU.mult, ALU.add).then_inc(s.up(), 1)
                    for tap_, sh in ((1, 1), (0, 2)):
                        dve.wait_ge(*s.own())
                        for f in range(2):
                            stt(y[:, f, sh:T], gp[:, f, 0:T - sh], cc1("conv_w", tap_ * FCH + 2 * j + f),
                                y[:, f, sh:T], ALU.mult, ALU.add)\
                                .then_inc(s.up("b1_conv_done" if (tap_, f) == (0, 1) else None), 1)

                def product(j):
                    dve.wait_ge(*s.at("b1_silu_done", j + 1))
                    tt(prod[:, 2 * j:2 * j + 2, :], pT[:, j % 2, :].rearrange("p (f t) -> p f t", f=2),
                       ps[2 * (j % 2)][:, :].rearrange("p (f t) -> p f t", f=2), ALU.mult)\
                        .then_inc(s.up("b1_product_ready"), 1)

                for j in range(UPT):
                    conv(j)
                    product(j)
                    if j in (2, 5):
                        accumulate(10 + j // 5)
                    if j in (4, 7):
                        mod_out(10 + j // 7)
                end = ("down", (FCH + 3) // 4 - 1)
                for c in range(2):
                    for n in range(2):
                        if (c, n) != (1, 1):
                            dve.wait_ge(*s.at("b1_down_done", 2 * c + n + 1))
                        else:
                            dve.wait_ge(tile_done, b1_used(L, B1_AT[end]))
                        name = ("b1_half_layer_added", "b1_layer_added")[c] if n else None
                        residual(4 + 2 * c + n, c, n, 1, name, 2 * c + n)
                s.end()

            dve.wait_ge(sems["qk_free"], 16 * (DEPTH + 1))
            for c in range(2):
                dve.wait_ge(sems["fin_rstd"], c + 1)
                stt(x[:, c, :], x[:, c, :], rs[:, c:c + 1], gfin, ALU.mult, ALU.mult)\
                    .then_inc(sems["b2_half_layer_added" if c == 0 else "b2_layer_added"], 1)

            with dve.Fori(0, DEPTH) as L:
                s = Count(sems, L, COUNTS, "b2_dve_step")
                cp(ccol[:, 0:NC2], cols[:, bass.ds(L * NC2 + (2 * NC1 + 8), NC2)]).then_inc(s.up(), 1)
                cp(crow[:, 0:NR2], rows[:, bass.ds(L * NR2 + 2 * NR1, NR2)]).then_inc(s.up(), 1)
                dve.wait_ge(*s.own())
                ts(kgain, tb("rows64"), cc2("kn"), None, ALU.mult).then_inc(s.up(), 1)
                norm_dve(s, "b2_", 0)
                evac_hT(s, "b2_", 0, lambda k: cc2("norm_mix", k), None)
                t768 = sm[:, 0:2, :].rearrange("p a n -> p (a n)")[:, 0:768]
                s12 = ssl.rearrange("p (t c h) -> p t c h", t=2, c=2)
                r12 = rsl.rearrange("p (t c h) -> p t c h", t=2, c=2)

                def k6(t, c):
                    return t[:, c, :].rearrange("p (h n) -> p h n", h=MLH)

                def latent_squares(q, t, scratch):
                    for c in range(2):
                        dve.wait_ge(*s.own())
                        tt(scratch, t[:, c, :], t[:, c, :], ALU.mult).then_inc(s.up(), 1)
                        dve.wait_ge(*s.own())
                        nc.vector.tensor_reduce(s12[:, q, c, :], scratch.rearrange("p (h d) -> p h d", h=MLH),
                                                AX.X, ALU.add)\
                            .then_inc(s.up("b2_latent_sumsq" if c else None), 1)

                def latent_norm(q, t, c, scratch):
                    dve.wait_ge(*s.at("b2_latent_rstd", q + 1))
                    gain = crow[:, 96 * q:96 * q + 96].unsqueeze(1).to_broadcast([P, MLH, MQK])
                    v = k6(t, c)
                    dve.wait_ge(*s.own())
                    tt(v, v, r12[:, q, c, :].unsqueeze(2).to_broadcast([P, MLH, MQK]), ALU.mult).then_inc(s.up(), 1)
                    dve.wait_ge(*s.own())
                    tt(v, v, gain, ALU.mult).then_inc(s.up(), 1)
                    dve.wait_ge(*s.own())
                    vr = v[:, :, 64:96].rearrange("p g (a d) -> p g a d", a=2)
                    t1 = scratch[:, 0:192].rearrange("p (g a d) -> p g a d", g=MLH, a=2)
                    t2 = scratch[:, 192:384].rearrange("p (g a d) -> p g a d", g=MLH, a=2)
                    ins = rope(s, vr, c, MLH, 16, tb("cosM")[:, c * 16:(c + 1) * 16],
                               tb("sinM")[:, c * 16:(c + 1) * 16], t1, t2)
                    ins.then_inc(s.up("b2_latent_ready" if (q, c) == (1, 1) else None), 1)

                for i, j in enumerate(IN2_ORDER):
                    dve.wait_ge(tile_done, b2_used(L, B2_AT[("in", j)]))
                    w = min(N, IN2 - j * N)
                    cp(proj2[:, 1, j * N:j * N + w], ps[2 * (i % 2) + 1][:, 0:w]).then_inc(s.up("b2_proj_by_dve"), 1)
                    if i == 0:
                        dve.wait_ge(*s.at("b2_compressed_rstd", 1))
                        for c in range(2):
                            for q, (o, n) in enumerate(((CQ2, 256), (CKV2, 128))):
                                v = proj2[:, c, o:o + n]
                                ts(v, v, rsc[:, 2 * c + q:2 * c + q + 1], None, ALU.mult)\
                                    .then_inc(s.up("b2_compressed_ready" if (c, q) == (1, 1) else None), 1)
                    if i == 2:
                        for hf in range(2):
                            dve.wait_ge(*s.at("b2_uq_done", hf + 3))
                            cp(qb[:, 1, hf * 288:(hf + 1) * 288], ps[5 + 2 * hf][:, 0:288])\
                                .then_inc(s.up("b2_uq_by_dve"), 1)
                        for hf in range(2):
                            dve.wait_ge(*s.at("b2_kv_done", hf + 3))
                            v = ps[5 + 2 * hf][:, 0:384].rearrange("p (h n) -> p h n", h=3)
                            cp(kb[:, 1, hf * 288:(hf + 1) * 288].rearrange("p (h n) -> p h n", h=3)[:, :, 0:64],
                               v[:, :, 0:64]).then_inc(s.up(), 1)
                            cp(vb[:, 1, 3 * hf:3 * hf + 3, :], v[:, :, 64:128]).then_inc(s.up("b2_kv_by_dve"), 1)
                        dve.wait_ge(*s.at("b2_kv_by_act", 2))
                        for c in range(2):
                            cp(k6(kb, c)[:, :, 64:96],
                               proj2[:, c, KR2:KR2 + 32].unsqueeze(1).to_broadcast([P, MLH, 32]))\
                                .then_inc(s.up(), 1)
                        dve.wait_ge(*s.at("b2_uq_by_act", 2))
                        latent_squares(0, qb, t768[:, 0:576])
                        latent_squares(1, kb, t768[:, 0:576])
                        for c in range(2):
                            latent_norm(0, qb, c, t768[:, 0:576])
                    if i == 3:
                        dve.wait_ge(*s.at("b2_proj_by_act", 4))
                        for c in range(2):
                            dve.wait_ge(*s.own())
                            v = proj2[:, c, 0:768]
                            tt(t768, v, v, ALU.mult).then_inc(s.up(), 1)
                            dve.wait_ge(*s.own())
                            nc.vector.tensor_reduce(ss[:, 12 * c:12 * c + 12],
                                                    t768.rearrange("p (h d) -> p h d", h=12), AX.X, ALU.add)\
                                .then_inc(s.up("b2_head_sumsq" if c else None), 1)
                        dve.wait_ge(*s.at("b2_head_rstd", 1))
                        for c in range(2):
                            v = proj2[:, c, 0:768].rearrange("p (h d) -> p h d", h=12)
                            tt(v, v, rs[:, 12 * c:12 * c + 12].unsqueeze(2).to_broadcast([P, 12, HD]), ALU.mult)\
                                .then_inc(s.up("b2_heads_normed" if c else None), 1)
                for c in range(2):
                    latent_norm(1, kb, c, t768[:, 0:576])
                dve.wait_ge(*s.own())
                dve.wait_ge(*s.at("b2_bias_ready", 1))

                def mask2(m):
                    mp = map2(m)
                    dve.wait_ge(*s.at("b2_scores_done", m + 1))
                    if m >= 3:
                        dve.wait_ge(*s.at("b2_probs_flipped", m - 2))
                    src, dst = ps[4 + m % 2][:, :], sm[:, m % 3, :]
                    if m < NAH:
                        stt(dst.rearrange("p (c k) -> p c k", c=2), src.rearrange("p (c k) -> p c k", c=2),
                            mp["scale"], nbias[:, m, :, :], ALU.mult, ALU.add)\
                            .then_inc(s.up("b2_scores_read"), 1)
                    else:
                        ts(dst, src, mp["scale"], None, ALU.mult).then_inc(s.up("b2_scores_read"), 1)
                    row_max(s, "b2_", m)

                def out2(m):
                    o = HD * m if m < NAH else 1152 + HD * (m - NAH)
                    out_norm(s, "b2_", m, proj2[:, :, o:o + HD])

                def mixed_scale(parts, late):
                    dve.wait_ge(*s.at("b2_mixed_rstd", late + 1))
                    for c in range(2):
                        for q in parts:
                            o, n = MIXED[q]
                            v = proj2[:, c, o:o + n]
                            ts(v, v, rsm[late][:, 3 * c + q:3 * c + q + 1], None, ALU.mult)\
                                .then_inc(s.up("b2_mixed_ready" if (c, q) == (1, 2) else None), 1)

                mask2(0)
                for m in range(MAPS2 + 2):
                    if m == MAPS2 - 1:
                        mixed_scale((0, 1), 0)
                    if m + 1 < MAPS2:
                        mask2(m + 1)
                    if m == 2:
                        dve.wait_ge(*s.at("b2_shifts_done", 1))
                        u = proj2[:, :, HC2:HC2 + 256]
                        tt(u, ps[0][:, :].rearrange("p (c n) -> p c n", c=2), u, ALU.add)\
                            .then_inc(s.up("b2_shifts_read"), 1)
                        dve.wait_ge(*s.own())
                        tt(u, u, proj2[:, :, BC2:BC2 + 256], ALU.mult).then_inc(s.up("b2_conv_ready"), 1)
                    if m >= 2:
                        out2(m - 2)
                mixed_scale((2,), 1)
                for j in (0, 2):
                    dve.wait_ge(*s.at("b2_heads_flipped", j + 1))
                    for i in range(2):
                        k = 2 * j + i
                        ts(h8[:, k, :], ps[4 + j][:, i * T:(i + 1) * T], cc2("out_norm", k), None, ALU.mult)\
                            .then_inc(s.up("b2_heads_by_dve" if i else None), 1)
                for i in range(4):
                    c, n = i % 2, i // 2
                    if c == 0:
                        dve.wait_ge(*s.at("b2_half_out_done", n + 1))
                    else:
                        dve.wait_ge(tile_done, b2_used(L, B2_AT[("out", n)]))
                    xv = x[:, c, n * N:(n + 1) * N]
                    tt(xv, ps[i][:, :], xv, ALU.add)\
                        .then_inc(s.up({2: "b2_half_mixer_added", 3: "b2_mixer_added"}.get(i)), 1)
                norm_dve(s, "b2_", 1)
                evac_hT(s, "b2_", 1, lambda k: cc2("norm_ffn", k), None)
                dve.wait_ge(*s.at("b2_logits_done", 1))
                a3 = aff.rearrange("p (c e) -> p c e", c=2)
                e3 = affe.rearrange("p (c e) -> p c e", c=2)
                tt(a3, ps[0][:, 0:32].rearrange("p (c e) -> p c e", c=2),
                   crow[:, 192:208].unsqueeze(1).to_broadcast([P, 2, EXP]), ALU.add)\
                    .then_inc(s.up(), 1)
                dve.wait_ge(*s.own())
                nc.vector.tensor_reduce(mx2, a3, AX.X, ALU.max, negate=True).then_inc(s.up("b2_logits_ready"), 1)
                dve.wait_ge(*s.at("b2_affinity_exps", 1))
                nc.vector.reciprocal(rd2, dn2).then_inc(s.up(), 1)
                dve.wait_ge(*s.own())
                tt(a3, e3, rd2.unsqueeze(2).to_broadcast([P, 2, EXP]), ALU.mult)\
                    .then_inc(s.up("b2_affinity_ready"), 1)
                dve.wait_ge(*s.at("b2_affinity_flipped", 1))
                work, sel, cum = rscratch[0:EXP, :], rsel[0:EXP, :], rcum[0:EXP, :]
                cp(work, ps[1][0:EXP, 0:T]).then_inc(s.up(), 1)
                for r in range(CAP // 8):
                    settle(s)
                    nc.vector.max(m8[0:EXP, :], work).then_inc(s.up(), 1)
                    settle(s)
                    nc.vector.match_replace(work, m8[0:EXP, :], work, -1.0).then_inc(s.up(), 1)
                dve.wait_ge(*s.own())
                ts(sel, work, 0.0, None, ALU.is_lt).then_inc(s.up(), 1)
                dve.wait_ge(*s.own())
                nc.vector.tensor_tensor_scan(cum, ones[0:EXP, 0:1].to_broadcast([EXP, T]), sel, 0.0,
                                             ALU.mult, ALU.add).then_inc(s.up(), 1)
                dve.wait_ge(*s.own())
                tt(cum, cum, sel, ALU.mult).then_inc(s.up("b2_slots_ready"), 1)
                dve.wait_ge(*s.at("b2_slots_flipped", 1))
                cp(slot, ps[0][:, 0:32]).then_inc(s.up(), 1)
                settle(s)
                s.end()

                with dve.Fori(0, GROUPS) as g:
                    s = Count(sems, L * GROUPS + g, COUNTS, "g_dve_step")
                    s3 = slot.rearrange("p (c e) -> p c e", c=2)
                    io = tb("iota").unsqueeze(1).to_broadcast([P, EG, CAP])
                    for c in range(2):
                        tt(selP[:, c, :, :], s3[:, c, bass.ds(g * EG, EG)].unsqueeze(2).to_broadcast([P, EG, CAP]),
                           io, ALU.is_equal).then_inc(s.up("g_chosen" if c else None), 1)
                    dve.wait_ge(*s.own())
                    for c in range(2):
                        tt(selG[:, c, :, :], selP[:, c, :, :],
                           a3[:, c, bass.ds(g * EG, EG)].unsqueeze(2).to_broadcast([P, EG, CAP]),
                           ALU.mult).then_inc(s.up("g_weighted" if c else None), 1)
                    dve.wait_ge(*s.at("g_rows_done", 1))
                    for q in range(4):
                        ts(xsT[:, q, :], ps[4][:, q * P:(q + 1) * P], cc2("norm_ffn", q), None, ALU.mult)\
                            .then_inc(s.up("g_rows_by_dve" if q == 3 else None), 1)
                    dve.wait_ge(*s.at("g_gate_silu", 2))
                    dve.wait_ge(tile_done, g_used(L, g, 2 * KD - 1))
                    for n in range(2):
                        hv = hid[:, n * N:(n + 1) * N]
                        tt(hv, ps[2 + n][:, :], hv, ALU.mult).then_inc(s.up("g_hidden_ready"), 1)
                    dve.wait_ge(*s.at("g_hidden_flipped", 1))
                    cp(hidT[:, 0:4, :], ps[4][:, :].rearrange("p (k s) -> p k s", k=4))\
                        .then_inc(s.up("g_hidden_by_dve"), 1)
                    dve.wait_ge(tile_done, g_used(L, g, G_TILES - 1))
                    cp(ysb[:, N:2 * N], ps[7][:, :]).then_inc(s.up("g_result_by_dve"), 1)
                    for i in range(4):
                        dve.wait_ge(*s.at("g_scatter_done", i + 1))
                        c, n = i // 2, i % 2
                        xv = x[:, c, n * N:(n + 1) * N]
                        tt(xv, ps[4 + i % 2][:, :], xv, ALU.add).then_inc(s.up("g_scatter_added"), 1)
                    s.end()
                cp(pad[:, 0:1], tb("half")[:, 0:1]).then_inc(sems["b2_half_layer_added"], 1)
                cp(mx2[:, 0:1], tb("half")[:, 0:1]).then_inc(sems["b2_layer_added"], 1)
        if MISCOUNT:
            raise AssertionError(f"counts: {sorted(set(MISCOUNT))}")


def table():
    t = np.zeros((P, NTAB), np.float32)

    def put(name, v):
        o, n = TAB[name]
        t[:, o:o + n] = v.reshape(v.shape[0], n)

    p = np.arange(P)
    put("E", (np.arange(384)[None, :] == p[:, None] + P).astype(np.float32))
    put("ones", np.ones((P, P), np.float32))
    q = (np.arange(2)[None, :, None] * P + p[:, None, None])
    k = np.arange(T)[None, None, :]

    def by_chunk(v):
        return np.concatenate([v[:, c, 0:n] for c, (_, n) in enumerate(CAUSAL_KEYS)], axis=1)

    put("causal", by_chunk(np.where(k <= q, 0.0, NEG)))
    n = np.zeros((P, 2, T))
    for window, d in ((128, 1), (512, 4), (2048, 16)):
        n += (k <= q) & ((q - k) % d == 0) & ((q - k) // d <= window // d)
    put("mult", by_chunk(np.where(n > 0, np.log(np.maximum(n, 1)), NEG)))
    put("tri", (p[:, None] <= np.arange(T)[None, :]).astype(np.float32))
    c = (p % GRID)[:, None]
    start = np.clip(c - 8, 0, GRID - 16)
    j = np.arange(GRID)[None, :]
    put("colmask", np.where((j >= start) & (j < start + 16), 0.0, NEG))
    pos = (np.arange(2)[None, :] * P + p[:, None]).astype(np.float32)[:, :, None]

    def angles(dim, kind):
        if kind == "M":
            inv = np.float32(10000.0) ** (-np.arange(dim // 2, dtype=np.float32) / np.float32(dim // 2))
        else:
            inv = np.float32(1.0) / (np.float32(10000.0) ** (np.arange(0, dim, 2, dtype=np.float32) / np.float32(dim)))
        ang = (pos * inv.astype(np.float32)[None, None, :]).astype(np.float32)
        for fn, name in ((np.cos, "cos"), (np.sin, "sin")):
            v = np.zeros((P, TAB[name + kind][1]), np.float32)
            v[:, 0:dim] = fn(ang).astype(np.float32).reshape(P, dim)
            put(name + kind, v)

    angles(32, "A")
    angles(64, "B")
    angles(32, "M")
    put("iota", np.tile(np.arange(1, CAP + 1, dtype=np.float32)[None, :], (P, 1)))
    for name, v in (("invC", [1 / 256, 1 / 128] * 2), ("invN", [1 / 384, 1 / 256, 1 / 384] * 2),
                    ("inv64", [1 / HD] * 24), ("inv96", [1 / MQK] * 24), ("invD", [1 / D] * 2), ("eps5", [1e-5] * 8),
                    ("eps6", [1e-6] * 28), ("half", [-0.5] * 28)):
        put(name, np.tile(np.array(v, np.float32)[None, :], (P, 1)))
    put("rows32", (p[:, None] // 32 == np.arange(4)[None, :]).astype(np.float32))
    put("rows64", (p[:, None] // 64 == np.arange(2)[None, :]).astype(np.float32))
    li = [0.8 - 0.6 * math.exp(-0.3 * layer) for layer in range(DEPTH)]
    put("lam", np.tile(np.array([v for x in li for v in (-x, 1.0 - x)], np.float32)[None, :], (P, 1)))
    return t


def kernel(**inputs):
    import numpy as _np
    import concourse.bacc as _bacc
    from concourse.bass_utils import run_bass_kernel_spmd as _run

    i = {k: _np.asarray(v) for k, v in inputs.items()}

    def col(v):
        return v.reshape(-1, P).T

    cols, rows = [], []
    for l in range(DEPTH):
        cols += [col(i[n][l]) for n in ("g_attn", "g_mlp", "b_mod", "conv_w", "conv_b")]
        rows += [i["subln_g"][l], i["forget_bias"][l], i["diff_lambda"][l].reshape(-1)]
    cols.append(col(i["c"]))
    for l in range(DEPTH):
        cols += [col(i[n][l]) for n in ("norm_mix_2", "norm_ffn_2", "out_norm_2", "cq_norm_2", "ckv_norm_2")]
        cols += [_np.concatenate([i[n][l], i[n][l]]).reshape(P, 1) for n in ("q_norm_a_2", "k_norm_a_2")]
        rows += [i["q_norm_b_2"][l], i["k_norm_b_2"][l], i["b_router_2"][l]]
    arrays = {
        "x": i["x"], "tab": table(),
        "cols": _np.ascontiguousarray(_np.concatenate(cols, axis=1)),
        "rows": _np.ascontiguousarray(_np.concatenate(rows).reshape(1, NROWS)),
        "rpb": _np.ascontiguousarray(i["rpb_2"][:, :, 4:11, :].reshape(DEPTH * NAH * 7, 31)),
        "g_final": i["g_final"].reshape(1, D),
    }
    for n in ("w_mod", "b_mod", "w_in", "w_out", "w_up", "w_down", "w_in_2", "w_out_2", "w_uq_2", "w_ukv_2",
              "w_router_2", "conv_w_2"):
        arrays[n] = i[n]
    for n in ("w_gate_2", "w_up_2", "w_down_2"):
        arrays[n] = i[n].reshape(DEPTH * EXP, D, EFF)
    nc = _bacc.Bacc("TRN2", target_bir_lowering=False, num_devices=1)
    aps = {n: nc.dram_tensor("in_" + n, v.shape, F32, kind="ExternalInput").ap() for n, v in arrays.items()}
    out = nc.dram_tensor("out", (1, T, D), F32, kind="ExternalOutput").ap()
    two_blocks(nc, aps, out)
    r = _run(nc, [{"in_" + n: v for n, v in arrays.items()}], core_ids=[0])
    return r.results[0]["out"]
```
